# Optimizing a Trainium2 kernel written in Bass

```python
import math
import jax, jax.numpy as jnp
from jax import lax
import numpy as np

D_MODEL = 1024
BATCH = 1
SEQ = 512
DEPTH = 1
DEC_BATCH = 8
DEC_SEQ = 8
PAST_LEN = 1024
PAGE_SIZE = 128

GLA_HEADS = 4
GLA_DK = 64
GLA_DV = 128
GLA_GATE_RANK = 16
GLA_TAU = 16.0
GLA_CHUNK = 64
NSA_HEADS = 8
NSA_KV_HEADS = 2
NSA_GROUP = NSA_HEADS // NSA_KV_HEADS
NSA_HD = 64
CMP_LEN = 32
CMP_STRIDE = 16
SEL_BLOCK = 64
N_SEL = 8
WINDOW = 512
NSA_QBLOCK = 128
N_EXPERTS = 32
TOP_K = 4
D_EXPERT = 1024
SWIGLU_LIMIT = 7.0
SWIGLU_ALPHA = 1.702
MOE_BLOCK = 128
RMS_EPS = 1e-6
NEG_INF = -1e30
FORCE_SCORE = 1e4

GLA_QK_WIDTH = GLA_HEADS * GLA_DK
GLA_WIDTH = GLA_HEADS * GLA_DV
NSA_WIDTH = NSA_HEADS * NSA_HD
NSA_KV_WIDTH = 2 * NSA_KV_HEADS * NSA_HD
IN_SPLITS = (GLA_QK_WIDTH, GLA_QK_WIDTH, GLA_WIDTH, GLA_WIDTH, GLA_GATE_RANK,
             NSA_WIDTH, NSA_KV_WIDTH, NSA_KV_WIDTH, NSA_KV_WIDTH, 3 * NSA_HEADS)
D_IN = sum(IN_SPLITS)
MIX_WIDTH = GLA_WIDTH + NSA_WIDTH

kernel_name = "hymba_gla_nsa_moe_adaln_step"

def rmsnorm(x, g):
    xf = x.astype(jnp.float32)
    y = xf * lax.rsqrt(jnp.mean(jnp.square(xf), axis=-1, keepdims=True) + RMS_EPS)
    return (y * g.astype(jnp.float32)).astype(x.dtype)

def adaln(c, w_ada, b_ada):
    mod = jax.nn.silu(c) @ w_ada + b_ada
    return mod.reshape(c.shape[0], 6, 1, D_MODEL)

def modulate(x, g, shift, scale):
    return rmsnorm(x, g) * (1.0 + scale) + shift

def masked_softmax(s, mask, axis):
    s = jnp.where(mask, s.astype(jnp.float32), NEG_INF)
    p = jnp.where(mask, jnp.exp(s - jnp.max(s, axis=axis, keepdims=True)), 0.0)
    return p / jnp.maximum(jnp.sum(p, axis=axis, keepdims=True), 1e-30)

def gla_recurrence(q, k, v, log_a, s0):
    b_sz, seq_len = q.shape[:2]
    chunk = math.gcd(seq_len, GLA_CHUNK)
    n_chunks = seq_len // chunk

    def chunks(t):
        return t.astype(jnp.float32).reshape(b_sz, n_chunks, chunk, *t.shape[2:]).swapaxes(0, 1)

    causal = jnp.tril(jnp.ones((chunk, chunk), dtype=bool))

    def step(state, inp):
        qc, kc, vc, gc = inp
        cum = jnp.cumsum(gc, axis=1)
        last = cum[:, -1]
        q_dec = qc * jnp.exp(cum)
        k_inv = kc * jnp.exp(-cum)
        k_end = kc * jnp.exp(last[:, None] - cum)
        att = jnp.where(causal, jnp.einsum('bthd,bshd->bhts', q_dec, k_inv), 0.0)
        out = jnp.einsum('bhts,bshv->bthv', att, vc) + jnp.einsum('bthd,bhdv->bthv', q_dec, state)
        state = jnp.exp(last)[..., None] * state + jnp.einsum('bshd,bshv->bhdv', k_end, vc)
        return state, out

    state, out = lax.scan(step, s0.astype(jnp.float32),
                          (chunks(q * GLA_DK ** -0.5), chunks(k), chunks(v), chunks(log_a)))
    return out.swapaxes(0, 1).reshape(b_sz, seq_len, GLA_HEADS, GLA_DV), state

def gla_mixer(q, k, v, r, a_low, w_a2, b_a, g_norm, s0):
    b_sz, seq_len = q.shape[:2]

    def heads(t, d):
        return t.reshape(b_sz, seq_len, GLA_HEADS, d)

    log_a = jax.nn.log_sigmoid((a_low @ w_a2 + b_a).astype(jnp.float32)) / GLA_TAU
    o, state = gla_recurrence(heads(q, GLA_DK), heads(k, GLA_DK), heads(v, GLA_DV), heads(log_a, GLA_DK), s0)
    o = rmsnorm(o, g_norm) * jax.nn.silu(heads(r, GLA_DV).astype(jnp.float32))
    return o.reshape(b_sz, seq_len, GLA_WIDTH), state

def nsa_compress(kv, phi_pe, phi_w):
    n_sub = kv.shape[0] // CMP_STRIDE
    ratio = CMP_LEN // CMP_STRIDE
    n_cmp = n_sub - ratio + 1
    sub = kv.reshape(n_sub, CMP_STRIDE, 2, NSA_KV_HEADS, NSA_HD)
    blocks = jnp.concatenate([sub[i:i + n_cmp] for i in range(ratio)], axis=1)
    blocks = blocks + phi_pe.transpose(1, 0, 2)[None, :, :, None, :]
    flat = blocks.transpose(0, 2, 3, 1, 4).reshape(n_cmp, 2, NSA_KV_HEADS, CMP_LEN * NSA_HD)
    return jnp.einsum('nckf,cfd->nckd', flat, phi_w)

def cmp_to_sel(n_cmp, n_sel):
    i0 = jnp.arange(n_cmp)[:, None] * CMP_STRIDE
    j0 = jnp.arange(n_sel)[None, :] * SEL_BLOCK
    return ((i0 < j0 + SEL_BLOCK) & (i0 + CMP_LEN > j0)).astype(jnp.float32)

def nsa_attend(q, qpos, gates, kc, vc, cmp_end, sel_k, sel_v, win_k, win_v, win_pos):
    scale = NSA_HD ** -0.5
    s_c = jnp.einsum('qhgd,nhd->qhgn', q, kc) * scale
    m_c = (cmp_end[None, :] <= qpos[:, None])[:, None, None, :]
    p_c = masked_softmax(s_c, m_c, -1)
    o_c = jnp.einsum('qhgn,nhd->qhgd', p_c, vc.astype(jnp.float32))
    n_sel = sel_k.shape[1]
    imp = jnp.einsum('qhgn,nj->qhj', p_c, cmp_to_sel(kc.shape[0], n_sel))
    blk = jnp.arange(n_sel)[None, :]
    cur = (qpos // SEL_BLOCK)[:, None]
    forced = (blk == 0) | (blk == cur) | (blk == cur - 1)
    future = blk * SEL_BLOCK > qpos[:, None]
    score = jnp.where(future[:, None], NEG_INF, jnp.where(forced[:, None], FORCE_SCORE, imp))
    _, idx = lax.top_k(score, min(N_SEL, n_sel))
    h_idx = jnp.arange(NSA_KV_HEADS)[None, :, None]
    k_sel = sel_k[h_idx, idx]
    v_sel = sel_v[h_idx, idx]
    pos_sel = idx[..., None] * SEL_BLOCK + jnp.arange(SEL_BLOCK)
    s_s = jnp.einsum('qhgd,qhnld->qhgnl', q, k_sel) * scale
    m_s = (pos_sel <= qpos[:, None, None, None])[:, :, None]
    p_s = masked_softmax(s_s, m_s, (-2, -1))
    o_s = jnp.einsum('qhgnl,qhnld->qhgd', p_s, v_sel.astype(jnp.float32))
    s_w = jnp.einsum('qhgd,khd->qhgk', q, win_k) * scale
    dpos = qpos[:, None] - win_pos[None, :]
    m_w = ((dpos >= 0) & (dpos < WINDOW) & (win_pos[None, :] >= 0))[:, None, None, :]
    p_w = masked_softmax(s_w, m_w, -1)
    o_w = jnp.einsum('qhgk,khd->qhgd', p_w, win_v.astype(jnp.float32))
    return gates[..., 0:1] * o_c + gates[..., 1:2] * o_s + gates[..., 2:3] * o_w

def nsa_prompt_seq(q, gates, kv_c, kv_s, kv_w, phi_pe, phi_w):
    seq_len = q.shape[0]
    cmp = nsa_compress(kv_c, phi_pe, phi_w)
    cmp_end = jnp.arange(cmp.shape[0]) * CMP_STRIDE + CMP_LEN - 1
    sel = kv_s.reshape(seq_len // SEL_BLOCK, SEL_BLOCK, 2, NSA_KV_HEADS, NSA_HD).transpose(2, 3, 0, 1, 4)
    win = jnp.pad(kv_w, ((WINDOW, 0), (0, 0), (0, 0), (0, 0)))
    qb = math.gcd(seq_len, NSA_QBLOCK)

    def block(i):
        start = i * qb
        kw = lax.dynamic_slice_in_dim(win, start, WINDOW + qb, axis=0)
        return nsa_attend(lax.dynamic_slice_in_dim(q, start, qb, 0), start + jnp.arange(qb),
                          lax.dynamic_slice_in_dim(gates, start, qb, 0),
                          cmp[:, 0], cmp[:, 1], cmp_end, sel[0], sel[1],
                          kw[:, 0], kw[:, 1], start - WINDOW + jnp.arange(WINDOW + qb))

    out = lax.map(block, jnp.arange(seq_len // qb))
    return out.reshape(seq_len, NSA_WIDTH)

def nsa_sample_seq(q, gates, new_c, new_s, win_rows, pages, cache_c, cache_s, phi_pe, phi_w):
    n_new = q.shape[0]
    past_len = pages.shape[0] * PAGE_SIZE
    total = past_len + n_new
    padded = -(-total // SEL_BLOCK) * SEL_BLOCK

    def logical_rows(pool, new):
        past = pool[pages].reshape(past_len, 2, NSA_KV_HEADS, NSA_HD)
        rows = jnp.concatenate([past, new.astype(pool.dtype)], axis=0)
        return jnp.pad(rows, ((0, padded - total), (0, 0), (0, 0), (0, 0)))

    cmp = nsa_compress(logical_rows(cache_c, new_c), phi_pe, phi_w)
    cmp_end = jnp.arange(cmp.shape[0]) * CMP_STRIDE + CMP_LEN - 1
    sel = logical_rows(cache_s, new_s).reshape(padded // SEL_BLOCK, SEL_BLOCK, 2, NSA_KV_HEADS, NSA_HD)
    sel = sel.transpose(2, 3, 0, 1, 4)
    n_win = win_rows.shape[0]
    win_pos = total - n_win + jnp.arange(n_win)
    out = nsa_attend(q, past_len + jnp.arange(n_new), gates, cmp[:, 0], cmp[:, 1], cmp_end,
                     sel[0], sel[1], win_rows[:, 0], win_rows[:, 1], win_pos)
    return out.reshape(n_new, NSA_WIDTH)

def hybrid_mixer(h, gla_s0, nsa_fn, w_in, w_a2, b_a, g_gla, w_out):
    b_sz, seq_len = h.shape[:2]
    points = np.cumsum(IN_SPLITS)[:-1].tolist()
    gq, gk, gv, gr, ga, nq, nkc, nks, nkw, ngate = jnp.split(h @ w_in, points, axis=-1)
    gla_o, gla_s = gla_mixer(gq, gk, gv, gr, ga, w_a2, b_a, g_gla, gla_s0)
    q = nq.reshape(b_sz, seq_len, NSA_KV_HEADS, NSA_GROUP, NSA_HD)
    gates = jax.nn.sigmoid(ngate.astype(jnp.float32)).reshape(b_sz, seq_len, NSA_KV_HEADS, NSA_GROUP, 3)

    def kv(t):
        return t.reshape(b_sz, seq_len, 2, NSA_KV_HEADS, NSA_HD)

    kv_c, kv_s, kv_w = kv(nkc), kv(nks), kv(nkw)
    nsa_o = nsa_fn(q, gates, kv_c, kv_s, kv_w)
    y = jnp.concatenate([gla_o.astype(h.dtype), nsa_o.astype(h.dtype)], axis=-1) @ w_out
    return y, gla_s, kv_c, kv_s, kv_w

def moe_ffn(h, w_router, b_router, w_gate, b_gate, w_up, b_up, w_down, b_down):
    n_tok = h.shape[0]
    n_assign = n_tok * TOP_K
    logits = (h @ w_router).astype(jnp.float32) + b_router.astype(jnp.float32)
    top_logit, top_idx = lax.top_k(logits, TOP_K)
    top_w = jax.nn.softmax(top_logit, axis=-1)
    flat_e = top_idx.reshape(n_assign)
    order = jnp.argsort(flat_e)
    e_sorted = flat_e[order]
    counts = jnp.bincount(flat_e, length=N_EXPERTS)
    padded = (counts + MOE_BLOCK - 1) // MOE_BLOCK * MOE_BLOCK
    start = jnp.cumsum(counts) - counts
    pad_end = jnp.cumsum(padded)
    dest = (pad_end - padded)[e_sorted] + jnp.arange(n_assign) - start[e_sorted]
    n_blocks = (n_assign + N_EXPERTS * (MOE_BLOCK - 1) + MOE_BLOCK - 1) // MOE_BLOCK
    n_rows = n_blocks * MOE_BLOCK
    row_tok = jnp.full((n_rows,), n_tok, jnp.int32).at[dest].set((order // TOP_K).astype(jnp.int32))
    row_w = jnp.zeros((n_rows,), jnp.float32).at[dest].set(top_w.reshape(n_assign)[order])
    block_e = jnp.minimum(jnp.searchsorted(pad_end, jnp.arange(n_blocks) * MOE_BLOCK, side='right'),
                          N_EXPERTS - 1)
    h_pad = jnp.concatenate([h, jnp.zeros((1, h.shape[1]), h.dtype)], axis=0)

    def expert_block(args):
        tok, e = args
        xb = h_pad[tok]
        gate = jnp.minimum(xb @ w_gate[e] + b_gate[e], SWIGLU_LIMIT)
        up = jnp.clip(xb @ w_up[e] + b_up[e], -SWIGLU_LIMIT, SWIGLU_LIMIT)
        return ((up + 1.0) * gate * jax.nn.sigmoid(SWIGLU_ALPHA * gate)) @ w_down[e] + b_down[e]

    y = lax.map(expert_block, (row_tok.reshape(n_blocks, MOE_BLOCK), block_e))
    y = y.reshape(n_rows, -1) * row_w[:, None].astype(h.dtype)
    return jnp.zeros_like(h_pad).at[row_tok].add(y)[:n_tok]

def setup_inputs(seed: int = 0) -> dict:
    key = jax.random.key(seed)
    ks = iter(jax.random.split(key, 29))
    n_pages = PAST_LEN // PAGE_SIZE
    n_pool = (DEC_BATCH * n_pages * 5) // 4
    win_buf = min(WINDOW, PAST_LEN)

    def nrm(shape, scale=1.0):
        return jax.random.normal(next(ks), shape, jnp.float32) * scale

    def gain(shape):
        return 1.0 + nrm(shape, 0.02)

    kv_row = (2, NSA_KV_HEADS, NSA_HD)
    x_prompt = nrm((BATCH, SEQ, D_MODEL))
    x_sample = nrm((DEC_BATCH, DEC_SEQ, D_MODEL))
    c_prompt = nrm((BATCH, D_MODEL))
    c_sample = nrm((DEC_BATCH, D_MODEL))
    cache_cmp = nrm((DEPTH, n_pool, PAGE_SIZE) + kv_row)
    cache_sel = nrm((DEPTH, n_pool, PAGE_SIZE) + kv_row)
    state_win = nrm((DEPTH, DEC_BATCH, win_buf) + kv_row)
    state_gla = nrm((DEPTH, DEC_BATCH, GLA_HEADS, GLA_DK, GLA_DV))
    page_table = jax.random.permutation(next(ks), n_pool)[:DEC_BATCH * n_pages]
    page_table = page_table.reshape(DEC_BATCH, n_pages).astype(jnp.int32)
    return {
        'x_prompt': x_prompt, 'x_sample': x_sample, 'c_prompt': c_prompt, 'c_sample': c_sample,
        'cache_cmp': cache_cmp, 'cache_sel': cache_sel, 'state_win': state_win, 'state_gla': state_gla,
        'page_table': page_table,
        'w_ada': nrm((DEPTH, D_MODEL, 6 * D_MODEL), 0.5 * D_MODEL ** -0.5),
        'b_ada': nrm((DEPTH, 6 * D_MODEL), 0.02),
        'g_mix': gain((DEPTH, D_MODEL)),
        'g_ffn': gain((DEPTH, D_MODEL)),
        'w_in': nrm((DEPTH, D_MODEL, D_IN), D_MODEL ** -0.5),
        'w_a2': nrm((DEPTH, GLA_GATE_RANK, GLA_QK_WIDTH), GLA_GATE_RANK ** -0.5),
        'b_a': nrm((DEPTH, GLA_QK_WIDTH), 0.1),
        'g_gla': gain((DEPTH, GLA_DV)),
        'phi_pe': nrm((DEPTH, 2, CMP_LEN, NSA_HD), 0.02),
        'phi_w': nrm((DEPTH, 2, CMP_LEN * NSA_HD, NSA_HD), (CMP_LEN * NSA_HD) ** -0.5),
        'w_out': nrm((DEPTH, MIX_WIDTH, D_MODEL), MIX_WIDTH ** -0.5),
        'w_router': nrm((DEPTH, D_MODEL, N_EXPERTS), D_MODEL ** -0.5),
        'b_router': nrm((DEPTH, N_EXPERTS), 0.01),
        'w_gate': nrm((DEPTH, N_EXPERTS, D_MODEL, D_EXPERT), D_MODEL ** -0.5),
        'b_gate': nrm((DEPTH, N_EXPERTS, D_EXPERT), 0.01),
        'w_up': nrm((DEPTH, N_EXPERTS, D_MODEL, D_EXPERT), D_MODEL ** -0.5),
        'b_up': nrm((DEPTH, N_EXPERTS, D_EXPERT), 0.01),
        'w_down': nrm((DEPTH, N_EXPERTS, D_EXPERT, D_MODEL), D_EXPERT ** -0.5),
        'b_down': nrm((DEPTH, N_EXPERTS, D_MODEL), 0.01),
        'g_final': gain((D_MODEL,)),
    }

def reference(x_prompt, x_sample, c_prompt, c_sample, cache_cmp, cache_sel, state_win, state_gla, page_table,
              w_ada, b_ada, g_mix, g_ffn, w_in, w_a2, b_a, g_gla, phi_pe, phi_w, w_out,
              w_router, b_router, w_gate, b_gate, w_up, b_up, w_down, b_down, g_final):
    xp, xs = x_prompt, x_sample
    bp, sp = xp.shape[:2]
    bs, ts = xs.shape[:2]
    win_buf = state_win.shape[2]
    cmp_p, sel_p, win_p, gla_p = [], [], [], []
    cmp_s, sel_s, win_s, gla_s = [], [], [], []
    for l in range(DEPTH):
        mod_p = adaln(c_prompt, w_ada[l], b_ada[l])
        mod_s = adaln(c_sample, w_ada[l], b_ada[l])

        def nsa_prompt(q, gates, kc, ks_, kw, l=l):
            return lax.map(lambda a: nsa_prompt_seq(*a, phi_pe[l], phi_w[l]), (q, gates, kc, ks_, kw))

        def nsa_sample(q, gates, kc, ks_, kw, l=l):
            win_rows = jnp.concatenate([state_win[l], kw.astype(state_win.dtype)], axis=1)
            return lax.map(lambda a: nsa_sample_seq(*a, cache_cmp[l], cache_sel[l], phi_pe[l], phi_w[l]),
                           (q, gates, kc, ks_, win_rows, page_table))

        hp = modulate(xp, g_mix[l], mod_p[:, 0], mod_p[:, 1])
        yp, gp, kc_p, ks_p, kw_p = hybrid_mixer(hp, jnp.zeros((bp, GLA_HEADS, GLA_DK, GLA_DV), jnp.float32),
                                                nsa_prompt, w_in[l], w_a2[l], b_a[l], g_gla[l], w_out[l])
        xp = xp + mod_p[:, 2] * yp
        hs = modulate(xs, g_mix[l], mod_s[:, 0], mod_s[:, 1])
        ys, gs, kc_s, ks_s, kw_s = hybrid_mixer(hs, state_gla[l], nsa_sample,
                                                w_in[l], w_a2[l], b_a[l], g_gla[l], w_out[l])
        xs = xs + mod_s[:, 2] * ys
        cmp_p.append(kc_p)
        sel_p.append(ks_p)
        win_p.append(jnp.pad(kw_p, ((0, 0), (win_buf, 0), (0, 0), (0, 0), (0, 0)))[:, -win_buf:])
        gla_p.append(gp)
        cmp_s.append(kc_s)
        sel_s.append(ks_s)
        win_s.append(jnp.concatenate([state_win[l], kw_s.astype(state_win.dtype)], axis=1)[:, -win_buf:])
        gla_s.append(gs)

        hp2 = modulate(xp, g_ffn[l], mod_p[:, 3], mod_p[:, 4])
        hs2 = modulate(xs, g_ffn[l], mod_s[:, 3], mod_s[:, 4])
        f = moe_ffn(jnp.concatenate([hp2.reshape(-1, D_MODEL), hs2.reshape(-1, D_MODEL)], axis=0),
                    w_router[l], b_router[l], w_gate[l], b_gate[l], w_up[l], b_up[l], w_down[l], b_down[l])
        xp = xp + mod_p[:, 5] * f[:bp * sp].reshape(bp, sp, D_MODEL)
        xs = xs + mod_s[:, 5] * f[bp * sp:].reshape(bs, ts, D_MODEL)

    y_prompt = rmsnorm(xp, g_final)
    y_sample = rmsnorm(xs, g_final)
    return (y_prompt, y_sample,
            jnp.stack(cmp_p), jnp.stack(sel_p), jnp.stack(win_p), jnp.stack(gla_p),
            jnp.stack(cmp_s), jnp.stack(sel_s), jnp.stack(win_s), jnp.stack(gla_s))


_drawn_inputs = setup_inputs


def setup_inputs(seed=0):
    import zlib

    import numpy as np

    out = dict(_drawn_inputs(seed))
    spreads = {}
    factors = {'cache_sel': 3.555,
     'g_ffn': 2.944,
     'g_gla': 6.768,
     'phi_pe': 5.952,
     'b_router': 5.26,
     'b_gate': 23.695,
     'b_up': 25.302,
     'b_down': 53.211,
     'g_final': 7.503}
    for name, (base, spread) in spreads.items():
        noise = np.random.default_rng([zlib.crc32(name.encode()), seed]).standard_normal(out[name].shape)
        drawn = base * np.exp(spread * noise) if base else spread * noise
        out[name] = __import__('jax').numpy.asarray(drawn.astype(out[name].dtype))
    for name, factor in factors.items():
        out[name] = (out[name] * factor).astype(out[name].dtype)
    return out
```

```python
from contextlib import ExitStack

import numpy as np

import concourse.bass as bass
from concourse import mybir

F32 = mybir.dt.float32
BF16 = mybir.dt.bfloat16
I32 = mybir.dt.int32
U32 = mybir.dt.uint32
ALU = mybir.AluOpType
ACT = mybir.ActivationFunctionType
AX = mybir.AxisListType

P = 128
D = 1024
KT = D // P
SEQ = 512
NSEQ, TS = 8, 8
NTOK = SEQ + NSEQ * TS
TILES = [(t * P, P) for t in range(SEQ // P)] + [(SEQ, NSEQ * TS)]
NT = len(TILES)
ST = NT - 1
PAST, PAGE = 1024, 128
GH, DK, DV, GRANK, CHUNK = 4, 64, 128, 16, 64
KVH, GRP, HD = 2, 4, 64
NE, TOPK, DE = 32, 4, 1024
BLK = 128
NSLOT = (NTOK * TOPK + NE * (BLK - 1)) // BLK
EPS = 1e-6
ARENA = 53200
NEG = -1e30
C_GQ, C_GK, C_GV, C_GR = 0, 256, 512, 1024
C_GA = 1536
C_NQ = C_GA + GRANK
C_KC, C_KS, C_KW = C_NQ + 512, C_NQ + 768, C_NQ + 1024
C_NG = C_NQ + 1280
DIN = C_NG + 3 * KVH * GRP
NCH = 6
CW = DIN // NCH
GAPS = 16
NCMP_P = SEQ // GAPS - 1
NCMP_S = PAST // GAPS - 1
NBLK_S = PAST // 64



def constants():
    p = np.arange(P)[:, None]
    cols, parts, at = {}, [], 0

    def put(name, a):
        nonlocal at
        full = np.zeros((P, a.shape[1]), np.float32)
        full[:a.shape[0]] = a
        cols[name] = (at, a.shape[1])
        parts.append(full)
        at += a.shape[1]

    c = np.arange(P)[None, :]
    put("ident", (p == c).astype(np.float32))
    s = p % 32
    put("exp_p", np.broadcast_to(s == 0, (P, P)).astype(np.float32))
    tok = np.arange(NSEQ * TS)[None, :]
    put("exp_s", (s - 1 == tok // TS).astype(np.float32))
    put("before", (p < c).astype(np.float32))
    put("iota_e", np.broadcast_to(np.arange(NE, dtype=np.float32), (P, NE)))
    put("iota_k", np.broadcast_to(np.arange(NSLOT + 1, dtype=np.float32), (P, NSLOT + 1)))
    put("token", (np.arange(NT) * P + p).astype(np.float32))
    put("eps", np.full((P, 1), EPS, np.float32))
    put("one", np.ones((P, 1), np.float32))
    n_a = at
    put("causal", np.where(c <= p, 0, NEG))
    put("gla_p", ((p // CHUNK == c // CHUNK) & (p <= c)).astype(np.float32))
    put("gla_s", ((p // TS == tok // TS) & (p <= tok)).astype(np.float32))
    b2, t8 = p // 64, p % TS
    put("same_q", ((p // 32 == c // 32) & (p % TS == c % TS)).astype(np.float32))
    put("new_keys", np.concatenate([np.where((tok // TS == 2 * i + b2) & (tok % TS <= t8), 0, NEG)
                                    for i in range(NSEQ // 2)], 1))
    put("win_old", np.where(np.arange(TS)[None, :] > t8, 0, NEG))
    blk = np.arange(NCMP_P)[None, :]
    put("cmp_p", np.concatenate([np.where(blk * GAPS + 2 * GAPS - 1 <= t * P + p, 0, NEG)
                                 for t in range(SEQ // P) for _ in range(KVH)], 1))
    put("seq_of", (p // TS == np.arange(NSEQ)[None, :]).astype(np.float32))
    n_b = at - n_a
    pos = np.arange(NTOK)[None, :]
    put("scan", np.broadcast_to(np.where(pos < SEQ, pos % CHUNK != 0, pos % TS != 0), (P, NTOK)).astype(np.float32))
    return cols, np.ascontiguousarray(np.concatenate(parts, 1), np.float32), n_a, n_b


CONST_COLS, CONST_ARRAY, N_CONST_A, N_CONST_B = constants()


class Core:

    def __init__(self, nc, ctx, io):
        self.nc, self.ctx, self.io = nc, ctx, io
        self.arena = ctx.enter_context(nc.sbuf_tensor("arena", [P, ARENA], F32))
        self.psum = ctx.enter_context(nc.psum_tensor("banks", [P, 8, 512], F32))
        self.top = 0
        self.sems = []

    def sem(self, name):
        s = self.nc.alloc_semaphore(name=name)
        self.sems.append(s)
        return s

    def stage_done(self):
        self.nc.clear_and_free_semaphores(self.sems)
        self.sems = []
        self.nc.all_engine_barrier()

    def take(self, words):
        at = self.top
        self.top += (words + 7) // 8 * 8
        return self.arena[:, at:at + words]

    def const(self, name):
        at, n = CONST_COLS[name]
        return self.consts[:, at:at + n]


class Stack:

    def __init__(self, core, at, end):
        self.core, self.at, self.end = core, at, end

    def take(self, words):
        at = self.at
        self.at += (words + 7) // 8 * 8
        assert self.at <= self.end, (self.at, self.end)
        return self.core.arena[:, at:at + words]


def linker(engine, sem):
    count = [0]

    def link(ins):
        count[0] += 1
        ins.then_inc(sem, 1)
        engine.wait_ge(sem, count[0])
    return link


def bcast(ap, dim, n):
    shape = list(ap.shape)
    return ap.unsqueeze(dim).to_broadcast(shape[:dim] + [n] + shape[dim:])


def project(core):
    nc, io, ps = core.nc, core.io, core.psum
    mod, proj, x, consts = core.mod, core.proj, core.x, core.consts
    ident = core.const("ident")
    own = Stack(core, core.z0, ARENA)
    ring = own.take(3 * 4096)
    hT = own.take(KT * NTOK).rearrange("p (k n) -> p k n", k=KT)
    ada = own.take(4 * D).rearrange("p (a n) -> p a n", a=4)
    tmp = own.take(2 * D).rearrange("p (a n) -> p a n", a=2)
    scT = own.take(KT * 9).rearrange("p (k n) -> p k n", k=KT)
    stat = own.take(2 * NT)
    junk = own.take(D)
    pr = core.proj_flat
    c9, cexp, brow = pr[0:9, 0:D], pr[0:9, D:2 * D], pr[0:1, 2 * D:2 * D + 6 * D]
    gmix = pr[:, 8 * D:9 * D]
    piece = [ring[:, i * 6 * D:(i + 1) * 6 * D] for i in range(2)]
    wchunk = [ring[:, i * 4096:i * 4096 + KT * CW].rearrange("p (k n) -> p k n", k=KT) for i in range(3)]
    w_ada = io["w_ada"].rearrange("a (p k) n -> (a p) k n", k=KT)
    w_in = io["w_in"].rearrange("a (p k) n -> (a p) k n", k=KT)

    s_const, s_c, s_x, s_b, s_g = (core.sem(n) for n in ("const_in", "c_in", "x_in", "b_ada_in", "g_mix_in"))
    s_ada = [core.sem(f"ada_in{i}") for i in range(2)]
    s_win = [core.sem(f"win_in{i}") for i in range(3)]
    s_adaused = core.sem("ada_used")
    s_cexp, s_silu, s_cT, s_scT = (core.sem(n) for n in ("c_exp", "c_silu", "cT_ps", "scT_ready"))
    s_mod, s_modcp, s_exps, s_expd = (core.sem(n) for n in ("mod_ps", "mod_ready", "expand_ps", "expand_read"))
    s_rstd, s_h, s_hps, s_hT, s_hT2 = (core.sem(n) for n in ("rstd_ready", "h_ready", "hT_ps", "hT_by_act", "hT_by_dve"))
    s_pj, s_pja, s_pjd = (core.sem(n) for n in ("proj_ps", "proj_by_act", "proj_by_dve"))
    s_dve, s_act = core.sem("dve_p1"), core.sem("act_p1")
    core.s_const = s_const

    with nc.Block() as block:
        @block.sync
        def _(sp):
            sp.dma_start(core.consts, io["consts"][:, 0:N_CONST_A + N_CONST_B]).then_inc(s_const, 16)
            sp.dma_start(c9[0:1, :], io["c_prompt"]).then_inc(s_c, 16)
            sp.dma_start(c9[1:9, :], io["c_sample"]).then_inc(s_c, 16)
            for kt in range(KT):
                if kt >= 2:
                    sp.wait_ge(s_adaused, kt - 1)
                sp.dma_start(piece[kt % 2], w_ada[:, kt, :]).then_inc(s_ada[kt % 2], 16)
                if kt == 0:
                    sp.dma_start(brow, io["b_ada"]).then_inc(s_b, 16)
                    sp.dma_start(gmix, io["g_mix"].to_broadcast([P, D])).then_inc(s_g, 16)
                if kt == 1:
                    for t, (t0, n) in enumerate(TILES):
                        src = io["x_prompt"][0, t0:t0 + n, :] if t < ST else io["x_sample"].rearrange("b t d -> (b t) d")
                        sp.dma_start(x[0:n, t, :], src).then_inc(s_x, 16)
            for c in range(NCH):
                if c == 0:
                    sp.wait_ge(s_adaused, KT - 1)
                elif c == 1:
                    sp.wait_ge(s_mod, 1)
                elif c >= 3:
                    sp.wait_ge(s_pj, NT * (c - 2))
                sp.dma_start(wchunk[c % 3], w_in[:, :, c * CW:(c + 1) * CW]).then_inc(s_win[c % 3], 16)

        @block.scalar
        def _(act):
            link = linker(act, s_act)
            act.wait_ge(s_c, 32)
            act.activation(cexp, c9, ACT.Exp, scale=-1.0).then_inc(s_cexp, 1)
            act.wait_ge(s_x, 16 * NT)
            act.wait_ge(s_const, 16)
            for t, (t0, n) in enumerate(TILES):
                link(act.activation(junk[0:n, :], x[0:n, t, :], ACT.Square, accum_out=stat[0:n, t:t + 1]))
                link(act.activation(stat[0:n, NT + t:NT + t + 1], stat[0:n, t:t + 1], ACT.Ln,
                                    scale=1.0 / D, bias=core.const("eps")[0:n, :]))
                act.activation(stat[0:n, NT + t:NT + t + 1], stat[0:n, NT + t:NT + t + 1], ACT.Exp,
                               scale=-0.5).then_inc(s_rstd, 1)
            for t, (t0, n) in enumerate(TILES):
                act.wait_ge(s_hps, 2 * t + 2)
                act.activation(hT[:, 4:8, t0:t0 + n], ps[:, 2 * (t % 2) + 1, 0:4 * n].rearrange("p (k n) -> p k n", k=4),
                               ACT.Copy).then_inc(s_hT, 1)
            for i in range(NCH * NT):
                if i % 2 == 0:
                    c, t = divmod(i, NT)
                    act.wait_ge(s_pj, i + 1)
                    act.activation(proj[0:TILES[t][1], t, c * CW:(c + 1) * CW], ps[0:TILES[t][1], 4 + i % 4, 0:CW],
                                   ACT.Copy).then_inc(s_pja, 1)

        def hcopy(dve, t):
            t0, n = TILES[t]
            dve.wait_ge(s_hps, 2 * t + 1)
            dve.tensor_copy(hT[:, 0:4, t0:t0 + n],
                            ps[:, 2 * (t % 2), 0:4 * n].rearrange("p (k n) -> p k n", k=4)).then_inc(s_hT2, 1)

        @block.vector
        def _(dve):
            link = linker(dve, s_dve)
            dve.wait_ge(s_cexp, 1)
            link(dve.tensor_scalar(cexp, cexp, 1.0, None, ALU.add))
            link(dve.reciprocal(cexp, cexp))
            dve.tensor_tensor(c9, c9, cexp, ALU.mult).then_inc(s_silu, 1)
            dve.wait_ge(s_cT, 1)
            dve.tensor_copy(scT, ps[:, 0, 0:KT * 9].rearrange("p (k n) -> p k n", k=KT)).then_inc(s_scT, 1)
            dve.wait_ge(s_mod, 1)
            for j in range(4):
                dve.tensor_copy(mod[32 * j:32 * j + 9, :, :], ps[32 * j:32 * j + 9, 1:4, :]).then_inc(s_modcp, 1)
            dve.wait_ge(s_g, 16)
            for who in range(2):
                rows = P if who == 0 else TILES[ST][1]
                bank = 4 if who == 0 else 0
                for n in range(4):
                    dve.wait_ge(s_exps, 4 * who + n + 1)
                    dst = ada[0:rows, 2 * who + n // 2, (n % 2) * 512:(n % 2) * 512 + 512]
                    if n < 2:
                        ins = dve.tensor_copy(dst, ps[0:rows, bank + n, :])
                    else:
                        ins = dve.scalar_tensor_tensor(dst, ps[0:rows, bank + n, :], 1.0,
                                                       gmix[0:rows, (n % 2) * 512:(n % 2) * 512 + 512], ALU.add, ALU.mult)
                    ins.then_inc(s_expd, 1)
            dve.wait_ge(s_expd, 8)
            for t, (t0, n) in enumerate(TILES):
                who = 2 * (t == ST)
                dve.wait_ge(s_rstd, t + 1)
                if t >= 2:
                    dve.wait_ge(s_hps, 2 * (t - 1))
                link(dve.scalar_tensor_tensor(tmp[0:n, t % 2, :], x[0:n, t, :], stat[0:n, NT + t:NT + t + 1],
                                              ada[0:n, who + 1, :], ALU.mult, ALU.mult))
                dve.tensor_tensor(tmp[0:n, t % 2, :], tmp[0:n, t % 2, :], ada[0:n, who, :], ALU.add).then_inc(s_h, 1)
                if t >= 1:
                    hcopy(dve, t - 1)
            hcopy(dve, NT - 1)
            for i in range(NCH * NT):
                if i % 2 == 1:
                    c, t = divmod(i, NT)
                    dve.wait_ge(s_pj, i + 1)
                    dve.tensor_copy(proj[0:TILES[t][1], t, c * CW:(c + 1) * CW],
                                    ps[0:TILES[t][1], 4 + i % 4, 0:CW]).then_inc(s_pjd, 1)

        @block.tensor
        def _(pe):
            pe.wait_ge(s_const, 16)
            pe.wait_ge(s_silu, 1)
            cv = c9.rearrange("s (p k) -> s k p", k=KT)
            for kt in range(KT):
                last = pe.transpose(ps[:, 0, kt * 9:kt * 9 + 9], cv[:, kt, :], ident[0:9, 0:9])
            last.then_inc(s_cT, 1)
            pe.wait_ge(s_scT, 1)
            pe.wait_ge(s_b, 16)
            for kt in range(KT):
                pe.wait_ge(s_ada[kt % 2], 16 * (kt // 2 + 1))
                for n in range(12):
                    b, j = divmod(n, 4)
                    out = ps[32 * j:32 * j + 9, 1 + b, :]
                    if kt == 0:
                        pe.matmul(out, core.const("exp_p")[0:1, 0:9], brow[:, n * 512:(n + 1) * 512], start=True, stop=False)
                    last = pe.matmul(out, scT[:, kt, :], piece[kt % 2][:, n * 512:(n + 1) * 512],
                                     start=False, stop=(kt == KT - 1))
                last.then_inc(s_adaused if kt < KT - 1 else s_mod, 1)
            pe.wait_ge(s_modcp, 4)
            for who, (name, rows, bank) in enumerate((("exp_p", P, 4), ("exp_s", 64, 0))):
                for n in range(4):
                    j = n % 4
                    pe.matmul(ps[0:rows, bank + n, :], core.const(name)[32 * j:32 * j + 9, 0:rows],
                              mod[32 * j:32 * j + 9, 0, :], start=True, stop=True).then_inc(s_exps, 1)
            for t, (t0, n) in enumerate(TILES):
                pe.wait_ge(s_h, t + 1)
                if t >= 2:
                    pe.wait_ge(s_hT, t - 1)
                    pe.wait_ge(s_hT2, t - 1)
                else:
                    pe.wait_ge(s_expd, 8)
                hv = tmp[0:n, t % 2, :].rearrange("s (p k) -> s k p", k=KT)
                for kt in range(KT):
                    last = pe.transpose(ps[:, 2 * (t % 2) + kt // 4, (kt % 4) * n:(kt % 4) * n + n], hv[:, kt, :],
                                        ident[0:n, 0:n])
                    if kt % 4 == 3:
                        last.then_inc(s_hps, 1)
            pe.wait_ge(s_hT, NT)
            pe.wait_ge(s_hT2, NT)
            for i in range(NCH * NT):
                c, t = divmod(i, NT)
                t0, n = TILES[t]
                if t == 0:
                    pe.wait_ge(s_win[c % 3], 16 * (c // 3 + 1))
                if i >= 4:
                    pe.wait_ge(s_pja if i % 2 == 0 else s_pjd, (i - 4) // 2 + 1)
                for kt in range(KT):
                    last = pe.matmul(ps[0:n, 4 + i % 4, 0:CW], hT[:, kt, t0:t0 + n], wchunk[c % 3][:, kt, :],
                                     start=(kt == 0), stop=(kt == KT - 1))
                last.then_inc(s_pj, 1)


QN, KSF, KWF, GQF, GKF, GAF, NF = 0, 4, 5, 6, 8, 10, 11


def gla(core):
    nc, io, ps = core.nc, core.io, core.psum
    proj, feat, mix = core.proj, core.feat, core.mix
    ident = core.const("ident")
    own = Stack(core, core.z0, core.z1)
    scan = own.take(NTOK)
    e1 = own.take(2 * NTOK).rearrange("p (j n) -> p j n", j=2)
    e2 = own.take(2 * NTOK).rearrange("p (j n) -> p j n", j=2)
    cum = own.take(2 * NTOK).rearrange("p (j n) -> p j n", j=2)
    qd = own.take(GH * NTOK).rearrange("p (h n) -> p h n", h=GH)
    kinv = own.take(2 * NTOK).rearrange("p (j n) -> p j n", j=2)
    kend = own.take(2 * NTOK).rearrange("p (j n) -> p j n", j=2)
    kt = own.take(NT * 256).rearrange("p (t n) -> p t n", t=NT)
    att = own.take(NT * GH * P).rearrange("p (t h n) -> p t h n", t=NT, h=GH)
    qdb = own.take(GH * NSEQ * 64).rearrange("p (h b n) -> p h b n", h=GH, b=NSEQ)
    st = own.take(2 * 2 * DV).rearrange("p (u j v) -> p u j v", u=2, j=2)
    ss = own.take(NSEQ * 2 * DV).rearrange("p (b j v) -> p b j v", b=NSEQ, j=2)
    kb = own.take(2 * 256).rearrange("p (u n) -> p u n", u=2)
    wa2, ba, dec, ggla = own.take(256), own.take(2), own.take(32).rearrange("p (j c) -> p j c", j=2), own.take(DV)
    sil, sq = own.take(512), own.take(512)
    r4 = own.take(2 * 4 * NT).rearrange("p (a t h) -> p a t h", a=2, t=NT)
    maskp = core.const("gla_p").bitcast(I32)
    masks = core.const("gla_s").bitcast(I32)

    s_in, s_out = core.sem("gla_in"), core.sem("gla_out")
    s_zero, s_ft, s_fa, s_fd = (core.sem(n) for n in ("gla_zeroed", "feat_ps", "feat_by_act", "feat_by_dve"))
    s_z, s_zc, s_l, s_cum, s_e, s_df, s_ke = (core.sem(n) for n in ("gate_ps", "gate_copied", "softplus", "cum_ready", "decays", "to_end", "end_decay"))
    s_qk, s_kend, s_ktp, s_kt = (core.sem(n) for n in ("qk_decayed", "kend_ready", "kt_ps", "kt_ready"))
    s_atp, s_att, s_u, s_s, s_o = (core.sem(n) for n in ("att_ps", "att_ready", "upd_ps", "state_ready", "o_ps"))
    s_kb, s_ub, s_sb = (core.sem(n) for n in ("kb_ready", "updb_ps", "stateb_ready"))
    s_osb, s_ssq, s_r4, s_er, s_mix = (core.sem(n) for n in ("o_copied", "o_sumsq", "o_rstd", "r_exp", "gla_mixed"))
    s_dve, s_act = core.sem("dve_p2"), core.sem("act_p2")
    core.s_kvout = core.sem("kv_stored")
    core.n_kvout = 0
    BPB = 3

    def queries(bank, t0, n, h, e):
        q = ps[64 * e:64 * e + 64, bank, :].rearrange("p (i n) -> p i n", i=4)
        return feat[64 * h:64 * h + 64, QN + e:QN + GRP:2, t0:t0 + n], q[:, 2 * h:2 * h + 2, 0:n]

    with nc.Block() as block:
        @block.sync
        def _(sp):
            sp.dma_start(scan, io["consts"][:, N_CONST_A + N_CONST_B:]).then_inc(s_in, 16)
            sp.dma_start(wa2[0:GRANK, :], io["w_a2"].rearrange("a r n -> (a r) n")).then_inc(s_in, 16)
            with nc.allow_non_contiguous_dma(reason="256 biases, one per partition"):
                sp.dma_start(ba, io["b_a"].rearrange("a (j p) -> p (a j)", j=2)).then_inc(s_in, 16)
            sp.dma_start(ggla, io["g_gla"].to_broadcast([P, DV])).then_inc(s_in, 16)
            sp.dma_start(ss, io["state_gla"].rearrange("a b (j e) d v -> (a e d) (b j) v", e=2)
                         .rearrange("p (b j) v -> p b j v", j=2)).then_inc(s_in, 16)
            for o, c in ((2, C_KC), (3, C_KS), (4, C_KW)):
                sp.dma_start(io[f"out_{o}"].rearrange("a b (t p) c h d -> p (a b t) (c h d)", p=P),
                             proj[:, 0:ST, c:c + 256]).then_inc(core.s_kvout, 16)
            for o, c in ((6, C_KC), (7, C_KS)):
                sp.dma_start(io[f"out_{o}"].rearrange("a b t c h d -> (a b t) (c h d)"),
                             proj[0:64, ST, c:c + 256]).then_inc(core.s_kvout, 16)
            for b in range(NSEQ):
                sp.dma_start(io["out_8"][0, b, SEQ - TS:SEQ].rearrange("t c h d -> t (c h d)"),
                             proj[TS * b:TS * b + TS, ST, C_KW:C_KW + 256]).then_inc(core.s_kvout, 16)
            sp.dma_start(io["out_8"][0, :, 0:SEQ - TS].rearrange("b t c h d -> b (t c h d)"),
                         io["state_win"][0, :, TS:SEQ].rearrange("b t c h d -> b (t c h d)")).then_inc(core.s_kvout, 16)
            core.n_kvout = 16 * (6 + NSEQ)
            sp.wait_ge(s_s, 1 + SEQ // CHUNK)
            sp.dma_start(io["out_5"].rearrange("a b (j e) d v -> (a b e d) j v", e=2), st[:, 0, :, :]).then_inc(s_out, 16)
            sp.wait_ge(s_sb, NSEQ)
            sp.dma_start(io["out_9"].rearrange("a b (j e) d v -> (a e d) (b j) v", e=2),
                         ss.rearrange("p b j v -> p (b j) v")).then_inc(s_out, 16)
            sp.wait_ge(s_out, 32)
            sp.wait_ge(core.s_kvout, core.n_kvout)

        @block.gpsimd
        def _(pool):
            pool.memset(qd, 0.0).then_inc(s_zero, 1)
            pool.memset(att, 0.0).then_inc(s_zero, 1)
            pool.memset(qdb, 0.0).then_inc(s_zero, 1)

        @block.tensor
        def _(pe):
            for t, (t0, n) in enumerate(TILES):
                pj = proj[0:n, t, :]
                srcs = [pj[:, c:c + P] for c in (C_NQ, C_NQ + P, C_NQ + 2 * P, C_NQ + 3 * P,
                                                 C_KS, C_KW, C_GQ, C_GQ + P, C_GK, C_GK + P)]
                base = BPB * (t % 2)
                if t >= 2:
                    pe.wait_ge(s_fa, 4 * (t - 1))
                    pe.wait_ge(s_fd, 3 * (t - 1))
                for i, src in enumerate(srcs):
                    last = pe.transpose(ps[:, base + i // 4, (i % 4) * P:(i % 4) * P + n], src, ident[0:n, 0:n])
                    if i in (3, 7):
                        last.then_inc(s_ft, 1)
                pe.transpose(ps[0:GRANK, base + 2, 2 * P:2 * P + n], pj[:, C_GA:C_GA + GRANK],
                             ident[0:n, 0:n]).then_inc(s_ft, 1)
            pe.wait_ge(s_fa, 4 * NT)
            pe.wait_ge(s_fd, 3 * NT)
            pe.wait_ge(s_in, 80)
            for j in range(2):
                w = wa2[0:GRANK, j * P:(j + 1) * P]
                pe.matmul(ps[:, 6 + j, :], w, feat[0:GRANK, GAF, 0:SEQ], start=True, stop=True)
                pe.matmul(ps[:, 5, j * 64:j * 64 + 64], w, feat[0:GRANK, GAF, SEQ:NTOK],
                          start=True, stop=True).then_inc(s_z, 1)
            pe.wait_ge(s_kend, 1)
            for t, (t0, n) in enumerate(TILES):
                for j in range(2):
                    last = pe.transpose(ps[0:n, t, j * P:(j + 1) * P], kend[:, j, t0:t0 + n], ident)
                last.then_inc(s_ktp, 1)
            pe.wait_ge(s_qk, 5)
            for t, (t0, n) in enumerate(TILES):
                if t >= 3:
                    pe.wait_ge(s_kt, t - 2)
                for h in range(GH):
                    last = pe.matmul(ps[0:n, (5 + t) % 8, h * n:h * n + n], kinv[:, h // 2, t0:t0 + n],
                                     qd[:, h, t0:t0 + n], start=True, stop=True)
                last.then_inc(s_atp, 1)
            pe.wait_ge(s_kt, NT)
            pe.wait_ge(s_att, NT)
            for ci in range(SEQ // CHUNK):
                t, c = divmod(ci, 2)
                r0 = CHUNK * c
                v = proj[:, t, C_GV:C_GV + 512]
                for j in range(2):
                    last = pe.matmul(ps[:, 4 + ci % 2, j * 256:(j + 1) * 256], kt[r0:r0 + CHUNK, t, j * P:(j + 1) * P],
                                     v[r0:r0 + CHUNK, j * 256:(j + 1) * 256], start=True, stop=True)
                last.then_inc(s_u, 1)
                pe.wait_ge(s_s, ci + 1)
                if c == 0 and t >= 2:
                    pe.wait_ge(s_osb, t - 1)
                for h in range(GH):
                    out = ps[r0:r0 + CHUNK, 2 + t % 2, h * DV:(h + 1) * DV]
                    pe.matmul(out, att[:, t, h, r0:r0 + CHUNK], v[:, h * DV:(h + 1) * DV], start=True, stop=False)
                    last = pe.matmul(out, qd[:, h, t * P + r0:t * P + r0 + CHUNK], st[:, ci % 2, h // 2, :],
                                     start=False, stop=True)
                if c == 1:
                    last.then_inc(s_o, 1)
            v = proj[0:64, ST, C_GV:C_GV + 512]
            pe.wait_ge(s_qk, 6)
            for h in range(GH):
                out = ps[0:64, 6, h * DV:(h + 1) * DV]
                pe.matmul(out, att[0:64, ST, h, 0:64], v[:, h * DV:(h + 1) * DV], start=True, stop=False)
                for b in range(NSEQ):
                    last = pe.matmul(out, qdb[:, h, b, :], ss[:, b, h // 2, :], start=False, stop=(b == NSEQ - 1))
            last.then_inc(s_o, 1)
            for b in range(NSEQ):
                pe.wait_ge(s_kb, b + 1)
                if b >= 2:
                    pe.wait_ge(s_sb, b - 1)
                for j in range(2):
                    last = pe.matmul(ps[:, b % 2, j * 256:(j + 1) * 256], kb[0:64, b % 2, j * P:(j + 1) * P],
                                     v[:, j * 256:(j + 1) * 256], start=True, stop=True)
                last.then_inc(s_ub, 1)

        @block.scalar
        def _(act):
            link = linker(act, s_act)
            for t, (t0, n) in enumerate(TILES):
                base = BPB * (t % 2)
                act.wait_ge(s_ft, 3 * t + 1)
                for h in range(KVH):
                    for e in range(2):
                        act.activation(*queries(base, t0, n, h, e), ACT.Copy).then_inc(s_fa, 1)
            act.wait_ge(s_in, 80)
            act.wait_ge(s_zc, 1)
            link(act.activation(e1, e2, ACT.Abs))
            link(act.activation(e1, e1, ACT.Exp, scale=-1.0))
            act.activation(e1, e1, ACT.Ln, bias=core.const("one")).then_inc(s_l, 1)
            act.wait_ge(s_cum, 2)
            g16 = 1.0 / 16.0
            act.activation(e1, cum, ACT.Exp, scale=g16)
            act.activation(dec[:, :, 0:8], cum[:, :, CHUNK - 1:SEQ:CHUNK], ACT.Exp, scale=g16)
            act.activation(dec[:, :, 8:16], cum[:, :, SEQ + TS - 1:NTOK:TS], ACT.Exp, scale=g16)
            act.activation(e2, cum, ACT.Exp, scale=-g16).then_inc(s_e, 1)
            act.wait_ge(s_df, 1)
            act.activation(kend, kend, ACT.Exp, scale=g16).then_inc(s_ke, 1)
            for t, (t0, n) in enumerate(TILES):
                act.wait_ge(s_ktp, t + 1)
                act.activation(kt[0:n, t, :], ps[0:n, t, 0:256], ACT.Copy).then_inc(s_kt, 1)
            for t, (t0, n) in enumerate(TILES):
                if t >= 1:
                    act.wait_ge(s_mix, t)
                act.activation(sil[0:n, :], proj[0:n, t, C_GR:C_GR + 512], ACT.Exp, scale=-1.0).then_inc(s_er, 1)
                act.wait_ge(s_o, t + 1)
                act.activation(mix[0:n, t, 0:512], ps[0:n, 2 + t % 2 if t < ST else 6, :], ACT.Copy).then_inc(s_osb, 1)
                act.wait_ge(s_ssq, t + 1)
                link(act.activation(r4[0:n, 1, t, :], r4[0:n, 0, t, :], ACT.Ln, scale=1.0 / DV,
                                    bias=core.const("eps")[0:n, :]))
                act.activation(r4[0:n, 1, t, :], r4[0:n, 1, t, :], ACT.Exp, scale=-0.5).then_inc(s_r4, 1)

        @block.vector
        def _(dve):
            link = linker(dve, s_dve)
            for t, (t0, n) in enumerate(TILES):
                base = BPB * (t % 2)
                dve.wait_ge(s_ft, 3 * t + 2)
                dve.tensor_copy(feat[:, 4:8, t0:t0 + n], ps[:, base + 1, :].rearrange("p (i n) -> p i n", i=4)[:, :, 0:n]
                                ).then_inc(s_fd, 1)
                dve.wait_ge(s_ft, 3 * t + 3)
                dve.tensor_copy(feat[:, 8:10, t0:t0 + n], ps[:, base + 2, 0:256].rearrange("p (i n) -> p i n", i=2)[:, :, 0:n]
                                ).then_inc(s_fd, 1)
                dve.tensor_copy(feat[0:GRANK, GAF, t0:t0 + n], ps[0:GRANK, base + 2, 2 * P:2 * P + n]).then_inc(s_fd, 1)
            dve.wait_ge(s_in, 80)
            dve.memset(st[:, 0], 0.0).then_inc(s_s, 1)
            dve.wait_ge(s_z, 2)
            for j in range(2):
                dve.tensor_scalar(e2[:, j, 0:SEQ], ps[:, 6 + j, :], ba[:, j:j + 1], None, ALU.add)
                last = dve.tensor_scalar(e2[:, j, SEQ:NTOK], ps[:, 5, j * 64:j * 64 + 64], ba[:, j:j + 1], None, ALU.add)
            last.then_inc(s_zc, 1)
            dve.wait_ge(s_l, 1)
            link(dve.scalar_tensor_tensor(e2, e2, 0.0, e1, ALU.min, ALU.subtract))
            for j in range(2):
                dve.tensor_tensor_scan(cum[:, j, :], scan, e2[:, j, :], 0.0, ALU.mult, ALU.add).then_inc(s_cum, 1)
            dve.wait_ge(s_cum, 2)
            for a, b, c in ((0, SEQ, CHUNK), (SEQ, NTOK, TS)):
                cv = cum[:, :, a:b].rearrange("p j (c n) -> p j c n", n=c)
                last = dve.tensor_tensor(kend[:, :, a:b].rearrange("p j (c n) -> p j c n", n=c),
                                         cv[:, :, :, c - 1:c].to_broadcast([P, 2, (b - a) // c, c]), cv, ALU.subtract)
            last.then_inc(s_df, 1)
            dve.wait_ge(s_ke, 1)
            dve.tensor_tensor(kend, kend, feat[:, GKF:GKF + 2, :], ALU.mult).then_inc(s_kend, 1)
            dve.wait_ge(s_e, 1)
            dve.wait_ge(s_zero, 3)
            for h in range(GH):
                e0 = 64 * (h % 2)
                dve.scalar_tensor_tensor(qd[e0:e0 + 64, h, :], feat[e0:e0 + 64, GQF + h // 2, :], DK ** -0.5,
                                         e1[e0:e0 + 64, h // 2, :], ALU.mult, ALU.mult).then_inc(s_qk, 1)
            dve.tensor_tensor(kinv, feat[:, GKF:GKF + 2, :], e2, ALU.mult).then_inc(s_qk, 1)
            dve.wait_ge(s_qk, 4)
            for h in range(GH):
                diag = qdb[:, h, :, :].rearrange("p b (c n) -> p (b c) n", n=TS)[:, 0::NSEQ + 1, :]
                last = dve.tensor_copy(diag, qd[:, h, SEQ:NTOK].rearrange("p (b n) -> p b n", n=TS))
            last.then_inc(s_qk, 1)
            for t, (t0, n) in enumerate(TILES):
                dve.wait_ge(s_atp, t + 1)
                m = maskp if t < ST else masks[0:64, :]
                dve.copy_predicated(att[0:n, t, :, 0:n], bcast(m, 1, GH),
                                    ps[0:n, (5 + t) % 8, 0:GH * n].rearrange("p (h n) -> p h n", h=GH)).then_inc(s_att, 1)

            def state_step(dst, src, bank, col):
                for h in range(GH):
                    j, e = divmod(h, 2)
                    last = dve.scalar_tensor_tensor(dst[64 * e:64 * e + 64, j, :], src[64 * e:64 * e + 64, j, :],
                                                    dec[64 * e:64 * e + 64, j, col:col + 1],
                                                    ps[64 * e:64 * e + 64, bank, h * DV:(h + 1) * DV], ALU.mult, ALU.add)
                return last

            def finish_tile(t):
                n = TILES[t][1]
                o = mix[0:n, t, 0:512]
                o4 = o.rearrange("p (h v) -> p h v", h=GH)
                dve.wait_ge(s_er, t + 1)
                link(dve.tensor_scalar(sil[0:n, :], sil[0:n, :], 1.0, None, ALU.add))
                link(dve.reciprocal(sil[0:n, :], sil[0:n, :]))
                link(dve.tensor_tensor(sil[0:n, :], sil[0:n, :], proj[0:n, t, C_GR:C_GR + 512], ALU.mult))
                dve.wait_ge(s_osb, t + 1)
                link(dve.tensor_tensor(sq[0:n, :], o, o, ALU.mult))
                dve.reduce_sum(r4[0:n, 0, t, :], sq[0:n, :].rearrange("p (h v) -> p h v", h=GH), AX.X).then_inc(s_ssq, 1)
                link(dve.tensor_tensor(sil[0:n, :].rearrange("p (h v) -> p h v", h=GH),
                                       sil[0:n, :].rearrange("p (h v) -> p h v", h=GH), bcast(ggla[0:n, :], 1, GH), ALU.mult))
                dve.wait_ge(s_r4, t + 1)
                link(dve.tensor_tensor(o4, o4, bcast(r4[0:n, 1, t, :], 2, DV), ALU.mult))
                dve.tensor_tensor(o, o, sil[0:n, :], ALU.mult).then_inc(s_mix, 1)

            for ci in range(SEQ // CHUNK):
                dve.wait_ge(s_u, ci + 1)
                dve.wait_ge(s_s, ci + 1)
                state_step(st[:, (ci + 1) % 2], st[:, ci % 2], 4 + ci % 2, ci).then_inc(s_s, 1)
                if ci % 2 == 1 and ci >= 3:
                    finish_tile(ci // 2 - 1)
            for b in range(NSEQ):
                if b >= 2:
                    dve.wait_ge(s_ub, b - 1)
                dve.tensor_scalar(kb[0:64, b % 2, :], kt[0:64, ST, :], core.const("seq_of")[0:64, b:b + 1], None,
                                  ALU.mult).then_inc(s_kb, 1)
                if b == 0:
                    finish_tile(ST - 1)
                if b >= 1:
                    dve.wait_ge(s_ub, b)
                    state_step(ss[:, b - 1], ss[:, b - 1], (b - 1) % 2, 8 + b - 1).then_inc(s_sb, 1)
            dve.wait_ge(s_ub, NSEQ)
            state_step(ss[:, NSEQ - 1], ss[:, NSEQ - 1], (NSEQ - 1) % 2, 8 + NSEQ - 1).then_inc(s_sb, 1)
            finish_tile(ST)


def compress(core):
    nc, io, ps = core.nc, core.io, core.psum
    proj, ident = core.proj, core.const("ident")
    own = Stack(core, core.z0, core.z1)
    NB = NCMP_S
    core.kc = own.take((NSEQ + 1) * NB).rearrange("p (s n) -> p s n", n=NB)
    core.vc = own.take((NSEQ + 1) * P).rearrange("p (s n) -> p s n", n=P)
    kc, vc = core.kc, core.vc
    core.z_att = own.at
    CL = 2 * GAPS
    phi = own.take(2 * CL * P).rearrange("p (c l n) -> p c l n", c=2, l=CL)
    rows = own.take(4 * 256).rearrange("p (u n) -> p u n", u=4)
    kvT = own.take(2 * 2 * PAST).rearrange("p (c s n) -> p c s n", c=2, s=2)
    pe_in, peT, peb = own.take(P), own.take(2 * CL), own.take(2)
    vT = own.take(2 * NB).rearrange("p (s n) -> p s n", n=NB)
    table = own.take(64).bitcast(I32)
    NPG = NSEQ * PAST // PAGE
    PPG = 2 * PAST // PAGE
    NGRP = NSEQ // 2

    s_in, s_zero, s_pt = (core.sem(n) for n in ("phi_in", "phi_zeroed", "table_in"))
    s_page = [core.sem(f"page_in{i}") for i in range(4)]
    s_tr, s_tra, s_trd, s_acc = (core.sem(n) for n in ("kvT_ps", "kvT_by_act", "kvT_by_dve", "cmp_ps"))
    s_peT, s_pec, s_peb, s_pebc = (core.sem(n) for n in ("peT_ps", "peT_ready", "pe_bias_ps", "pe_bias"))
    s_kc, s_vt, s_vtp, s_vc = (core.sem(n) for n in ("kc_ready", "vT_ready", "vc_ps", "vc_ready"))
    cache = io["cache_cmp"].rearrange("a n t c h d -> (a n) t (c h d)")

    with nc.Block() as block:
        def results(act, g):
            n = 2 if g < NGRP else 1
            nb = NB if g < NGRP else NCMP_P
            act.wait_ge(s_acc, g + 1)
            src = [ps[:, 4 + 2 * c + g % 2, 0:n * nb].rearrange("p (s n) -> p s n", n=nb) for c in range(2)]
            act.activation(kc[:, 2 * g:2 * g + n, 0:nb], src[0], ACT.Identity, bias=peb[:, 0:1]).then_inc(s_kc, 1)
            if g > 0:
                act.wait_ge(s_vtp, g)
            act.activation(vT[:, 0:n, 0:nb], src[1], ACT.Identity, bias=peb[:, 1:2]).then_inc(s_vt, 1)

        def kv_copy(eng, i, copy):
            g, r = divmod(i, PPG // 2)
            s, q = divmod(r, PPG // 4)
            if r < 2 and g > 0:
                eng.wait_ge(s_acc, g)
            return copy(kvT[:, :, s, q * 2 * PAGE:(q + 1) * 2 * PAGE], ps[:, i % 4, :].rearrange("p (c n) -> p c n", c=2))

        def v_out(dve, g):
            n = 2 if g < NGRP else 1
            nb = NB if g < NGRP else NCMP_P
            dve.wait_ge(s_vtp, g + 1)
            dve.tensor_copy(vc[0:nb, 2 * g:2 * g + n, :],
                            ps[0:nb, 6 + g % 2, 256:256 + n * P].rearrange("p (s n) -> p s n", n=P)).then_inc(s_vc, 1)

        @block.gpsimd
        def _(pool):
            for h in range(KVH):
                pool.memset(phi[64 * h:64 * h + 64, :, :, 64 * (1 - h):64 * (1 - h) + 64], 0.0).then_inc(s_zero, 1)

        @block.scalar
        def _(act):
            for h in range(KVH):
                for c in range(2):
                    act.dma_start(phi[64 * h:64 * h + 64, c, :, 64 * h:64 * h + 64],
                                  io["phi_w"][0, c].rearrange("(l d) n -> d l n", d=HD)).then_inc(s_in, 16)
                act.dma_start(pe_in[0:2 * CL, 64 * h:64 * h + 64],
                              io["phi_pe"].rearrange("a c l d -> (a c l) d")).then_inc(s_in, 16)
            act.wait_ge(s_peb, 1)
            act.activation(peb, ps[:, 5, 0:2], ACT.Copy).then_inc(s_pebc, 1)
            act.wait_ge(s_pebc, 1)
            for i in range(NGRP * PPG // 2 + 2):
                if i % 2 == 0:
                    act.wait_ge(s_tr, i + 1)
                    kv_copy(act, i, lambda o, s: act.activation(o, s, ACT.Copy)).then_inc(s_tra, 1)
                g, r = divmod(i, PPG // 2)
                if g > 0 and r == 1:
                    results(act, g - 1)
            results(act, NGRP)

        @block.vector
        def _(dve):
            dve.wait_ge(s_peT, 1)
            dve.tensor_copy(peT, ps[:, 4, 0:2 * CL]).then_inc(s_pec, 1)
            for i in range(NGRP * PPG // 2 + 2):
                if i % 2 == 1:
                    dve.wait_ge(s_tr, i + 1)
                    kv_copy(dve, i, dve.tensor_copy).then_inc(s_trd, 1)
                g, r = divmod(i, PPG // 2)
                if g > 0 and r == 1:
                    v_out(dve, g - 1)
            v_out(dve, NGRP)

        @block.tensor
        def _(pe):
            pe.wait_ge(s_in, 96)
            pe.transpose(ps[:, 4, 0:2 * CL], pe_in[0:2 * CL, :], ident[0:2 * CL, 0:2 * CL]).then_inc(s_peT, 1)
            pe.wait_ge(s_pec, 1)
            pe.wait_ge(s_zero, 2)
            for c in range(2):
                for l in range(CL):
                    last = pe.matmul(ps[:, 5, c:c + 1], phi[:, c, l, :], peT[:, c * CL + l:c * CL + l + 1],
                                     start=(l == 0), stop=(l == CL - 1))
            last.then_inc(s_peb, 1)

            def accumulate(g):
                n = 2 if g < NGRP else 1
                nb = NB if g < NGRP else NCMP_P
                done = (g + 1) * PPG // 4 if g < NGRP else NGRP * PPG // 4 + 1
                pe.wait_ge(s_tra, done)
                pe.wait_ge(s_trd, done)
                if g == 0:
                    pe.wait_ge(s_pebc, 1)
                if g >= 2:
                    pe.wait_ge(s_vt, g - 1)
                    pe.wait_ge(s_vc, g - 1)
                for c in range(2):
                    for l in range(CL):
                        last = pe.matmul(ps[:, 4 + 2 * c + g % 2, 0:n * nb].rearrange("p (s n) -> p s n", n=nb),
                                         phi[:, c, l, :], kvT[:, c, 0:n, l:l + GAPS * (nb - 1) + 1:GAPS],
                                         start=(l == 0), stop=(l == CL - 1))
                last.then_inc(s_acc, 1)

            def v_back(g):
                n = 2 if g < NGRP else 1
                nb = NB if g < NGRP else NCMP_P
                pe.wait_ge(s_vt, g + 1)
                for s in range(n):
                    last = pe.transpose(ps[0:nb, 6 + g % 2, 256 + s * P:256 + (s + 1) * P], vT[:, s, 0:nb], ident)
                last.then_inc(s_vtp, 1)

            for i in range(NGRP * PPG // 2 + 2):
                g, r = divmod(i, PPG // 2)
                if i >= 4:
                    pe.wait_ge(s_tra if i % 2 == 0 else s_trd, (i - 4) // 2 + 1)
                for u in range(2):
                    k = 2 * i + u
                    if g < NGRP:
                        pe.wait_ge(s_page[k % 4], 16 * (k // 4 + 1))
                    for c in range(2):
                        src = (rows[:, k % 4, c * P:(c + 1) * P] if g < NGRP
                               else proj[:, 2 * r + u, C_KC + c * P:C_KC + (c + 1) * P])
                        last = pe.transpose(ps[:, i % 4, c * 256 + u * P:c * 256 + (u + 1) * P], src, ident)
                last.then_inc(s_tr, 1)
                if r == PPG // 2 - 1:
                    accumulate(g)
                if g > 0 and r == 1:
                    v_back(g - 1)
            accumulate(NGRP)
            v_back(NGRP)

        @block.sync
        def _(sp):
            sp.dma_start(table[0:1, 0:NPG], io["page_table"].rearrange("b n -> (b n)").unsqueeze(0)).then_inc(s_pt, 16)
            sp.wait_ge(s_pt, 16)

            def load(k, u):
                page = sp.value_load(table[0:1, bass.ds(k, 1)] if not isinstance(k, int) else table[0:1, k:k + 1],
                                     min_val=0, max_val=cache.shape[0] - 1)
                sp.dma_start(rows[:, u, :], cache[bass.ds(page, 1), :, :].rearrange("n t c -> (n t) c")
                             ).then_inc(s_page[u], 16)
            for u in range(4):
                load(u, u)
            with sp.Fori(1, NPG // 4) as q:
                for u in range(4):
                    if u % 2 == 0:
                        sp.wait_ge(s_tr, 2 * (q - 1) + u // 2 + 1)
                    load(4 * q + u, u)


BIG = 1e28


def prompt_attention(core):
    nc, io, ps = core.nc, core.io, core.psum
    proj, feat, mix, ident, kc, vc = core.proj, core.feat, core.mix, core.const("ident"), core.kc, core.vc
    own = Stack(core, core.z_att, core.z1)
    core.gates = own.take(NT * 24).rearrange("p (t n) -> p t n", t=NT)
    core.identb = own.take(P // 2).bitcast(BF16)
    core.maskb = own.take((P + 256 + 8 + 8 * NCMP_P) // 2).bitcast(BF16)
    core.z_samp = own.at
    gates, identb, maskb = core.gates, core.identb, core.maskb
    kz = own.take(2 * KVH * SEQ).rearrange("p (b h n) -> p b h n", b=2, h=KVH)
    kzc = own.take(KVH * NCMP_P)
    pp = own.take(2 * 2 * KVH * SEQ).rearrange("p (u b h n) -> p u b h n", u=2, b=2, h=KVH)
    pc = own.take(2 * KVH * NCMP_P).rearrange("p (u h n) -> p u h n", u=2, h=KVH)
    pT = own.take(2 * 4 * P).rearrange("p (u k n) -> p u k n", u=2, k=4)
    mx = own.take(2 * 6).rearrange("p (u n) -> p u n", u=2)
    su = own.take(2 * 6).rearrange("p (u n) -> p u n", u=2)
    co = own.take(2 * 6).rearrange("p (u n) -> p u n", u=2)
    tmp = own.take(6 * HD).rearrange("p (b n) -> p b n", b=6)
    NU = (SEQ // P) * GRP
    SC = HD ** -0.5

    s_zero, s_prep, s_ge = core.sem("kz_zeroed"), core.sem("prompt_prep"), core.sem("gates_exp")
    s_scw, s_scs, s_scc = core.sem("win_scores"), core.sem("sel_scores"), core.sem("cmp_scores")
    s_mx, s_p = core.sem("max_ready"), core.sem("probs_ready")
    s_pt, s_pta, s_ptd, s_o, s_ou = (core.sem(n) for n in ("pT_ps", "pT_by_act", "pT_by_dve", "po_ps", "po_used"))
    s_dve = core.sem("dve_p4")
    NR = 5

    with nc.Block() as block:
        @block.gpsimd
        def _(pool):
            for h in range(KVH):
                rows = slice(64 * (1 - h), 64 * (1 - h) + 64)
                pool.memset(kz[rows, :, h, :], 0.0).then_inc(s_zero, 1)
                pool.memset(kzc[rows, h * NCMP_P:(h + 1) * NCMP_P], 0.0).then_inc(s_zero, 1)

        def move_pT(eng, k, copy):
            u, r = divmod(k, NR)
            nb = u // GRP + 1
            eng.wait_ge(s_pt, k + 1)
            if r == 0:
                return copy(pT[0:NCMP_P, k % 2, 0:KVH, :],
                            ps[0:NCMP_P, 5 + k % 2, 0:KVH * P].rearrange("p (k n) -> p k n", n=P))
            return copy(pT[:, k % 2, 0:nb, :], ps[:, 5 + k % 2, 0:nb * P].rearrange("p (k n) -> p k n", n=P))

        @block.scalar
        def _(act):
            act.activation(gates[:, 0:ST, :], proj[:, 0:ST, C_NG:C_NG + 24], ACT.Exp, scale=-1.0)
            act.activation(gates[0:64, ST, :], proj[0:64, ST, C_NG:C_NG + 24], ACT.Exp, scale=-1.0).then_inc(s_ge, 1)

            def exps(u):
                nk = (u // GRP + 1) * P
                act.wait_ge(s_mx, u + 1)
                for h in range(KVH):
                    act.activation(pc[:, u % 2, h, :], ps[:, 4, h * NCMP_P:(h + 1) * NCMP_P], ACT.Exp, scale=SC,
                                   bias=mx[:, u % 2, h:h + 1], accum_out=su[:, u % 2, h:h + 1])
                for b in range(2):
                    for h in range(KVH):
                        last = act.activation(pp[:, u % 2, b, h, 0:nk], ps[:, 2 * b + h, 0:nk], ACT.Exp, scale=SC,
                                              bias=mx[:, u % 2, 2 + 2 * b + h:3 + 2 * b + h],
                                              accum_out=su[:, u % 2, 2 + 2 * b + h:3 + 2 * b + h])
                last.then_inc(s_p, 1)

            exps(0)
            for u in range(NU):
                if u + 1 < NU:
                    exps(u + 1)
                for k in range(NR * u, NR * u + NR):
                    if k % 2 == 0:
                        move_pT(act, k, lambda o, s: act.activation(o, s, ACT.Copy)).then_inc(s_pta, 1)

        @block.vector
        def _(dve):
            link = linker(dve, s_dve)
            dve.wait_ge(s_zero, 4)
            for h in range(KVH):
                rows = slice(64 * h, 64 * h + 64)
                dve.tensor_copy(kz[rows, 0, h, :], feat[rows, KSF, 0:SEQ])
                dve.tensor_copy(kz[rows, 1, h, :], feat[rows, KWF, 0:SEQ])
                dve.tensor_copy(kzc[rows, h * NCMP_P:(h + 1) * NCMP_P], kc[rows, NSEQ, 0:NCMP_P])
            dve.tensor_copy(identb, ident)
            at = 0
            for name in ("causal", "new_keys", "win_old", "cmp_p"):
                m = core.const(name)
                last = dve.tensor_copy(maskb[:, at:at + m.shape[1]], m)
                at += m.shape[1]
            last.then_inc(s_prep, 1)
            dve.wait_ge(s_ge, 1)
            for g in (gates[:, 0:ST, :], gates[0:64, ST, :]):
                link(dve.tensor_scalar(g, g, 1.0, None, ALU.add))
                link(dve.reciprocal(g, g))

            def maxima(u):
                nk = (u // GRP + 1) * P
                m = mx[:, u % 2, :]
                dve.wait_ge(s_scc, u + 1)
                if u >= 2:
                    dve.wait_ge(s_p, u - 1)
                dve.tensor_reduce(m[:, 0:2], ps[:, 4, 0:KVH * NCMP_P].rearrange("p (h n) -> p h n", h=KVH), AX.X, ALU.max)
                dve.wait_ge(s_scs, u + 1)
                dve.tensor_reduce(m[:, 2:4], ps[:, 0:2, 0:nk], AX.X, ALU.max)
                dve.wait_ge(s_scw, u + 1)
                link(dve.tensor_reduce(m[:, 4:6], ps[:, 2:4, 0:nk], AX.X, ALU.max))
                dve.tensor_scalar(m, m, -SC, BIG, ALU.mult, ALU.min).then_inc(s_mx, 1)

            maxima(0)
            for u in range(NU):
                t, g = divmod(u, GRP)
                if u + 1 < NU:
                    maxima(u + 1)
                for k in range(NR * u, NR * u + NR):
                    if k % 2 == 1:
                        move_pT(dve, k, dve.tensor_copy).then_inc(s_ptd, 1)
                dve.wait_ge(s_p, u + 1)
                c, s = co[:, u % 2, :], su[:, u % 2, :]
                link(dve.tensor_scalar(c, s, 1e-30, None, ALU.max))
                link(dve.reciprocal(c, c))
                gv = gates[:, t, :].rearrange("p (h g b) -> p b h g", h=KVH, g=GRP)[:, :, :, g]
                cv = c.rearrange("p (b h) -> p b h", h=KVH)
                link(dve.tensor_tensor(cv, cv, gv, ALU.mult))
                dve.wait_ge(s_o, u + 1)
                o = ps[:, 7, 0:6 * HD].rearrange("p (b n) -> p b n", b=6)
                dve.tensor_tensor(tmp, o, bcast(c, 2, HD), ALU.mult).then_inc(s_ou, 1)
                dve.wait_ge(s_ou, u + 1)
                dst = mix[:, t, 512:1024].rearrange("p (h g d) -> p g h d", h=KVH, g=GRP)[:, g]
                link(dve.tensor_tensor(dst, tmp[:, 0:2, :], tmp[:, 2:4, :], ALU.add))
                link(dve.tensor_tensor(dst, dst, tmp[:, 4:6, :], ALU.add))

        @block.tensor
        def _(pe):
            cmp_at = P + 256 + 8

            def scores(u):
                t, g = divmod(u, GRP)
                nk = (t + 1) * P
                q = feat[:, QN + g, t * P:(t + 1) * P]
                if u >= 1:
                    pe.wait_ge(s_p, u)
                pe.matmul(ps[:, 4, 0:KVH * NCMP_P], q, kzc, start=True, stop=False)
                pe.matmul(ps[:, 4, 0:KVH * NCMP_P], identb,
                          maskb[:, cmp_at + t * 2 * NCMP_P:cmp_at + (t + 1) * 2 * NCMP_P],
                          start=False, stop=True).then_inc(s_scc, 1)
                for b, sem in enumerate((s_scs, s_scw)):
                    for h in range(KVH):
                        pe.matmul(ps[:, 2 * b + h, 0:nk], q, kz[:, b, h, 0:nk], start=True, stop=False)
                        last = pe.matmul(ps[:, 2 * b + h, nk - P:nk], identb, maskb[:, 0:P], start=False, stop=True)
                    last.then_inc(sem, 1)

            def to_key_major(k):
                u, r = divmod(k, NR)
                if k >= 2:
                    pe.wait_ge(s_pta if k % 2 == 0 else s_ptd, (k - 2) // 2 + 1)
                if r == 0:
                    for h in range(KVH):
                        last = pe.transpose(ps[0:NCMP_P, 5 + k % 2, h * P:(h + 1) * P], pc[:, u % 2, h, :], ident)
                else:
                    b, h = divmod(r - 1, KVH)
                    for kb in range(u // GRP + 1):
                        last = pe.transpose(ps[:, 5 + k % 2, kb * P:(kb + 1) * P],
                                            pp[:, u % 2, b, h, kb * P:(kb + 1) * P], ident)
                last.then_inc(s_pt, 1)

            def values(k):
                u, r = divmod(k, NR)
                pe.wait_ge(s_pta if k % 2 == 0 else s_ptd, k // 2 + 1)
                if r == 0 and u >= 1:
                    pe.wait_ge(s_ou, u)
                if r == 0:
                    for h in range(KVH):
                        last = pe.matmul(ps[:, 7, h * HD:(h + 1) * HD], pT[0:NCMP_P, k % 2, h, :],
                                         vc[0:NCMP_P, NSEQ, h * HD:(h + 1) * HD], start=True, stop=True)
                else:
                    b, h = divmod(r - 1, KVH)
                    c0 = (C_KS, C_KW)[b] + P + h * HD
                    nb = u // GRP + 1
                    for kb in range(nb):
                        last = pe.matmul(ps[:, 7, (2 + 2 * b + h) * HD:(3 + 2 * b + h) * HD], pT[:, k % 2, kb, :],
                                         proj[:, kb, c0:c0 + HD], start=(kb == 0), stop=(kb == nb - 1))
                if r == NR - 1:
                    last.then_inc(s_o, 1)

            pe.wait_ge(s_prep, 1)
            scores(0)
            for u in range(NU):
                if u + 1 < NU:
                    scores(u + 1)
                else:
                    pe.wait_ge(s_p, u + 1)
                for r in range(NR):
                    to_key_major(NR * u + r)
                    if r >= 1:
                        values(NR * u + r - 1)
                values(NR * u + NR - 1)


def sample_attention(core):
    nc, io, ps = core.nc, core.io, core.psum
    proj, feat, mix, ident, kc, vc = core.proj, core.feat, core.mix, core.const("ident"), core.kc, core.vc
    gates, identb, maskb = core.gates, core.identb, core.maskb
    own = Stack(core, core.z_samp, core.z1)
    NP, R = PAST // PAGE, NSEQ * TS
    NWT = SEQ // P
    NKS, NKW = PAST + R, SEQ + R
    qs = own.take(NSEQ * 64).rearrange("p (b n) -> p b n", b=NSEQ)
    grow = own.take(NSEQ // 2 * 3).rearrange("p (i b) -> p i b", b=3)
    sel = own.take(4 * NP * 256).rearrange("p (u k n) -> p u k n", u=4, k=NP)
    win = proj[:, 0:ST, 0:NWT * 256].rearrange("p u (k n) -> p u k n", k=NWT)
    kTs = own.take(2 * PAST).rearrange("p (s n) -> p s n", s=2)
    kTw = own.take(2 * SEQ).rearrange("p (s n) -> p s n", s=2)
    ss, ws, pc = own.take(NKS), own.take(NKW), own.take(64)
    pT = own.take(16 * P).rearrange("p (k n) -> p k n", k=16)
    im, sc, sc2, v8, bm = own.take(16), own.take(16), own.take(16), own.take(8), own.take(16)
    mx, su, co = own.take(3), own.take(3), own.take(3)
    res = own.take(2 * P).rearrange("p (u n) -> p u n", u=2)
    table = own.take(64).bitcast(I32)
    nsa_d = nc.dram_tensor("nsa_rows", [KVH, GRP, NSEQ, TS, HD], F32).ap()
    gate_d = nc.dram_tensor("gate_rows", [R, 24], F32).ap()
    cache = io["cache_sel"].rearrange("a n t c h d -> (a n) t (c h d)")
    old_win = io["state_win"].rearrange("a b (k p) c h d -> (a b) p k (c h d)", p=P)
    NU, SC = NSEQ // 2, HD ** -0.5
    A, C, W, O, T0 = 0, 2, 3, 4, 5

    rounds = [("k", 0, r) for r in range(6)]
    for i in range(NU):
        if i + 1 < NU:
            rounds += [("k", i + 1, r) for r in range(6)]
        rounds += [("p", i, r) for r in range(4)]
    number = {x: n for n, x in enumerate(rounds)}

    s_zero, s_q, s_pt, s_gd, s_gr = (core.sem(n) for n in ("qs_zeroed", "qs_ready", "table2_in", "gates_out", "gate_rows_in"))
    s_vin = [core.sem(f"sel_in{i}") for i in range(4)]
    s_win = [core.sem(f"old_win_in{i}") for i in range(4)]
    s_tr, s_ea, s_ed = core.sem("tr_ps"), core.sem("tr_by_act"), core.sem("tr_by_dve")
    s_sc, s_cc, s_wc, s_mc, s_ec = (core.sem(n) for n in ("scores_ps", "small_copied", "win_copied", "cmp_max", "cmp_exp"))
    s_im, s_imp, s_pn = core.sem("imp_rows"), core.sem("imp_ps"), core.sem("cmp_normed")
    s_ms, s_mw, s_es, s_ew = (core.sem(n) for n in ("sel_max", "win_max", "sel_exp", "win_exp"))
    s_pv, s_res, s_back = (core.sem(n) for n in ("pv_ps", "res_ready", "nsa_in"))
    s_rout = [core.sem(f"res_out{u}") for u in range(2)]
    s_dve = core.sem("dve_p5")

    def evacuate(eng, n, copy):
        kind, i, r = rounds[n]
        src = ps[:, T0 + n % 3, :]
        eng.wait_ge(s_tr, n + 1)
        if kind == "p":
            rows = 64 if r == 2 else P
            nb = 3 if r == 2 else 4
            return copy(pT[0:rows, 4 * r:4 * r + nb, :], src[0:rows, 0:nb * P].rearrange("p (k n) -> p k n", n=P))
        s, q = divmod(r, 3)
        if q < 2:
            return copy(kTs[:, s, q * 512:(q + 1) * 512], src)
        return copy(kTw[:, s, :], src)

    def by_act(n):
        return n % 2 == 0

    with nc.Block() as block:
        @block.sync
        def _(sp):
            sp.dma_start(table[0:1, 0:NSEQ * NP], io["page_table"].rearrange("b n -> (b n)").unsqueeze(0)).then_inc(s_pt, 16)
            sp.dma_start(gate_d, gates[0:R, ST, :]).then_inc(s_gd, 16)
            sp.wait_ge(s_pt, 16)

            def load(b):
                if b >= 4:
                    sp.wait_ge(s_pv, (b - 4) // 2 + 1)
                for k in range(NP):
                    page = sp.value_load(table[0:1, b * NP + k:b * NP + k + 1], min_val=0, max_val=cache.shape[0] - 1)
                    sp.dma_start(sel[:, b % 4, k, :], cache[bass.ds(page, 1), :, :].rearrange("n t c -> (n t) c")
                                 ).then_inc(s_vin[b % 4], 16)
                sp.dma_start(win[:, b % 4, :, :], old_win[b]).then_inc(s_win[b % 4], 16)

            load(0)
            load(1)
            sp.wait_ge(s_gd, 16)
            for b in range(NSEQ):
                sp.dma_start(grow[64 * (b % 2):64 * (b % 2) + 64, b // 2, :],
                             gate_d[TS * b:TS * b + TS, :].rearrange("t (q b) -> q t b", b=3)).then_inc(s_gr, 16)
            for b in range(2, NSEQ):
                load(b)
            for u in range(2):
                sp.wait_ge(s_rout[u], 64 * NU // 2)
            sp.dma_start(mix[0:R, ST, 512:1024].rearrange("p (q d) -> p q d", d=HD),
                         nsa_d.rearrange("h g b t d -> (b t) (h g) d")).then_inc(s_back, 16)
            sp.wait_ge(s_back, 16)

        @block.gpsimd
        def _(pool):
            pool.memset(qs, 0.0).then_inc(s_zero, 1)
            pool.memset(pc, 0.0).then_inc(s_zero, 1)
            for i in range(NU):
                pool.wait_ge(s_res, i + 1)
                for s in range(2):
                    for h in range(KVH):
                        pool.dma_start(nsa_d[h, :, 2 * i + s, :, :],
                                       res[64 * s + 32 * h:64 * s + 32 * h + 32, i % 2, h * HD:(h + 1) * HD]
                                       ).then_inc(s_rout[i % 2], 16)

        @block.scalar
        def _(act):
            def copy(o, s):
                return act.activation(o, s, ACT.Copy)

            def turn(ns):
                for n in ns:
                    if by_act(n):
                        evacuate(act, n, copy).then_inc(s_ea, 1)

            turn(range(6))
            for i in range(NU):
                act.wait_ge(s_sc, i + 1)
                if i > 0:
                    act.wait_ge(s_tr, number[("p", i - 1, 3)] + 1)
                act.activation(ws[:, 0:SEQ], ps[:, W, :], ACT.Copy).then_inc(s_wc, 1)
                act.wait_ge(s_mc, i + 1)
                act.activation(pc[:, 0:NCMP_S], pc[:, 0:NCMP_S], ACT.Exp, scale=SC, bias=mx[:, 0:1],
                               accum_out=su[:, 0:1]).then_inc(s_ec, 1)
                act.wait_ge(s_mw, i + 1)
                act.activation(ws, ws, ACT.Exp, scale=SC, bias=mx[:, 2:3], accum_out=su[:, 2:3]).then_inc(s_ew, 1)
                act.wait_ge(s_ms, i + 1)
                act.activation(ss, ss, ACT.Exp, scale=SC, bias=mx[:, 1:2], accum_out=su[:, 1:2]).then_inc(s_es, 1)
                if i + 1 < NU:
                    turn(number[("k", i + 1, r)] for r in range(6))
                turn(number[("p", i, r)] for r in range(4))

        @block.vector
        def _(dve):
            link = linker(dve, s_dve)

            def turn(ns):
                for n in ns:
                    if not by_act(n):
                        evacuate(dve, n, dve.tensor_copy).then_inc(s_ed, 1)

            dve.wait_ge(s_zero, 2)
            for h in range(KVH):
                rows = slice(64 * h, 64 * h + 64)
                for g in range(GRP):
                    last = dve.tensor_copy(qs[rows, :, 32 * h + 8 * g:32 * h + 8 * g + 8],
                                           feat[rows, QN + g, SEQ:NTOK].rearrange("p (b t) -> p b t", t=TS))
            last.then_inc(s_q, 1)
            turn(range(6))
            for i in range(NU):
                dve.wait_ge(s_sc, i + 1)
                if i > 0:
                    dve.wait_ge(s_tr, number[("p", i - 1, 3)] + 1)
                link(dve.tensor_copy(pc[:, 0:NCMP_S], ps[:, C, 0:NCMP_S]))
                dve.tensor_copy(ss[:, PAST:NKS], ps[:, C, 64:64 + R])
                dve.tensor_copy(ws[:, SEQ:NKW], ps[:, C, 128:128 + R]).then_inc(s_cc, 1)
                link(dve.tensor_reduce(mx[:, 0:1], pc[:, 0:NCMP_S], AX.X, ALU.max))
                dve.tensor_scalar(mx[:, 0:1], mx[:, 0:1], -SC, BIG, ALU.mult, ALU.min).then_inc(s_mc, 1)
                dve.wait_ge(s_cc, i + 1)
                dve.wait_ge(s_wc, i + 1)
                link(dve.tensor_reduce(mx[:, 2:3], ws, AX.X, ALU.max))
                dve.tensor_scalar(mx[:, 2:3], mx[:, 2:3], -SC, BIG, ALU.mult, ALU.min).then_inc(s_mw, 1)
                dve.wait_ge(s_ec, i + 1)
                link(dve.tensor_scalar(co[:, 0:1], su[:, 0:1], 1e-30, None, ALU.max))
                link(dve.reciprocal(co[:, 0:1], co[:, 0:1]))
                link(dve.tensor_scalar(pc[:, 0:NCMP_S], pc[:, 0:NCMP_S], co[:, 0:1], None, ALU.mult))
                link(dve.tensor_reduce(im, pc.rearrange("p (j n) -> p j n", n=4), AX.X, ALU.add))
                dve.tensor_tensor(im[:, 1:16], im[:, 1:16], pc[:, 3:63:4], ALU.add).then_inc(s_im, 1)
                dve.wait_ge(s_imp, i + 1)
                link(dve.tensor_copy(sc, ps[:, O, 384:400]))
                link(dve.memset(sc[:, 0:16:15], -1.0))
                link(dve.max(v8, sc))
                link(dve.memset(v8[:, 5:8], 3e38))
                link(dve.match_replace(sc2, v8, sc, -2.0))
                link(dve.tensor_scalar(bm, sc2, -2.0, None, ALU.is_equal))
                link(dve.tensor_scalar(bm, bm, -1.0, -NEG, ALU.add, ALU.mult))
                link(dve.memset(bm[:, 0:16:15], 0.0))
                link(dve.tensor_tensor(ss[:, 0:PAST].rearrange("p (k n) -> p k n", k=NBLK_S),
                                       ps[:, A:A + 2, :].rearrange("p a n -> p (a n)").rearrange("p (k n) -> p k n", k=NBLK_S),
                                       bcast(bm, 2, 64), ALU.add))
                link(dve.tensor_reduce(mx[:, 1:2], ss, AX.X, ALU.max))
                dve.tensor_scalar(mx[:, 1:2], mx[:, 1:2], -SC, BIG, ALU.mult, ALU.min).then_inc(s_ms, 1)
                if i + 1 < NU:
                    turn(number[("k", i + 1, r)] for r in range(6))
                turn(number[("p", i, r)] for r in range(4))
                dve.wait_ge(s_ew, i + 1)
                dve.wait_ge(s_es, i + 1)
                link(dve.tensor_scalar(co[:, 1:3], su[:, 1:3], 1e-30, None, ALU.max))
                link(dve.reciprocal(co[:, 1:3], co[:, 1:3]))
                dve.wait_ge(s_gr, 16 * NSEQ)
                link(dve.tensor_tensor(co[:, 1:3], co[:, 1:3], grow[:, i, 1:3], ALU.mult))
                dve.wait_ge(s_pv, i + 1)
                if i >= 2:
                    dve.wait_ge(s_rout[i % 2], 64 * (i // 2))
                r = res[:, i % 2, :]
                link(dve.tensor_scalar(r, ps[:, O, 0:P], grow[:, i, 0:1], None, ALU.mult))
                link(dve.scalar_tensor_tensor(r, ps[:, O, P:2 * P], co[:, 1:2], r, ALU.mult, ALU.add))
                dve.scalar_tensor_tensor(r, ps[:, O, 2 * P:3 * P], co[:, 2:3], r, ALU.mult, ALU.add).then_inc(s_res, 1)

        @block.tensor
        def _(pe):
            def take_bank(n):
                if n >= 3:
                    m = n - 3
                    pe.wait_ge(s_ea if by_act(m) else s_ed, sum(by_act(x) == by_act(m) for x in range(m + 1)))

            def evacuated(n):
                pe.wait_ge(s_ea, sum(by_act(x) for x in range(n + 1)))
                pe.wait_ge(s_ed, sum(not by_act(x) for x in range(n + 1)))

            def keys(i):
                for r in range(6):
                    n = number[("k", i, r)]
                    s, q = divmod(r, 3)
                    b = 2 * i + s
                    if q == 0:
                        pe.wait_ge(s_vin[b % 4], 16 * NP * (b // 4 + 1))
                    if q == 2:
                        pe.wait_ge(s_win[b % 4], 16 * (b // 4 + 1))
                    take_bank(n)
                    for k in range(4):
                        src = sel[:, b % 4, 4 * q + k, 0:P] if q < 2 else win[:, b % 4, k, 0:P]
                        last = pe.transpose(ps[:, T0 + n % 3, k * P:(k + 1) * P], src, ident)
                    last.then_inc(s_tr, 1)

            def scores(i):
                evacuated(number[("k", i, 5)])
                if i > 0:
                    pe.wait_ge(s_ms, i)
                    pe.wait_ge(s_mw, i)
                nm = maskb[:, P + 64 * i:P + 64 * i + R]
                old = maskb[:, P + 256:P + 256 + TS]

                def rows(s, bank, a, b, rhs, stop):
                    return pe.matmul(ps[64 * s:64 * s + 64, bank, a:b], qs[:, 2 * i + s, :], rhs, start=True, stop=stop)
                for s in range(2):
                    last = rows(s, C, 0, NCMP_S, kc[:, 2 * i + s, :], True)
                for a, slot in ((64, KSF), (128, KWF)):
                    for s in range(2):
                        rows(s, C, a, a + R, feat[:, slot, SEQ:NTOK], False)
                    pe.matmul(ps[:, C, a:a + R], identb, nm, start=False, stop=True)
                for s in range(2):
                    rows(s, W, 0, SEQ, kTw[:, s, :], False)
                pe.matmul(ps[:, W, 0:TS], identb, old, start=False, stop=True)
                for half in range(2):
                    for s in range(2):
                        last = rows(s, A + half, 0, 512, kTs[:, s, half * 512:(half + 1) * 512], True)
                last.then_inc(s_sc, 1)

            def weights(i):
                for r in range(4):
                    n = number[("p", i, r)]
                    if r == 0:
                        pe.wait_ge(s_es, i + 1)
                        pe.wait_ge(s_ew, i + 1)
                    take_bank(n)
                    if r == 0 and i > 0:
                        pe.wait_ge(s_pv, i)
                    srcs = {0: [ss[:, k * P:(k + 1) * P] for k in range(4)],
                            1: [ss[:, k * P:(k + 1) * P] for k in range(4, 8)],
                            2: [ss[:, PAST:NKS], ws[:, SEQ:NKW], pc],
                            3: [ws[:, k * P:(k + 1) * P] for k in range(4)]}[r]
                    for k, src in enumerate(srcs):
                        last = pe.transpose(ps[0:src.shape[1], T0 + n % 3, k * P:(k + 1) * P], src, ident)
                    last.then_inc(s_tr, 1)
                evacuated(number[("p", i, 3)])
                if i > 0:
                    pe.wait_ge(s_res, i)
                for s in range(2):
                    b, c = 2 * i + s, slice(64 * s, 64 * s + 64)

                    def group(br, terms):
                        for k, (w, v) in enumerate(terms):
                            last = pe.matmul(ps[c, O, br * P:(br + 1) * P], w, v, start=(k == 0), stop=(k == len(terms) - 1))
                        return last
                    group(0, [(pT[0:NCMP_S, 10, c], vc[0:NCMP_S, b, :])])
                    group(1, [(pT[:, k, c], sel[:, b % 4, k, P:256]) for k in range(NP)]
                          + [(pT[0:64, 8, c], proj[0:64, ST, C_KS + P:C_KS + 256])])
                    last = group(2, [(pT[:, 12 + k, c], win[:, b % 4, k, P:256]) for k in range(NWT)]
                                 + [(pT[0:64, 9, c], proj[0:64, ST, C_KW + P:C_KW + 256])])
                last.then_inc(s_pv, 1)

            pe.wait_ge(s_q, 1)
            keys(0)
            scores(0)
            for i in range(NU):
                pe.wait_ge(s_im, i + 1)
                if i > 0:
                    pe.wait_ge(s_res, i)
                pe.matmul(ps[:, O, 384:400], core.const("same_q"), im, start=True, stop=True).then_inc(s_imp, 1)
                if i + 1 < NU:
                    keys(i + 1)
                    scores(i + 1)
                weights(i)


def output_and_router(core):
    nc, io, ps = core.nc, core.io, core.psum
    x, mod, mix, ident = core.x, core.mod, core.mix, core.const("ident")
    own = Stack(core, core.pf, core.z1)
    core.gate2 = own.take(2 * D).rearrange("p (w n) -> p w n", w=2)
    core.blocks = own.take(NSLOT + 3).bitcast(I32)
    core.z_moe = own.at
    gate2 = core.gate2
    slot = own.take(NT * TOPK).bitcast(I32).rearrange("p (t j) -> p t j", t=NT)
    wt = own.take(NT * TOPK).rearrange("p (t j) -> p t j", t=NT)
    pair = own.take(NT * TOPK * 2).rearrange("p (t j w) -> p t j w", t=NT, j=TOPK)
    mixT = own.take(KT * NTOK).rearrange("p (k n) -> p k n", k=KT)
    wout = own.take(KT * D).rearrange("p (k n) -> p k n", k=KT)
    ex = own.take(6 * D).rearrange("p (w v n) -> p w v n", w=2, v=3)
    wr = own.take(KT * NE).rearrange("p (k n) -> p k n", k=KT)
    gffn, br, junk = own.take(D), own.take(NE), own.take(D)
    h2 = own.take(2 * D).rearrange("p (u n) -> p u n", u=2)
    h2T = own.take(KT * P).rearrange("p (k n) -> p k n", k=KT)
    stat = own.take(2 * NT)
    lg = own.take(NT * NE).rearrange("p (t e) -> p t e", t=NT)
    v8 = own.take(NT * 8).rearrange("p (t e) -> p t e", t=NT)
    i8 = own.take(NT * 8).bitcast(U32).rearrange("p (t e) -> p t e", t=NT)
    i8f = own.take(NT * TOPK).rearrange("p (t e) -> p t e", t=NT)
    nv0, wsum = own.take(NT), own.take(NT)
    oh = own.take(NT * TOPK * NE).rearrange("p (t j e) -> p t j e", t=NT, j=TOPK)
    selb = own.take(NT * NE // 2).bitcast(BF16).rearrange("p (t e) -> p t e", t=NT)
    beforeb, onesb = own.take(P // 2).bitcast(BF16), own.take(P // 2).bitcast(BF16)
    cnt, nblk, bend, base, ones = (own.take(NE) for _ in range(5))
    rk = own.take(NE)
    pick = own.take(TOPK * NE).rearrange("p (j e) -> p j e", j=TOPK)
    slotf = own.take(NT * TOPK).rearrange("p (t j) -> p t j", t=NT)
    cmpk = own.take((NSLOT + 1) * NE).rearrange("p (k e) -> p k e", e=NE)
    ek = own.take(NSLOT + 3)
    upper = Stack(core, core.z1 + NT * D, ARENA)
    b32 = own.take(3 * D)
    filler = own.take(BLK * 2).bitcast(I32).rearrange("p (c w) -> p c w", w=2)
    zero = upper.take(D)
    bparts = upper.take(3 * 3 * D // 2).bitcast(BF16).rearrange("p (a n) -> p a n", a=3)
    core.h2_d = nc.dram_tensor("h2_rows", [NTOK + BLK, D], F32).ap()
    core.ffn_d = nc.dram_tensor("ffn_rows", [NTOK + BLK, D], F32).ap()
    core.slot_d = nc.dram_tensor("slot_rows", [NSLOT * BLK, 2], I32).ap()
    core.bias_d = nc.dram_tensor("bias_parts", [NE, 3, 3 * D], BF16).ap()

    (s_w, s_wo, s_b, s_rt, s_exp, s_exa, s_exd, s_mt, s_mta, s_mtd, s_yp, s_res, s_rs, s_h, s_hd, s_hd1, s_htp, s_ht, s_lp,
     s_lg, s_nv, s_ew, s_ohr, s_rk, s_cnt, s_slot, s_blk, s_fill, s_bp, s_bo, s_wb, s_tok, s_zero, s_zo) = (core.sem(n) for n in (
         "g_ffn_in", "w_out_in", "biases_in", "router_in", "expand2_ps", "expand2_by_act", "expand2_by_dve", "mixT_ps",
         "mixT_by_act", "mixT_by_dve", "y_ps", "residual", "rstd2_ready", "h2_ready", "h2_out0", "h2_out1", "h2T_ps",
         "h2T_ready", "logits_ps", "logits_ready", "neg_max", "weights_exp", "chosen", "ranks_ps", "ranks_read",
         "slots_ready", "blocks_ready", "filler_ready", "bias_parts", "bias_out", "bf16_consts", "fillers_out", "zero_ready", "zeros_out"))
    s_dve, s_act, s_pool = core.sem("dve_p6"), core.sem("act_p6"), core.sem("pool_p6")
    s_scat = core.sem("slots_scattered")
    s_h2o = [s_hd, s_hd1]

    with nc.Block() as block:
        @block.sync
        def _(sp):
            sp.wait_ge(s_zero, 1)
            zeroed = 1
            sp.dma_start(core.h2_d[NTOK:, :], zero).then_inc(s_zo, 16)
            for t0 in range(0, NTOK + BLK, P):
                sp.dma_start(core.ffn_d[t0:min(t0 + P, NTOK + BLK), :], zero[0:min(P, NTOK + BLK - t0), :]).then_inc(s_zo, 16)
                zeroed += 1
            sp.dma_start(gffn, io["g_ffn"].to_broadcast([P, D])).then_inc(s_w, 16)
            sp.dma_start(wout, io["w_out"].rearrange("a (p k) n -> (a p) k n", k=KT)).then_inc(s_wo, 16)
            for i, name in enumerate(("b_gate", "b_up", "b_down")):
                sp.dma_start(b32[0:NE, i * D:(i + 1) * D], io[name][0]).then_inc(s_b, 16)
            sp.dma_start(wr, io["w_router"].rearrange("a (p k) n -> (a p) k n", k=KT)).then_inc(s_rt, 16)
            sp.dma_start(br, io["b_router"].to_broadcast([P, NE])).then_inc(s_rt, 16)
            for t, (t0, n) in enumerate(TILES):
                sp.wait_ge(s_h, t + 1)
                sp.dma_start(core.h2_d[t0:t0 + n, :], h2[0:n, t % 2, :]).then_inc(s_h2o[t % 2], 16)
            for u in range(2):
                sp.wait_ge(s_h2o[u], 16 * ((NT + 1 - u) // 2))
            sp.wait_ge(s_zo, 16 * zeroed)

        @block.gpsimd
        def _(pool):
            link = linker(pool, s_pool)
            pool.memset(zero, 0.0).then_inc(s_zero, 1)
            link(pool.memset(filler[0:NSLOT], 0))
            pool.iota(filler[0:NSLOT, :, 0], [[1, BLK]], base=NTOK, channel_multiplier=0).then_inc(s_fill, 1)
            pool.wait_ge(s_fill, 1)
            pool.dma_start(core.slot_d.rearrange("(k c) w -> k c w", c=BLK), filler[0:NSLOT]).then_inc(s_tok, 16)
            pool.wait_ge(s_b, 48)
            b = b32[0:NE, :]
            for a in range(3):
                if a < 2:
                    link(pool.tensor_copy(bparts[0:NE, a, :], b))
                    link(pool.tensor_tensor(b, b, bparts[0:NE, a, :], ALU.subtract))
                else:
                    pool.tensor_copy(bparts[0:NE, a, :], b).then_inc(s_bp, 1)
            pool.wait_ge(s_bp, 1)
            pool.dma_start(core.bias_d, bparts[0:NE, :, :]).then_inc(s_bo, 16)
            pool.wait_ge(s_tok, 16)
            pool.wait_ge(s_slot, 1)
            for t, (t0, n) in enumerate(TILES):
                for j in range(TOPK):
                    pool.indirect_dma_start(core.slot_d, bass.IndirectOffsetOnAxis(ap=slot[0:n, t, j:j + 1].bitcast(U32), axis=0),
                                            pair[0:n, t, j, :].bitcast(I32), None).then_inc(s_scat, 16)
            pool.wait_ge(s_scat, 16 * NT * TOPK)
            pool.wait_ge(s_bo, 16)

        @block.tensor
        def _(pe):
            for who, (name, rows) in enumerate((("exp_p", P), ("exp_s", 64))):
                if who:
                    pe.wait_ge(s_exa, 1)
                    pe.wait_ge(s_exd, 1)
                for n in range(4, 12):
                    b, j = divmod(n, 4)
                    last = pe.matmul(ps[0:rows, n - 4, :], core.const(name)[32 * j:32 * j + 9, 0:rows],
                                     mod[32 * j:32 * j + 9, b, :], start=True, stop=True)
                last.then_inc(s_exp, 1)
            pe.wait_ge(s_exa, 2)
            pe.wait_ge(s_exd, 2)

            def to_feature_major(src, n, bank):
                v = src.rearrange("s (p k) -> s k p", k=KT)
                for kt in range(KT):
                    last = pe.transpose(ps[:, bank + kt // 4, (kt % 4) * n:(kt % 4) * n + n], v[:, kt, :], ident[0:n, 0:n])
                return last

            for t, (t0, n) in enumerate(TILES):
                if t >= 2:
                    pe.wait_ge(s_mta, t - 1)
                    pe.wait_ge(s_mtd, t - 1)
                to_feature_major(mix[0:n, t, :], n, 2 * (t % 2)).then_inc(s_mt, 1)
            pe.wait_ge(s_mta, NT)
            pe.wait_ge(s_mtd, NT)
            pe.wait_ge(s_wo, 16)
            pe.wait_ge(s_rt, 32)

            def project_out(t):
                t0, n = TILES[t]
                if t >= 2:
                    pe.wait_ge(s_res, t - 1)
                for kt in range(KT):
                    for c in range(2):
                        last = pe.matmul(ps[0:n, 4 + 2 * (t % 2) + c, :], mixT[:, kt, t0:t0 + n],
                                         wout[:, kt, c * 512:(c + 1) * 512], start=(kt == 0), stop=(kt == KT - 1))
                last.then_inc(s_yp, 1)

            def route(t):
                t0, n = TILES[t]
                pe.wait_ge(s_h, t + 1)
                to_feature_major(h2[0:n, t % 2, :], n, 0).then_inc(s_htp, 1)
                pe.wait_ge(s_ht, t + 1)
                if t >= 2:
                    pe.wait_ge(s_lg, t - 1)
                for kt in range(KT):
                    last = pe.matmul(ps[0:n, 2 + t % 2, 0:NE], h2T[:, kt, 0:n], wr[:, kt, :],
                                     start=(kt == 0), stop=(kt == KT - 1))
                last.then_inc(s_lp, 1)

            for t in range(NT):
                project_out(t)
                if t >= 1:
                    route(t - 1)
            route(NT - 1)
            pe.wait_ge(s_ohr, NT)
            pe.wait_ge(s_wb, 1)
            pe.wait_ge(s_res, NT)
            for t in range(NT + 1):
                m = TILES[t][1] if t < NT else P
                terms = [(onesb[0:TILES[q][1], 0:m], q) for q in range(min(t, NT))]
                if t < NT:
                    terms.append((beforeb[0:m, 0:m], t))
                for i, (w, q) in enumerate(terms):
                    last = pe.matmul(ps[0:m, 4, t * NE:(t + 1) * NE], w, selb[0:TILES[q][1], q, :],
                                     start=(i == 0), stop=(i == len(terms) - 1))
            last.then_inc(s_rk, 1)

        @block.scalar
        def _(act):
            link = linker(act, s_act)
            for who, rows in enumerate((P, 64)):
                act.wait_ge(s_exp, who + 1)
                act.activation(ex[0:rows, who, 0:2, :].rearrange("p v n -> p (v n)"),
                               ps[0:rows, 0:4, :].rearrange("p b n -> p (b n)"), ACT.Copy)
                act.activation(gate2[0:rows, who, :], ps[0:rows, 6:8, :].rearrange("p b n -> p (b n)"),
                               ACT.Copy).then_inc(s_exa, 1)
            for t, (t0, n) in enumerate(TILES):
                act.wait_ge(s_mt, t + 1)
                act.activation(mixT[:, 0:4, t0:t0 + n], ps[:, 2 * (t % 2), 0:4 * n].rearrange("p (k n) -> p k n", k=4),
                               ACT.Copy).then_inc(s_mta, 1)
            for t, (t0, n) in enumerate(TILES):
                act.wait_ge(s_res, t + 1)
                link(act.activation(junk[0:n, :], x[0:n, t, :], ACT.Square, accum_out=stat[0:n, t:t + 1]))
                link(act.activation(stat[0:n, NT + t:NT + t + 1], stat[0:n, t:t + 1], ACT.Ln,
                                    scale=1.0 / D, bias=core.const("eps")[0:n, :]))
                act.activation(stat[0:n, NT + t:NT + t + 1], stat[0:n, NT + t:NT + t + 1], ACT.Exp,
                               scale=-0.5).then_inc(s_rs, 1)
                act.wait_ge(s_htp, t + 1)
                act.activation(h2T[:, :, 0:n].rearrange("p (a k) n -> p a k n", a=2),
                               ps[:, 0:2, 0:4 * n].rearrange("p a (k n) -> p a k n", k=4), ACT.Copy).then_inc(s_ht, 1)
                act.wait_ge(s_nv, t + 1)
                act.activation(wt[0:n, t, :], v8[0:n, t, 0:TOPK], ACT.Exp, bias=nv0[0:n, t:t + 1],
                               accum_out=wsum[0:n, t:t + 1]).then_inc(s_ew, 1)

        @block.vector
        def _(dve):
            link = linker(dve, s_dve)
            link(dve.memset(ones, 1.0))
            dve.tensor_copy(beforeb, core.const("before"))
            dve.tensor_copy(onesb, bcast(core.const("one")[:, 0], 1, P))
            dve.tensor_copy(pair.bitcast(I32)[:, :, :, 0], bcast(core.const("token"), 2, TOPK)).then_inc(s_wb, 1)
            dve.wait_ge(s_w, 16)
            for who, rows in enumerate((P, 64)):
                dve.wait_ge(s_exp, who + 1)
                dve.scalar_tensor_tensor(ex[0:rows, who, 2, :], ps[0:rows, 4:6, :].rearrange("p b n -> p (b n)"), 1.0,
                                         gffn[0:rows, :], ALU.add, ALU.mult).then_inc(s_exd, 1)
            for t, (t0, n) in enumerate(TILES):
                dve.wait_ge(s_mt, t + 1)
                dve.tensor_copy(mixT[:, 4:8, t0:t0 + n],
                                ps[:, 2 * (t % 2) + 1, 0:4 * n].rearrange("p (k n) -> p k n", k=4)).then_inc(s_mtd, 1)
            dve.wait_ge(s_exd, 2)
            dve.wait_ge(s_exa, 2)

            def choose(t):
                n = TILES[t][1]
                dve.wait_ge(s_lp, t + 1)
                dve.tensor_tensor(lg[0:n, t, :], ps[0:n, 2 + t % 2, 0:NE], br[0:n, :], ALU.add).then_inc(s_lg, 1)
                dve.wait_ge(s_lg, t + 1)
                link(dve.max(v8[0:n, t, :], lg[0:n, t, :]))
                dve.tensor_scalar(nv0[0:n, t:t + 1], v8[0:n, t, 0:1], -1.0, None, ALU.mult).then_inc(s_nv, 1)
                link(dve.max_index(i8[0:n, t, :], v8[0:n, t, :], lg[0:n, t, :]))
                link(dve.tensor_copy(i8f[0:n, t, :], i8[0:n, t, 0:TOPK]))
                for j in range(TOPK):
                    last = dve.tensor_scalar(oh[0:n, t, j, :], core.const("iota_e")[0:n, :], i8f[0:n, t, j:j + 1], None,
                                             ALU.is_equal)
                link(last)
                with nc.allow_low_precision(reason="sums of 0 and 1 that are 0 or 1"):
                    dve.tensor_reduce(selb[0:n, t, :], oh[0:n, t, :, :].rearrange("p j e -> p e j"), AX.X, ALU.add
                                      ).then_inc(s_ohr, 1)
                dve.wait_ge(s_ew, t + 1)
                link(dve.reciprocal(wsum[0:n, t:t + 1], wsum[0:n, t:t + 1]))
                dve.tensor_scalar(pair[0:n, t, :, 1], wt[0:n, t, :], wsum[0:n, t:t + 1], None, ALU.mult)

            for t, (t0, n) in enumerate(TILES):
                who = int(t == ST)
                hh = h2[0:n, t % 2, :]
                dve.wait_ge(s_yp, t + 1)
                if t >= 2:
                    dve.wait_ge(s_h2o[t % 2], 16 * (t // 2))
                    dve.wait_ge(s_htp, t - 1)
                link(dve.tensor_tensor(hh, ps[0:n, 4 + 2 * (t % 2):6 + 2 * (t % 2), :].rearrange("p b n -> p (b n)"),
                                       ex[0:n, who, 0, :], ALU.mult))
                dve.tensor_tensor(x[0:n, t, :], x[0:n, t, :], hh, ALU.add).then_inc(s_res, 1)
                if t >= 1:
                    choose(t - 1)
                dve.wait_ge(s_rs, t + 1)
                link(dve.scalar_tensor_tensor(hh, x[0:n, t, :], stat[0:n, NT + t:NT + t + 1], ex[0:n, who, 2, :],
                                              ALU.mult, ALU.mult))
                dve.tensor_tensor(hh, hh, ex[0:n, who, 1, :], ALU.add).then_inc(s_h, 1)
            choose(NT - 1)
            dve.wait_ge(s_rk, 1)
            link(dve.tensor_copy(cnt, ps[:, 4, NT * NE:(NT + 1) * NE]))
            link(dve.tensor_scalar(nblk, cnt, 0.0, None, ALU.is_gt))
            for b in range(1, -(-NTOK // BLK)):
                link(dve.scalar_tensor_tensor(nblk, cnt, float(b * BLK), nblk, ALU.is_gt, ALU.add))
            link(dve.tensor_tensor_scan(bend, ones, nblk, 0.0, ALU.mult, ALU.add))
            link(dve.tensor_tensor(base, bend, nblk, ALU.subtract))
            link(dve.tensor_scalar(base, base, float(BLK), None, ALU.mult))
            one = slice(0, 1)
            link(dve.tensor_tensor(cmpk[one], bcast(bend[one, :], 1, NSLOT + 1), bcast(core.const("iota_k")[one, :], 2, NE),
                                   ALU.is_le))
            link(dve.tensor_reduce(ek[one, 0:NSLOT + 1], cmpk[one], AX.X, ALU.add))
            link(dve.tensor_scalar(ek[one, 0:NSLOT], ek[one, 0:NSLOT], float(NE - 1), None, ALU.min))
            for i in range(3):
                link(dve.tensor_scalar(ek[one, NSLOT + i:NSLOT + i + 1], bend[one, NE - 1:NE], float(-i), None, ALU.add))
            dve.tensor_copy(core.blocks[one, :], ek[one, :]).then_inc(s_blk, 1)
            for t, (t0, n) in enumerate(TILES):
                link(dve.tensor_tensor(rk[0:n, :], ps[0:n, 4, t * NE:(t + 1) * NE], base[0:n, :], ALU.add))
                link(dve.tensor_tensor(pick[0:n], oh[0:n, t], bcast(rk[0:n, :], 1, TOPK), ALU.mult))
                link(dve.tensor_reduce(slotf[0:n, t, :], pick[0:n], AX.X, ALU.add))
                last = dve.tensor_copy(slot[0:n, t, :], slotf[0:n, t, :])
            last.then_inc(s_slot, 1)


LIMIT, ALPHA = 7.0, 1.702


def is_zero(n):
    return isinstance(n, int) and n == 0


def experts(core):
    nc, io, ps = core.nc, core.io, core.psum
    ident, blocks = core.const("ident"), core.blocks
    own = Stack(core, core.z_moe, ARENA)
    HK = KT // 2
    w = own.take(6 * HK * D).rearrange("p (s k n) -> p s k n", s=6, k=HK)
    bias = own.take(3 * D // 2).bitcast(BF16).rearrange("p (m n) -> p m n", m=3)
    ones = own.take(P // 2).bitcast(BF16)
    xg, g, u, s, a, y = (own.take(D) for _ in range(6))
    xT = own.take(KT * P).rearrange("p (k n) -> p k n", k=KT)
    aT = own.take(KT * P).rearrange("p (k n) -> p k n", k=KT)
    sums = [own.take(1), own.take(1)]
    row_in, row_out = own.take(2), own.take(2)
    slot_blk = core.slot_d.rearrange("(k p) w -> k p w", p=BLK)
    mats = [io[n].rearrange("a e (p k) n -> (a e) p k n", k=KT) for n in ("w_gate", "w_up", "w_down")]
    GB, UB, DB, TB = 0, 2, 4, 6

    s_w = [core.sem(f"w_in{i}") for i in range(6)]
    s_bias = [core.sem(f"bias_in{i}") for i in range(3)]
    s_half = [core.sem(f"half_used{i}") for i in range(3)]
    s_done = [core.sem(f"product{i}") for i in range(3)]
    s_ones, s_row, s_rowo, s_xg, s_xtp, s_xt = (core.sem(n) for n in ("ones_ready", "tokens_in", "weights_in", "rows_gathered", "xT_ps", "xT_ready"))
    s_g, s_u, s_sig, s_a, s_atp, s_at = (core.sem(n) for n in ("gate_read", "up_read", "sigmoid", "act_ready", "aT_ps", "aT_ready"))
    s_y, s_yo, s_t = core.sem("down_read"), core.sem("rows_added"), core.sem("swiglu_part")

    s_sum = [core.sem("gather_allowed"), core.sem("add_allowed")]

    def used_blocks(eng):
        return [eng.value_load(blocks[0:1, NSLOT + i:NSLOT + i + 1], min_val=NTOK * TOPK // BLK - i, max_val=NSLOT - i)
                for i in range(3)]

    with nc.Block() as block:
        @block.sync
        def _(sp):
            _, nb1, _ = used_blocks(sp)

            def load(m, k):
                e = sp.value_load(blocks[0:1, bass.ds(k, 1)], min_val=0, max_val=NE - 1)
                for half in range(2):
                    if not is_zero(k):
                        sp.wait_ge(s_half[m] if half == 0 else s_done[m], k)
                    sp.dma_start(w[:, 2 * m + half, :, :],
                                 mats[m][bass.ds(e, 1), :, half * HK:(half + 1) * HK, :].rearrange("e p k n -> (e p) k n")
                                 ).then_inc(s_w[2 * m + half], 16)
                sp.dma_start(bias[0:3, m, :], core.bias_d[bass.ds(e, 1), :, m * D:(m + 1) * D]
                             .rearrange("e a n -> (e a) n")).then_inc(s_bias[m], 16)

            for m in range(3):
                load(m, 0)
            load(0, 1)
            load(1, 1)
            with sp.Fori(1, nb1) as k:
                load(0, k + 1)
                load(1, k + 1)
                load(2, k)
            load(2, nb1)

        @block.gpsimd
        def _(pool):
            nb, nb1, nb2 = used_blocks(pool)

            def take_waits(sem, n):
                if not is_zero(n):
                    pool.wait_ge(sem, n)
                pool.tensor_tensor(sums[s_sum.index(sem)], core.const("one"), core.const("one"), ALU.add).then_inc(sem, 1)

            def read_slots(dst, k, sem, n):
                pool.dma_start(dst.bitcast(I32), slot_blk[bass.ds(k, 1), :, :].rearrange("k p w -> (k p) w")).then_inc(sem, 16)
                pool.wait_ge(sem, 16 * n)

            def gather(k):
                read_slots(row_in, k, s_row, k + 1)
                if not is_zero(k):
                    pool.wait_ge(s_xtp, k)
                take_waits(s_sum[0], k)
                pool.indirect_dma_start(xg, None, core.h2_d, bass.IndirectOffsetOnAxis(ap=row_in[:, 0:1].bitcast(U32), axis=0)
                                        ).then_inc(s_xg, 16)
                pool.wait_ge(s_xg, 16 * (k + 1))

            def add_rows(k, n, before):
                read_slots(row_out, k, s_rowo, n)
                pool.wait_ge(s_y, n)
                take_waits(s_sum[1], before)
                pool.indirect_dma_start(core.ffn_d, bass.IndirectOffsetOnAxis(ap=row_out[:, 0:1].bitcast(U32), axis=0), y, None,
                                        compute_op=ALU.add).then_inc(s_yo, 16)
                pool.wait_ge(s_yo, 16 * n)

            gather(0)
            gather(1)
            gather(2)
            add_rows(0, 1, 0)
            with pool.Fori(3, nb) as k:
                gather(k)
                add_rows(k - 2, k - 1, k - 2)
            add_rows(nb2, nb1, nb2)
            add_rows(nb1, nb, nb1)

        @block.tensor
        def _(pe):
            nb, nb1, nb2 = used_blocks(pe)

            def product(m, n, xs, bank):
                pe.wait_ge(s_bias[m], 16 * n)
                for c in range(2):
                    pe.matmul(ps[:, bank + c, :], ones[0:3, :], bias[0:3, m, c * 512:(c + 1) * 512], start=True, stop=False)
                for kt in range(KT):
                    if kt % HK == 0:
                        pe.wait_ge(s_w[2 * m + kt // HK], 16 * n)
                    for c in range(2):
                        last = pe.matmul(ps[:, bank + c, :], xs[:, kt, :], w[:, 2 * m + kt // HK, kt % HK, c * 512:(c + 1) * 512],
                                         start=False, stop=(kt == KT - 1))
                    if kt == HK - 1:
                        last.then_inc(s_half[m], 1)
                last.then_inc(s_done[m], 1)

            def turn(src, sem):
                v = src.rearrange("s (p k) -> s k p", k=KT)
                for kt in range(KT):
                    last = pe.transpose(ps[:, TB + kt // 4, (kt % 4) * P:(kt % 4 + 1) * P], v[:, kt, :], ident)
                last.then_inc(sem, 1)

            def gate(k):
                pe.wait_ge(s_xt, k + 1)
                if not is_zero(k):
                    pe.wait_ge(s_g, k)
                product(0, k + 1, xT, GB)

            def up(k):
                if not is_zero(k):
                    pe.wait_ge(s_u, k)
                product(1, k + 1, xT, UB)

            def turn_rows(k, first=False):
                pe.wait_ge(s_xg, 16 * (k + 1))
                if not first:
                    pe.wait_ge(s_at, k - 1)
                turn(xg, s_xtp)

            def turn_act(k):
                pe.wait_ge(s_a, k)
                pe.wait_ge(s_xt, k + 1)
                turn(a, s_atp)

            def down(n, before):
                pe.wait_ge(s_at, n)
                if not is_zero(before):
                    pe.wait_ge(s_y, before)
                product(2, n, aT, DB)

            pe.wait_ge(s_ones, 1)
            turn_rows(0, first=True)
            gate(0)
            up(0)
            turn_rows(1, first=True)

            def step(k):
                gate(k)
                turn_act(k)
                up(k)
                turn_rows(k + 1)
                down(k, k - 1)

            step(1)
            with pe.Fori(2, nb1) as k:
                step(k)
            gate(nb1)
            turn_act(nb1)
            up(nb1)
            down(nb1, nb2)
            pe.wait_ge(s_a, nb)
            turn(a, s_atp)
            down(nb, nb1)

        @block.scalar
        def _(act):
            nb, nb1, nb2 = used_blocks(act)

            def from_banks(dst, bank, sem):
                act.activation(dst, ps[:, bank:bank + 2, :].rearrange("p b n -> p (b n)"), ACT.Copy).then_inc(sem, 1)

            def rows_T(k):
                act.wait_ge(s_xtp, k + 1)
                from_banks(xT.rearrange("p k n -> p (k n)"), TB, s_xt)

            def acts_T(k):
                act.wait_ge(s_atp, k)
                from_banks(aT.rearrange("p k n -> p (k n)"), TB, s_at)

            def sigmoid(k):
                act.wait_ge(s_g, k + 1)
                act.activation(s, g, ACT.Sigmoid, scale=ALPHA).then_inc(s_sig, 1)

            def weigh(n, before):
                act.wait_ge(s_done[2], n)
                act.wait_ge(s_rowo, 16 * n)
                if not is_zero(before):
                    act.wait_ge(s_yo, 16 * before)
                act.activation(y, ps[:, DB:DB + 2, :].rearrange("p b n -> p (b n)"), ACT.Copy, scale=row_out[:, 1:2]
                               ).then_inc(s_y, 1)

            rows_T(0)
            sigmoid(0)
            rows_T(1)

            def step(k):
                acts_T(k)
                sigmoid(k)
                rows_T(k + 1)
                weigh(k, k - 1)

            step(1)
            with act.Fori(2, nb1) as k:
                step(k)
            acts_T(nb1)
            sigmoid(nb1)
            weigh(nb1, nb2)
            acts_T(nb)
            weigh(nb, nb1)

        @block.vector
        def _(dve):
            nb, _, _ = used_blocks(dve)
            dve.memset(ones, 1.0).then_inc(s_ones, 1)

            def swiglu(k):
                dve.wait_ge(s_done[0], k + 1)
                dve.tensor_scalar(g, ps[:, GB:GB + 2, :].rearrange("p b n -> p (b n)"), LIMIT, None, ALU.min).then_inc(s_g, 1)
                dve.wait_ge(s_done[1], k + 1)
                dve.tensor_scalar(u, ps[:, UB:UB + 2, :].rearrange("p b n -> p (b n)"), -LIMIT, LIMIT, ALU.max, ALU.min
                                  ).then_inc(s_u, 1)
                dve.wait_ge(s_u, k + 1)
                dve.scalar_tensor_tensor(u, u, 1.0, g, ALU.add, ALU.mult).then_inc(s_t, 1)
                dve.wait_ge(s_t, k + 1)
                dve.wait_ge(s_sig, k + 1)
                if not is_zero(k):
                    dve.wait_ge(s_atp, k)
                dve.tensor_tensor(a, u, s, ALU.mult).then_inc(s_a, 1)

            swiglu(0)
            with dve.Fori(1, nb) as k:
                swiglu(k)


def combine(core):
    nc, io = core.nc, core.io
    x, gate2 = core.x, core.gate2
    own = Stack(core, core.z_moe, ARENA)
    f = own.take(NT * D).rearrange("p (t d) -> p t d", t=NT)
    junk, gfin = own.take(D), own.take(D)
    out = own.take(NT * D).rearrange("p (t d) -> p t d", t=NT)
    stat = own.take(2 * NT)
    s_gf, s_x, s_rs, s_o, s_out, s_act, s_dve = (core.sem(n) for n in (
        "g_final_in", "x_final", "rstd3_ready", "out_ready", "out_stored", "act_p8", "dve_p8"))
    s_f = [core.sem(f"sums_in{t}") for t in range(NT)]

    with nc.Block() as block:
        @block.sync
        def _(sp):
            for t, (t0, n) in enumerate(TILES):
                sp.dma_start(f[0:n, t, :], core.ffn_d[t0:t0 + n, :]).then_inc(s_f[t], 16)
                if t == 0:
                    sp.dma_start(gfin, io["g_final"].unsqueeze(0).to_broadcast([P, D])).then_inc(s_gf, 16)
            for t, (t0, n) in enumerate(TILES):
                sp.wait_ge(s_o, t + 1)
                dst = io["out_0"][0, t0:t0 + n, :] if t < ST else io["out_1"].rearrange("b t d -> (b t) d")
                sp.dma_start(dst, out[0:n, t, :]).then_inc(s_out, 16)
            sp.wait_ge(s_out, 16 * NT)

        @block.scalar
        def _(act):
            link = linker(act, s_act)
            for t, (t0, n) in enumerate(TILES):
                act.wait_ge(s_x, t + 1)
                link(act.activation(junk[0:n, :], x[0:n, t, :], ACT.Square, accum_out=stat[0:n, t:t + 1]))
                link(act.activation(stat[0:n, NT + t:NT + t + 1], stat[0:n, t:t + 1], ACT.Ln,
                                    scale=1.0 / D, bias=core.const("eps")[0:n, :]))
                act.activation(stat[0:n, NT + t:NT + t + 1], stat[0:n, NT + t:NT + t + 1], ACT.Exp,
                               scale=-0.5).then_inc(s_rs, 1)

        @block.vector
        def _(dve):
            link = linker(dve, s_dve)

            def finish(t):
                n = TILES[t][1]
                dve.wait_ge(s_rs, t + 1)
                dve.scalar_tensor_tensor(out[0:n, t, :], x[0:n, t, :], stat[0:n, NT + t:NT + t + 1], gfin[0:n, :],
                                         ALU.mult, ALU.mult).then_inc(s_o, 1)

            for t, (t0, n) in enumerate(TILES):
                dve.wait_ge(s_f[t], 16)
                link(dve.tensor_tensor(f[0:n, t, :], f[0:n, t, :], gate2[0:n, int(t == ST), :], ALU.mult))
                dve.tensor_tensor(x[0:n, t, :], x[0:n, t, :], f[0:n, t, :], ALU.add).then_inc(s_x, 1)
                if t == 0:
                    dve.wait_ge(s_gf, 16)
                if t >= 1:
                    finish(t - 1)
            finish(NT - 1)


STAGES = [project, gla, compress, prompt_attention, sample_attention, output_and_router, experts, combine]


INPUTS = ["x_prompt", "x_sample", "c_prompt", "c_sample", "cache_cmp", "cache_sel", "state_win", "state_gla",
          "page_table", "w_ada", "b_ada", "g_mix", "g_ffn", "w_in", "w_a2", "b_a", "g_gla", "phi_pe", "phi_w", "w_out",
          "w_router", "b_router", "w_gate", "b_gate", "w_up", "b_up", "w_down", "b_down", "g_final"]
KV = (2, KVH, HD)
OUTPUTS = [(1, SEQ, D), (NSEQ, TS, D), (1, 1, SEQ) + KV, (1, 1, SEQ) + KV, (1, 1, SEQ) + KV, (1, 1, GH, DK, DV),
           (1, NSEQ, TS) + KV, (1, NSEQ, TS) + KV, (1, NSEQ, SEQ) + KV, (1, NSEQ, GH, DK, DV)]

ZONE = ARENA - 22464 - NT * D - NF * NTOK


def build(nc, io, stages=None):
    with ExitStack() as ctx:
        core = Core(nc, ctx, io)
        core.x = core.take(NT * D).rearrange("p (t d) -> p t d", t=NT)
        core.mod = core.take(3 * 512).rearrange("p (b n) -> p b n", b=3)
        core.consts = core.take(N_CONST_A + N_CONST_B)
        core.pf = core.top
        core.proj_flat = core.take(NT * DIN)
        core.proj = core.proj_flat.rearrange("p (t n) -> p t n", t=NT)
        core.z0, core.z1 = core.top, core.top + ZONE
        mixed = Stack(core, core.z1, ARENA)
        core.mix = mixed.take(NT * D).rearrange("p (t d) -> p t d", t=NT)
        core.feat = mixed.take(NF * NTOK).rearrange("p (i n) -> p i n", i=NF)
        for stage in stages or STAGES:
            stage(core)
            core.stage_done()


def kernel(**inputs):
    import concourse.bacc as bacc
    from concourse.bass_utils import run_bass_kernel_spmd

    nc = bacc.Bacc("TRN2", target_bir_lowering=False, num_devices=1)
    arrays, io = {}, {}
    for name in INPUTS:
        a = np.ascontiguousarray(inputs[name])
        arrays["in_" + name] = a
        io[name] = nc.dram_tensor("in_" + name, a.shape, mybir.dt.from_np(a.dtype), kind="ExternalInput").ap()
    arrays["consts"] = CONST_ARRAY
    io["consts"] = nc.dram_tensor("consts", CONST_ARRAY.shape, F32, kind="ExternalInput").ap()
    for i, shape in enumerate(OUTPUTS):
        io[f"out_{i}"] = nc.dram_tensor(f"out_{i}", shape, F32, kind="ExternalOutput").ap()
    build(nc, io)
    r = run_bass_kernel_spmd(nc, [arrays], core_ids=[0])
    return tuple(np.asarray(r.results[0][f"out_{i}"]) for i in range(len(OUTPUTS)))
```

```python
from contextlib import ExitStack

import numpy as np

import concourse.bass as bass
from concourse import mybir

F32 = mybir.dt.float32
F32R = mybir.dt.float32r
BF16 = mybir.dt.bfloat16
I32 = mybir.dt.int32
U32 = mybir.dt.uint32
ALU = mybir.AluOpType
ACT = mybir.ActivationFunctionType
AX = mybir.AxisListType

P = 128
D = 1024
KT = D // P
SEQ = 512
NSEQ, TS = 8, 8
NTOK = SEQ + NSEQ * TS
TILES = [(t * P, P) for t in range(SEQ // P)] + [(SEQ, NSEQ * TS)]
NT = len(TILES)
ST = NT - 1
PAST, PAGE = 1024, 128
GH, DK, DV, GRANK, CHUNK = 4, 64, 128, 16, 64
KVH, GRP, HD = 2, 4, 64
NE, TOPK, DE = 32, 4, 1024
BLK = 128
NSLOT = (NTOK * TOPK + NE * (BLK - 1)) // BLK
EPS = 1e-6
ARENA = 53200
NEG = -1e30
C_GQ, C_GK, C_GV, C_GR = 0, 256, 512, 1024
C_GA = 1536
C_NQ = C_GA + GRANK
C_KC, C_KS, C_KW = C_NQ + 512, C_NQ + 768, C_NQ + 1024
C_NG = C_NQ + 1280
DIN = C_NG + 3 * KVH * GRP
NCH = 6
CW = DIN // NCH
GAPS = 16
NCMP_P = SEQ // GAPS - 1
NCMP_S = PAST // GAPS - 1
NBLK_S = PAST // 64



def constants():
    p = np.arange(P)[:, None]
    cols, parts, at = {}, [], 0

    def put(name, a):
        nonlocal at
        full = np.zeros((P, a.shape[1]), np.float32)
        full[:a.shape[0]] = a
        cols[name] = (at, a.shape[1])
        parts.append(full)
        at += a.shape[1]

    c = np.arange(P)[None, :]
    put("ident", (p == c).astype(np.float32))
    s = p % 32
    put("exp_p", np.broadcast_to(s == 0, (P, P)).astype(np.float32))
    tok = np.arange(NSEQ * TS)[None, :]
    put("exp_s", (s - 1 == tok // TS).astype(np.float32))
    put("before", (p < c).astype(np.float32))
    put("iota_e", np.broadcast_to(np.arange(NE, dtype=np.float32), (P, NE)))
    put("iota_k", np.broadcast_to(np.arange(NSLOT + 1, dtype=np.float32), (P, NSLOT + 1)))
    put("token", (np.arange(NT) * P + p).astype(np.float32))
    put("eps", np.full((P, 1), EPS, np.float32))
    put("one", np.ones((P, 1), np.float32))
    n_a = at
    put("causal", np.where(c <= p, 0, NEG))
    put("gla_p", ((p // CHUNK == c // CHUNK) & (p <= c)).astype(np.float32))
    put("gla_s", ((p // TS == tok // TS) & (p <= tok)).astype(np.float32))
    b2, t8 = p // 64, p % TS
    put("same_q", ((p // 32 == c // 32) & (p % TS == c % TS)).astype(np.float32))
    put("new_keys", np.concatenate([np.where((tok // TS == 2 * i + b2) & (tok % TS <= t8), 0, NEG)
                                    for i in range(NSEQ // 2)], 1))
    put("win_old", np.where(np.arange(TS)[None, :] > t8, 0, NEG))
    blk = np.arange(NCMP_P)[None, :]
    put("cmp_p", np.concatenate([np.where(blk * GAPS + 2 * GAPS - 1 <= t * P + p, 0, NEG)
                                 for t in range(SEQ // P) for _ in range(KVH)], 1))
    put("seq_of", (p // TS == np.arange(NSEQ)[None, :]).astype(np.float32))
    n_b = at - n_a
    pos = np.arange(NTOK)[None, :]
    put("scan", np.broadcast_to(np.where(pos < SEQ, pos % CHUNK != 0, pos % TS != 0), (P, NTOK)).astype(np.float32))
    return cols, np.ascontiguousarray(np.concatenate(parts, 1), np.float32), n_a, n_b


CONST_COLS, CONST_ARRAY, N_CONST_A, N_CONST_B = constants()


class Core:

    def __init__(self, nc, ctx, io):
        self.nc, self.ctx, self.io = nc, ctx, io
        self.arena_at = (nc.sbuf_base + 31) // 32 * 32
        self.arena = ctx.enter_context(nc.sbuf_tensor("arena", [P, ARENA], F32))
        self.psum = ctx.enter_context(nc.psum_tensor("banks", [P, 8, 512], F32))
        self.top = 0
        self.sems, self.carried = [], []

    def sem(self, name, carry=False):
        s = self.nc.alloc_semaphore(name=name)
        (self.carried if carry else self.sems).append(s)
        return s

    def stage_done(self):
        self.nc.clear_and_free_semaphores(self.sems)
        self.sems, self.carried = self.carried, []
        self.nc.all_engine_barrier()

    def named(self, name, at, words):
        return self.nc.alloc_sbuf_tensor_at(name, [P, words], F32, offset=self.arena_at + 4 * at)

    def take(self, words):
        at = self.top
        self.top += (words + 7) // 8 * 8
        return self.arena[:, at:at + words]

    def const(self, name):
        at, n = CONST_COLS[name]
        return self.consts[:, at:at + n]


class Stack:

    def __init__(self, core, at, end, tensor=None):
        self.tensor, self.at, self.end = core.arena if tensor is None else tensor, at, end

    def take(self, words):
        at = self.at
        self.at += (words + 7) // 8 * 8
        assert self.at <= self.end, (self.at, self.end)
        return self.tensor[:, at:at + words]


def linker(engine, sem):
    count = [0]

    def link(ins):
        count[0] += 1
        ins.then_inc(sem, 1)
        engine.wait_ge(sem, count[0])
    return link


def bcast(ap, dim, n):
    shape = list(ap.shape)
    return ap.unsqueeze(dim).to_broadcast(shape[:dim] + [n] + shape[dim:])


def project(core):
    nc, io, ps = core.nc, core.io, core.psum
    mod, proj, x, consts = core.mod, core.proj, core.x, core.consts
    ident = core.const("ident")
    own = Stack(core, core.z0, ARENA)
    ring = own.take(3 * 4096)
    hT = own.take(KT * NTOK).rearrange("p (k n) -> p k n", k=KT)
    ada = own.take(4 * D).rearrange("p (a n) -> p a n", a=4)
    tmp = own.take(2 * D).rearrange("p (a n) -> p a n", a=2)
    scT = own.take(KT * 9).rearrange("p (k n) -> p k n", k=KT)
    stat = own.take(2 * NT)
    junk = own.take(D)
    pr = core.proj_flat
    c9, cexp, brow = pr[0:9, 0:D], pr[0:9, D:2 * D], pr[0:1, 2 * D:2 * D + 6 * D]
    gmix = pr[:, 8 * D:9 * D]
    piece = [ring[:, i * 6 * D:(i + 1) * 6 * D] for i in range(2)]
    wchunk = [ring[:, i * 4096:i * 4096 + KT * CW].rearrange("p (k n) -> p k n", k=KT) for i in range(3)]
    w_ada = io["w_ada"].rearrange("a (p k) n -> (a p) k n", k=KT)
    w_in = io["w_in"].rearrange("a (p k) n -> (a p) k n", k=KT)

    s_const, s_c, s_x, s_b, s_g = (core.sem(n) for n in ("const_in", "c_in", "x_in", "b_ada_in", "g_mix_in"))
    s_ada = [core.sem(f"ada_in{i}") for i in range(2)]
    s_win = [core.sem(f"win_in{i}") for i in range(3)]
    s_adaused = core.sem("ada_used")
    s_cexp, s_silu, s_cT, s_scT = (core.sem(n) for n in ("c_exp", "c_silu", "cT_ps", "scT_ready"))
    s_mod, s_modcp, s_exps, s_expd = (core.sem(n) for n in ("mod_ps", "mod_ready", "expand_ps", "expand_read"))
    s_rstd, s_h, s_hps, s_hT, s_hT2 = (core.sem(n) for n in ("rstd_ready", "h_ready", "hT_ps", "hT_by_act", "hT_by_dve"))
    s_pj, s_pja, s_pjd = (core.sem(n) for n in ("proj_ps", "proj_by_act", "proj_by_dve"))
    s_dve, s_act = core.sem("dve_p1"), core.sem("act_p1")
    core.s_const = s_const
    core.mod_d = nc.dram_tensor("modulation", [9, 6 * D], F32).ap()
    s_modout = core.sem("mod_out")

    with nc.Block() as block:
        @block.sync
        def _(sp):
            sp.dma_start(core.consts, io["consts"][:, 0:N_CONST_A + N_CONST_B]).then_inc(s_const, 16)
            sp.dma_start(c9[0:1, :], io["c_prompt"]).then_inc(s_c, 16)
            sp.dma_start(c9[1:9, :], io["c_sample"]).then_inc(s_c, 16)
            for kt in range(KT):
                if kt >= 2:
                    sp.wait_ge(s_adaused, kt - 1)
                sp.dma_start(piece[kt % 2], w_ada[:, kt, :]).then_inc(s_ada[kt % 2], 16)
                if kt == 0:
                    sp.dma_start(brow, io["b_ada"]).then_inc(s_b, 16)
                    sp.dma_start(gmix, io["g_mix"].to_broadcast([P, D])).then_inc(s_g, 16)
                if kt == 1:
                    for t, (t0, n) in enumerate(TILES):
                        src = io["x_prompt"][0, t0:t0 + n, :] if t < ST else io["x_sample"].rearrange("b t d -> (b t) d")
                        sp.dma_start(x[0:n, t, :], src).then_inc(s_x, 16)
            for c in range(NCH):
                if c == 0:
                    sp.wait_ge(s_adaused, KT - 1)
                elif c == 1:
                    sp.wait_ge(s_mod, 1)
                elif c >= 3:
                    sp.wait_ge(s_pj, NT * (c - 2))
                sp.dma_start(wchunk[c % 3], w_in[:, :, c * CW:(c + 1) * CW]).then_inc(s_win[c % 3], 16)
            sp.wait_ge(s_modcp, 4)
            for j in range(4):
                sp.dma_start(core.mod_d.rearrange("s (b j n) -> s b j n", b=3, j=4)[:, :, j, :],
                             mod[32 * j:32 * j + 9, :, :]).then_inc(s_modout, 16)
            sp.wait_ge(s_modout, 64)

        @block.scalar
        def _(act):
            link = linker(act, s_act)
            act.wait_ge(s_c, 32)
            act.activation(cexp, c9, ACT.Exp, scale=-1.0).then_inc(s_cexp, 1)
            act.wait_ge(s_x, 16 * NT)
            act.wait_ge(s_const, 16)
            for t, (t0, n) in enumerate(TILES):
                link(act.activation(junk[0:n, :], x[0:n, t, :], ACT.Square, accum_out=stat[0:n, t:t + 1]))
                link(act.activation(stat[0:n, NT + t:NT + t + 1], stat[0:n, t:t + 1], ACT.Ln,
                                    scale=1.0 / D, bias=core.const("eps")[0:n, :]))
                act.activation(stat[0:n, NT + t:NT + t + 1], stat[0:n, NT + t:NT + t + 1], ACT.Exp,
                               scale=-0.5).then_inc(s_rstd, 1)
            for t, (t0, n) in enumerate(TILES):
                act.wait_ge(s_hps, 2 * t + 2)
                act.activation(hT[:, 4:8, t0:t0 + n], ps[:, 2 * (t % 2) + 1, 0:4 * n].rearrange("p (k n) -> p k n", k=4),
                               ACT.Copy).then_inc(s_hT, 1)
            for i in range(NCH * NT):
                if i % 2 == 0:
                    c, t = divmod(i, NT)
                    act.wait_ge(s_pj, i + 1)
                    act.activation(proj[0:TILES[t][1], t, c * CW:(c + 1) * CW], ps[0:TILES[t][1], 4 + i % 4, 0:CW],
                                   ACT.Copy).then_inc(s_pja, 1)

        def hcopy(dve, t):
            t0, n = TILES[t]
            dve.wait_ge(s_hps, 2 * t + 1)
            dve.tensor_copy(hT[:, 0:4, t0:t0 + n],
                            ps[:, 2 * (t % 2), 0:4 * n].rearrange("p (k n) -> p k n", k=4)).then_inc(s_hT2, 1)

        @block.vector
        def _(dve):
            link = linker(dve, s_dve)
            dve.wait_ge(s_cexp, 1)
            link(dve.tensor_scalar(cexp, cexp, 1.0, None, ALU.add))
            link(dve.reciprocal(cexp, cexp))
            dve.tensor_tensor(c9, c9, cexp, ALU.mult).then_inc(s_silu, 1)
            dve.wait_ge(s_cT, 1)
            dve.tensor_copy(scT, ps[:, 0, 0:KT * 9].rearrange("p (k n) -> p k n", k=KT)).then_inc(s_scT, 1)
            dve.wait_ge(s_mod, 1)
            for j in range(4):
                dve.tensor_copy(mod[32 * j:32 * j + 9, :, :], ps[32 * j:32 * j + 9, 1:4, :]).then_inc(s_modcp, 1)
            dve.wait_ge(s_g, 16)
            for who in range(2):
                rows = P if who == 0 else TILES[ST][1]
                bank = 4 if who == 0 else 0
                for n in range(4):
                    dve.wait_ge(s_exps, 4 * who + n + 1)
                    dst = ada[0:rows, 2 * who + n // 2, (n % 2) * 512:(n % 2) * 512 + 512]
                    if n < 2:
                        ins = dve.tensor_copy(dst, ps[0:rows, bank + n, :])
                    else:
                        ins = dve.scalar_tensor_tensor(dst, ps[0:rows, bank + n, :], 1.0,
                                                       gmix[0:rows, (n % 2) * 512:(n % 2) * 512 + 512], ALU.add, ALU.mult)
                    ins.then_inc(s_expd, 1)
            dve.wait_ge(s_expd, 8)
            for t, (t0, n) in enumerate(TILES):
                who = 2 * (t == ST)
                dve.wait_ge(s_rstd, t + 1)
                if t >= 2:
                    dve.wait_ge(s_hps, 2 * (t - 1))
                link(dve.scalar_tensor_tensor(tmp[0:n, t % 2, :], x[0:n, t, :], stat[0:n, NT + t:NT + t + 1],
                                              ada[0:n, who + 1, :], ALU.mult, ALU.mult))
                dve.tensor_tensor(tmp[0:n, t % 2, :], tmp[0:n, t % 2, :], ada[0:n, who, :], ALU.add).then_inc(s_h, 1)
                if t >= 1:
                    hcopy(dve, t - 1)
            hcopy(dve, NT - 1)
            for i in range(NCH * NT):
                if i % 2 == 1:
                    c, t = divmod(i, NT)
                    dve.wait_ge(s_pj, i + 1)
                    dve.tensor_copy(proj[0:TILES[t][1], t, c * CW:(c + 1) * CW],
                                    ps[0:TILES[t][1], 4 + i % 4, 0:CW]).then_inc(s_pjd, 1)

        @block.tensor
        def _(pe):
            pe.wait_ge(s_const, 16)
            pe.wait_ge(s_silu, 1)
            cv = c9.rearrange("s (p k) -> s k p", k=KT)
            for kt in range(KT):
                last = pe.transpose(ps[:, 0, kt * 9:kt * 9 + 9], cv[:, kt, :], ident[0:9, 0:9])
            last.then_inc(s_cT, 1)
            pe.wait_ge(s_scT, 1)
            pe.wait_ge(s_b, 16)
            for kt in range(KT):
                pe.wait_ge(s_ada[kt % 2], 16 * (kt // 2 + 1))
                for n in range(12):
                    b, j = divmod(n, 4)
                    out = ps[32 * j:32 * j + 9, 1 + b, :]
                    if kt == 0:
                        pe.matmul(out, core.const("exp_p")[0:1, 0:9], brow[:, n * 512:(n + 1) * 512], start=True, stop=False)
                    last = pe.matmul(out, scT[:, kt, :], piece[kt % 2][:, n * 512:(n + 1) * 512],
                                     start=False, stop=(kt == KT - 1))
                last.then_inc(s_adaused if kt < KT - 1 else s_mod, 1)
            pe.wait_ge(s_modcp, 4)
            for who, (name, rows, bank) in enumerate((("exp_p", P, 4), ("exp_s", 64, 0))):
                for n in range(4):
                    j = n % 4
                    pe.matmul(ps[0:rows, bank + n, :], core.const(name)[32 * j:32 * j + 9, 0:rows],
                              mod[32 * j:32 * j + 9, 0, :], start=True, stop=True).then_inc(s_exps, 1)
            for t, (t0, n) in enumerate(TILES):
                pe.wait_ge(s_h, t + 1)
                if t >= 2:
                    pe.wait_ge(s_hT, t - 1)
                    pe.wait_ge(s_hT2, t - 1)
                else:
                    pe.wait_ge(s_expd, 8)
                hv = tmp[0:n, t % 2, :].rearrange("s (p k) -> s k p", k=KT)
                for kt in range(KT):
                    last = pe.transpose(ps[:, 2 * (t % 2) + kt // 4, (kt % 4) * n:(kt % 4) * n + n], hv[:, kt, :],
                                        ident[0:n, 0:n])
                    if kt % 4 == 3:
                        last.then_inc(s_hps, 1)
            pe.wait_ge(s_hT, NT)
            pe.wait_ge(s_hT2, NT)
            for i in range(NCH * NT):
                c, t = divmod(i, NT)
                t0, n = TILES[t]
                if t == 0:
                    pe.wait_ge(s_win[c % 3], 16 * (c // 3 + 1))
                if i >= 4:
                    pe.wait_ge(s_pja if i % 2 == 0 else s_pjd, (i - 4) // 2 + 1)
                for kt in range(KT):
                    last = pe.matmul(ps[0:n, 4 + i % 4, 0:CW], hT[:, kt, t0:t0 + n], wchunk[c % 3][:, kt, :],
                                     start=(kt == 0), stop=(kt == KT - 1))
                last.then_inc(s_pj, 1)


QN, KSF, KWF, GQF, GKF, GAF, NF = 0, 4, 5, 6, 8, 10, 11


def gla(core):
    nc, io, ps = core.nc, core.io, core.psum
    proj, feat, mix = core.proj, core.feat, core.mix
    ident = core.const("ident")
    own = Stack(core, core.z0, core.z1)
    scan = own.take(NTOK)
    e1 = own.take(2 * NTOK).rearrange("p (j n) -> p j n", j=2)
    e2 = own.take(2 * NTOK).rearrange("p (j n) -> p j n", j=2)
    cum = own.take(2 * NTOK).rearrange("p (j n) -> p j n", j=2)
    qd = own.take(GH * NTOK).rearrange("p (h n) -> p h n", h=GH)
    kinv = own.take(2 * NTOK).rearrange("p (j n) -> p j n", j=2)
    kend = own.take(2 * NTOK).rearrange("p (j n) -> p j n", j=2)
    kt = own.take(NT * 256).rearrange("p (t n) -> p t n", t=NT)
    att = own.take(NT * GH * P).rearrange("p (t h n) -> p t h n", t=NT, h=GH)
    qdb = own.take(GH * NSEQ * 64).rearrange("p (h b n) -> p h b n", h=GH, b=NSEQ)
    st = own.take(2 * 2 * DV).rearrange("p (u j v) -> p u j v", u=2, j=2)
    ss = own.take(NSEQ * 2 * DV).rearrange("p (b j v) -> p b j v", b=NSEQ, j=2)
    kb = own.take(2 * 256).rearrange("p (u n) -> p u n", u=2)
    wa2, ba, dec, ggla = own.take(256), own.take(2), own.take(32).rearrange("p (j c) -> p j c", j=2), own.take(DV)
    sil, sq = own.take(512), own.take(512)
    r4 = own.take(2 * 4 * NT).rearrange("p (a t h) -> p a t h", a=2, t=NT)
    maskp = core.const("gla_p").bitcast(I32)
    masks = core.const("gla_s").bitcast(I32)

    s_in, s_out = core.sem("gla_in"), core.sem("gla_out")
    s_zero, s_ft, s_fa, s_fd = (core.sem(n) for n in ("gla_zeroed", "feat_ps", "feat_by_act", "feat_by_dve"))
    s_z, s_zc, s_l, s_cum, s_e, s_df, s_ke = (core.sem(n) for n in ("gate_ps", "gate_copied", "softplus", "cum_ready", "decays", "to_end", "end_decay"))
    s_qk, s_kend, s_ktp, s_kt = (core.sem(n) for n in ("qk_decayed", "kend_ready", "kt_ps", "kt_ready"))
    s_atp, s_att, s_u, s_s, s_o = (core.sem(n) for n in ("att_ps", "att_ready", "upd_ps", "state_ready", "o_ps"))
    s_kb, s_ub, s_sb = (core.sem(n) for n in ("kb_ready", "updb_ps", "stateb_ready"))
    s_osb, s_ssq, s_r4, s_er, s_mix = (core.sem(n) for n in ("o_copied", "o_sumsq", "o_rstd", "r_exp", "gla_mixed"))
    s_dve, s_act = core.sem("dve_p2"), core.sem("act_p2")
    core.s_kvout = core.sem("kv_stored")
    core.n_kvout = 0
    BPB = 3

    def queries(bank, t0, n, h, e):
        q = ps[64 * e:64 * e + 64, bank, :].rearrange("p (i n) -> p i n", i=4)
        return feat[64 * h:64 * h + 64, QN + e:QN + GRP:2, t0:t0 + n], q[:, 2 * h:2 * h + 2, 0:n]

    with nc.Block() as block:
        @block.sync
        def _(sp):
            sp.dma_start(scan, io["consts"][:, N_CONST_A + N_CONST_B:]).then_inc(s_in, 16)
            sp.dma_start(wa2[0:GRANK, :], io["w_a2"].rearrange("a r n -> (a r) n")).then_inc(s_in, 16)
            with nc.allow_non_contiguous_dma(reason="256 biases, one per partition"):
                sp.dma_start(ba, io["b_a"].rearrange("a (j p) -> p (a j)", j=2)).then_inc(s_in, 16)
            sp.dma_start(ggla, io["g_gla"].to_broadcast([P, DV])).then_inc(s_in, 16)
            sp.dma_start(ss, io["state_gla"].rearrange("a b (j e) d v -> (a e d) (b j) v", e=2)
                         .rearrange("p (b j) v -> p b j v", j=2)).then_inc(s_in, 16)
            for o, c in ((2, C_KC), (3, C_KS), (4, C_KW)):
                sp.dma_start(io[f"out_{o}"].rearrange("a b (t p) c h d -> p (a b t) (c h d)", p=P),
                             proj[:, 0:ST, c:c + 256]).then_inc(core.s_kvout, 16)
            for o, c in ((6, C_KC), (7, C_KS)):
                sp.dma_start(io[f"out_{o}"].rearrange("a b t c h d -> (a b t) (c h d)"),
                             proj[0:64, ST, c:c + 256]).then_inc(core.s_kvout, 16)
            for b in range(NSEQ):
                sp.dma_start(io["out_8"][0, b, SEQ - TS:SEQ].rearrange("t c h d -> t (c h d)"),
                             proj[TS * b:TS * b + TS, ST, C_KW:C_KW + 256]).then_inc(core.s_kvout, 16)
            sp.dma_start(io["out_8"][0, :, 0:SEQ - TS].rearrange("b t c h d -> b (t c h d)"),
                         io["state_win"][0, :, TS:SEQ].rearrange("b t c h d -> b (t c h d)")).then_inc(core.s_kvout, 16)
            core.n_kvout = 16 * (6 + NSEQ)
            sp.wait_ge(s_s, 1 + SEQ // CHUNK)
            sp.dma_start(io["out_5"].rearrange("a b (j e) d v -> (a b e d) j v", e=2), st[:, 0, :, :]).then_inc(s_out, 16)
            sp.wait_ge(s_sb, NSEQ)
            sp.dma_start(io["out_9"].rearrange("a b (j e) d v -> (a e d) (b j) v", e=2),
                         ss.rearrange("p b j v -> p (b j) v")).then_inc(s_out, 16)
            sp.wait_ge(s_out, 32)
            sp.wait_ge(core.s_kvout, core.n_kvout)

        @block.gpsimd
        def _(pool):
            pool.memset(qd, 0.0).then_inc(s_zero, 1)
            pool.memset(att, 0.0).then_inc(s_zero, 1)
            pool.memset(qdb, 0.0).then_inc(s_zero, 1)

        @block.tensor
        def _(pe):
            for t, (t0, n) in enumerate(TILES):
                pj = proj[0:n, t, :]
                srcs = [pj[:, c:c + P] for c in (C_NQ, C_NQ + P, C_NQ + 2 * P, C_NQ + 3 * P,
                                                 C_KS, C_KW, C_GQ, C_GQ + P, C_GK, C_GK + P)]
                base = BPB * (t % 2)
                if t >= 2:
                    pe.wait_ge(s_fa, 4 * (t - 1))
                    pe.wait_ge(s_fd, 3 * (t - 1))
                for i, src in enumerate(srcs):
                    last = pe.transpose(ps[:, base + i // 4, (i % 4) * P:(i % 4) * P + n], src, ident[0:n, 0:n])
                    if i in (3, 7):
                        last.then_inc(s_ft, 1)
                pe.transpose(ps[0:GRANK, base + 2, 2 * P:2 * P + n], pj[:, C_GA:C_GA + GRANK],
                             ident[0:n, 0:n]).then_inc(s_ft, 1)
            pe.wait_ge(s_fa, 4 * NT)
            pe.wait_ge(s_fd, 3 * NT)
            pe.wait_ge(s_in, 80)
            for j in range(2):
                w = wa2[0:GRANK, j * P:(j + 1) * P]
                pe.matmul(ps[:, 6 + j, :], w, feat[0:GRANK, GAF, 0:SEQ], start=True, stop=True)
                pe.matmul(ps[:, 5, j * 64:j * 64 + 64], w, feat[0:GRANK, GAF, SEQ:NTOK],
                          start=True, stop=True).then_inc(s_z, 1)
            pe.wait_ge(s_kend, 1)
            for t, (t0, n) in enumerate(TILES):
                for j in range(2):
                    last = pe.transpose(ps[0:n, t, j * P:(j + 1) * P], kend[:, j, t0:t0 + n], ident)
                last.then_inc(s_ktp, 1)
            pe.wait_ge(s_qk, 5)
            for t, (t0, n) in enumerate(TILES):
                if t >= 3:
                    pe.wait_ge(s_kt, t - 2)
                for h in range(GH):
                    last = pe.matmul(ps[0:n, (5 + t) % 8, h * n:h * n + n], kinv[:, h // 2, t0:t0 + n],
                                     qd[:, h, t0:t0 + n], start=True, stop=True)
                last.then_inc(s_atp, 1)
            pe.wait_ge(s_kt, NT)
            pe.wait_ge(s_att, NT)
            for ci in range(SEQ // CHUNK):
                t, c = divmod(ci, 2)
                r0 = CHUNK * c
                v = proj[:, t, C_GV:C_GV + 512]
                for j in range(2):
                    last = pe.matmul(ps[:, 4 + ci % 2, j * 256:(j + 1) * 256], kt[r0:r0 + CHUNK, t, j * P:(j + 1) * P],
                                     v[r0:r0 + CHUNK, j * 256:(j + 1) * 256], start=True, stop=True)
                last.then_inc(s_u, 1)
                pe.wait_ge(s_s, ci + 1)
                if c == 0 and t >= 2:
                    pe.wait_ge(s_osb, t - 1)
                for h in range(GH):
                    out = ps[r0:r0 + CHUNK, 2 + t % 2, h * DV:(h + 1) * DV]
                    pe.matmul(out, att[:, t, h, r0:r0 + CHUNK], v[:, h * DV:(h + 1) * DV], start=True, stop=False)
                    last = pe.matmul(out, qd[:, h, t * P + r0:t * P + r0 + CHUNK], st[:, ci % 2, h // 2, :],
                                     start=False, stop=True)
                if c == 1:
                    last.then_inc(s_o, 1)
            v = proj[0:64, ST, C_GV:C_GV + 512]
            pe.wait_ge(s_qk, 6)
            for h in range(GH):
                out = ps[0:64, 6, h * DV:(h + 1) * DV]
                pe.matmul(out, att[0:64, ST, h, 0:64], v[:, h * DV:(h + 1) * DV], start=True, stop=False)
                for b in range(NSEQ):
                    last = pe.matmul(out, qdb[:, h, b, :], ss[:, b, h // 2, :], start=False, stop=(b == NSEQ - 1))
            last.then_inc(s_o, 1)
            for b in range(NSEQ):
                pe.wait_ge(s_kb, b + 1)
                if b >= 2:
                    pe.wait_ge(s_sb, b - 1)
                for j in range(2):
                    last = pe.matmul(ps[:, b % 2, j * 256:(j + 1) * 256], kb[0:64, b % 2, j * P:(j + 1) * P],
                                     v[:, j * 256:(j + 1) * 256], start=True, stop=True)
                last.then_inc(s_ub, 1)

        @block.scalar
        def _(act):
            link = linker(act, s_act)
            for t, (t0, n) in enumerate(TILES):
                base = BPB * (t % 2)
                act.wait_ge(s_ft, 3 * t + 1)
                for h in range(KVH):
                    for e in range(2):
                        act.activation(*queries(base, t0, n, h, e), ACT.Copy).then_inc(s_fa, 1)
            act.wait_ge(s_in, 80)
            act.wait_ge(s_zc, 1)
            link(act.activation(e1, e2, ACT.Abs))
            link(act.activation(e1, e1, ACT.Exp, scale=-1.0))
            act.activation(e1, e1, ACT.Ln, bias=core.const("one")).then_inc(s_l, 1)
            act.wait_ge(s_cum, 2)
            g16 = 1.0 / 16.0
            act.activation(e1, cum, ACT.Exp, scale=g16)
            act.activation(dec[:, :, 0:8], cum[:, :, CHUNK - 1:SEQ:CHUNK], ACT.Exp, scale=g16)
            act.activation(dec[:, :, 8:16], cum[:, :, SEQ + TS - 1:NTOK:TS], ACT.Exp, scale=g16)
            act.activation(e2, cum, ACT.Exp, scale=-g16).then_inc(s_e, 1)
            act.wait_ge(s_df, 1)
            act.activation(kend, kend, ACT.Exp, scale=g16).then_inc(s_ke, 1)
            for t, (t0, n) in enumerate(TILES):
                act.wait_ge(s_ktp, t + 1)
                act.activation(kt[0:n, t, :], ps[0:n, t, 0:256], ACT.Copy).then_inc(s_kt, 1)
            for t, (t0, n) in enumerate(TILES):
                if t >= 1:
                    act.wait_ge(s_mix, t)
                act.activation(sil[0:n, :], proj[0:n, t, C_GR:C_GR + 512], ACT.Exp, scale=-1.0).then_inc(s_er, 1)
                act.wait_ge(s_o, t + 1)
                act.activation(mix[0:n, t, 0:512], ps[0:n, 2 + t % 2 if t < ST else 6, :], ACT.Copy).then_inc(s_osb, 1)
                act.wait_ge(s_ssq, t + 1)
                link(act.activation(r4[0:n, 1, t, :], r4[0:n, 0, t, :], ACT.Ln, scale=1.0 / DV,
                                    bias=core.const("eps")[0:n, :]))
                act.activation(r4[0:n, 1, t, :], r4[0:n, 1, t, :], ACT.Exp, scale=-0.5).then_inc(s_r4, 1)

        @block.vector
        def _(dve):
            link = linker(dve, s_dve)
            for t, (t0, n) in enumerate(TILES):
                base = BPB * (t % 2)
                dve.wait_ge(s_ft, 3 * t + 2)
                dve.tensor_copy(feat[:, 4:8, t0:t0 + n], ps[:, base + 1, :].rearrange("p (i n) -> p i n", i=4)[:, :, 0:n]
                                ).then_inc(s_fd, 1)
                dve.wait_ge(s_ft, 3 * t + 3)
                dve.tensor_copy(feat[:, 8:10, t0:t0 + n], ps[:, base + 2, 0:256].rearrange("p (i n) -> p i n", i=2)[:, :, 0:n]
                                ).then_inc(s_fd, 1)
                dve.tensor_copy(feat[0:GRANK, GAF, t0:t0 + n], ps[0:GRANK, base + 2, 2 * P:2 * P + n]).then_inc(s_fd, 1)
            dve.wait_ge(s_in, 80)
            dve.memset(st[:, 0], 0.0).then_inc(s_s, 1)
            dve.wait_ge(s_z, 2)
            for j in range(2):
                dve.tensor_scalar(e2[:, j, 0:SEQ], ps[:, 6 + j, :], ba[:, j:j + 1], None, ALU.add)
                last = dve.tensor_scalar(e2[:, j, SEQ:NTOK], ps[:, 5, j * 64:j * 64 + 64], ba[:, j:j + 1], None, ALU.add)
            last.then_inc(s_zc, 1)
            dve.wait_ge(s_l, 1)
            link(dve.scalar_tensor_tensor(e2, e2, 0.0, e1, ALU.min, ALU.subtract))
            for j in range(2):
                dve.tensor_tensor_scan(cum[:, j, :], scan, e2[:, j, :], 0.0, ALU.mult, ALU.add).then_inc(s_cum, 1)
            dve.wait_ge(s_cum, 2)
            for a, b, c in ((0, SEQ, CHUNK), (SEQ, NTOK, TS)):
                cv = cum[:, :, a:b].rearrange("p j (c n) -> p j c n", n=c)
                last = dve.tensor_tensor(kend[:, :, a:b].rearrange("p j (c n) -> p j c n", n=c),
                                         cv[:, :, :, c - 1:c].to_broadcast([P, 2, (b - a) // c, c]), cv, ALU.subtract)
            last.then_inc(s_df, 1)
            dve.wait_ge(s_ke, 1)
            dve.tensor_tensor(kend, kend, feat[:, GKF:GKF + 2, :], ALU.mult).then_inc(s_kend, 1)
            dve.wait_ge(s_e, 1)
            dve.wait_ge(s_zero, 3)
            for h in range(GH):
                e0 = 64 * (h % 2)
                dve.scalar_tensor_tensor(qd[e0:e0 + 64, h, :], feat[e0:e0 + 64, GQF + h // 2, :], DK ** -0.5,
                                         e1[e0:e0 + 64, h // 2, :], ALU.mult, ALU.mult).then_inc(s_qk, 1)
            dve.tensor_tensor(kinv, feat[:, GKF:GKF + 2, :], e2, ALU.mult).then_inc(s_qk, 1)
            dve.wait_ge(s_qk, 4)
            for h in range(GH):
                diag = qdb[:, h, :, :].rearrange("p b (c n) -> p (b c) n", n=TS)[:, 0::NSEQ + 1, :]
                last = dve.tensor_copy(diag, qd[:, h, SEQ:NTOK].rearrange("p (b n) -> p b n", n=TS))
            last.then_inc(s_qk, 1)
            for t, (t0, n) in enumerate(TILES):
                dve.wait_ge(s_atp, t + 1)
                m = maskp if t < ST else masks[0:64, :]
                dve.copy_predicated(att[0:n, t, :, 0:n], bcast(m, 1, GH),
                                    ps[0:n, (5 + t) % 8, 0:GH * n].rearrange("p (h n) -> p h n", h=GH)).then_inc(s_att, 1)

            def state_step(dst, src, bank, col):
                for h in range(GH):
                    j, e = divmod(h, 2)
                    last = dve.scalar_tensor_tensor(dst[64 * e:64 * e + 64, j, :], src[64 * e:64 * e + 64, j, :],
                                                    dec[64 * e:64 * e + 64, j, col:col + 1],
                                                    ps[64 * e:64 * e + 64, bank, h * DV:(h + 1) * DV], ALU.mult, ALU.add)
                return last

            def finish_tile(t):
                n = TILES[t][1]
                o = mix[0:n, t, 0:512]
                o4 = o.rearrange("p (h v) -> p h v", h=GH)
                dve.wait_ge(s_er, t + 1)
                link(dve.tensor_scalar(sil[0:n, :], sil[0:n, :], 1.0, None, ALU.add))
                link(dve.reciprocal(sil[0:n, :], sil[0:n, :]))
                link(dve.tensor_tensor(sil[0:n, :], sil[0:n, :], proj[0:n, t, C_GR:C_GR + 512], ALU.mult))
                dve.wait_ge(s_osb, t + 1)
                link(dve.tensor_tensor(sq[0:n, :], o, o, ALU.mult))
                dve.reduce_sum(r4[0:n, 0, t, :], sq[0:n, :].rearrange("p (h v) -> p h v", h=GH), AX.X).then_inc(s_ssq, 1)
                link(dve.tensor_tensor(sil[0:n, :].rearrange("p (h v) -> p h v", h=GH),
                                       sil[0:n, :].rearrange("p (h v) -> p h v", h=GH), bcast(ggla[0:n, :], 1, GH), ALU.mult))
                dve.wait_ge(s_r4, t + 1)
                link(dve.tensor_tensor(o4, o4, bcast(r4[0:n, 1, t, :], 2, DV), ALU.mult))
                dve.tensor_tensor(o, o, sil[0:n, :], ALU.mult).then_inc(s_mix, 1)

            for ci in range(SEQ // CHUNK):
                dve.wait_ge(s_u, ci + 1)
                dve.wait_ge(s_s, ci + 1)
                state_step(st[:, (ci + 1) % 2], st[:, ci % 2], 4 + ci % 2, ci).then_inc(s_s, 1)
                if ci % 2 == 1 and ci >= 3:
                    finish_tile(ci // 2 - 1)
            for b in range(NSEQ):
                if b >= 2:
                    dve.wait_ge(s_ub, b - 1)
                dve.tensor_scalar(kb[0:64, b % 2, :], kt[0:64, ST, :], core.const("seq_of")[0:64, b:b + 1], None,
                                  ALU.mult).then_inc(s_kb, 1)
                if b == 0:
                    finish_tile(ST - 1)
                if b >= 1:
                    dve.wait_ge(s_ub, b)
                    state_step(ss[:, b - 1], ss[:, b - 1], (b - 1) % 2, 8 + b - 1).then_inc(s_sb, 1)
            dve.wait_ge(s_ub, NSEQ)
            state_step(ss[:, NSEQ - 1], ss[:, NSEQ - 1], (NSEQ - 1) % 2, 8 + NSEQ - 1).then_inc(s_sb, 1)
            finish_tile(ST)


def compress(core):
    nc, io, ps = core.nc, core.io, core.psum
    proj, ident = core.proj, core.const("ident")
    own = Stack(core, core.z0, core.z1)
    NB = NCMP_S
    core.kc = own.take((NSEQ + 1) * NB).rearrange("p (s n) -> p s n", n=NB)
    core.vc = own.take((NSEQ + 1) * P).rearrange("p (s n) -> p s n", n=P)
    kc, vc = core.kc, core.vc
    core.z_att = own.at
    CL = 2 * GAPS
    phi = own.take(2 * CL * P).rearrange("p (c l n) -> p c l n", c=2, l=CL)
    RING = 2 * PAST // PAGE
    rows = own.take(RING * 256).rearrange("p (u n) -> p u n", u=RING)
    kvT = own.take(2 * 2 * PAST).rearrange("p (c s n) -> p c s n", c=2, s=2)
    pe_in, peb = own.take(P), own.take(2)
    vT = own.take(2 * NB).rearrange("p (s n) -> p s n", n=NB)
    table = own.take(64).bitcast(I32)
    NPG = NSEQ * PAST // PAGE
    NGRP = 1 + NSEQ // 2
    NP0 = SEQ // PAGE // 2
    PAIRS = [(0, 0, q) for q in range(NP0)] + [(g, s, q) for g in range(1, NGRP) for s in range(2)
                                               for q in range(PAST // PAGE // 2)]
    PPG = RING // 2
    UPTO = [NP0 + PPG * g for g in range(NGRP)]

    def group(g):
        return (NSEQ, 1, NCMP_P) if g == 0 else (2 * g - 2, 2, NCMP_S)

    def starts(i):
        g = PAIRS[i][0]
        return g if g > 0 and i == UPTO[g - 1] + 1 else None

    s_in, s_zero, s_pt = (core.sem(n) for n in ("phi_in", "phi_zeroed", "table_in"))
    s_page = [core.sem(f"page_in{i}") for i in range(RING)]
    s_tr, s_tra, s_trd, s_acc = (core.sem(n) for n in ("kvT_ps", "kvT_by_act", "kvT_by_dve", "cmp_ps"))
    s_peT, s_pec, s_pebc = (core.sem(n) for n in ("peT_ps", "peT_ready", "pe_bias"))
    s_kc, s_vt, s_vtp, s_vc = (core.sem(n) for n in ("kc_ready", "vT_ready", "vc_ps", "vc_ready"))
    cache = io["cache_cmp"].rearrange("a n t c h d -> (a n) t (c h d)")

    with nc.Block() as block:
        def results(act, g):
            first, n, nb = group(g)
            act.wait_ge(s_acc, g + 1)
            if g == 0:
                for c in range(2):
                    last = act.activation(peb[:, c:c + 1], ps[:, 4 + 2 * c, nb:nb + 1], ACT.Copy)
                last.then_inc(s_pebc, 1)
                act.wait_ge(s_pebc, 1)
            src = [ps[:, 4 + 2 * c + g % 2, 0:n * nb].rearrange("p (s n) -> p s n", n=nb) for c in range(2)]
            act.activation(kc[:, first:first + n, 0:nb], src[0], ACT.Identity, bias=peb[:, 0:1]).then_inc(s_kc, 1)
            if g > 0:
                act.wait_ge(s_vtp, g)
            act.activation(vT[:, 0:n, 0:nb], src[1], ACT.Identity, bias=peb[:, 1:2]).then_inc(s_vt, 1)

        def kv_copy(eng, i, copy):
            g, s, q = PAIRS[i]
            if g > 0 and i < UPTO[g - 1] + 2:
                eng.wait_ge(s_acc, g)
            return copy(kvT[:, :, s, q * 2 * PAGE:(q + 1) * 2 * PAGE], ps[:, i % 4, :].rearrange("p (c n) -> p c n", c=2))

        def v_out(dve, g):
            first, n, nb = group(g)
            dve.wait_ge(s_vtp, g + 1)
            dve.tensor_copy(vc[0:nb, first:first + n, :],
                            ps[0:nb, 6 + g % 2, 256:256 + n * P].rearrange("p (s n) -> p s n", n=P)).then_inc(s_vc, 1)

        @block.gpsimd
        def _(pool):
            pool.memset(kvT[:, :, 1, CL:SEQ], 0.0).then_inc(s_zero, 1)
            for h in range(KVH):
                pool.wait_ge(s_zero, 1 + h)
                pool.memset(phi[64 * h:64 * h + 64, :, :, 64 * (1 - h):64 * (1 - h) + 64], 0.0).then_inc(s_zero, 1)

        @block.scalar
        def _(act):
            for h in range(KVH):
                for c in range(2):
                    act.dma_start(phi[64 * h:64 * h + 64, c, :, 64 * h:64 * h + 64],
                                  io["phi_w"][0, c].rearrange("(l d) n -> d l n", d=HD)).then_inc(s_in, 16)
                act.dma_start(pe_in[0:2 * CL, 64 * h:64 * h + 64],
                              io["phi_pe"].rearrange("a c l d -> (a c l) d")).then_inc(s_in, 16)
            for i in range(len(PAIRS)):
                if i % 2 == 0:
                    act.wait_ge(s_tr, i + 1)
                    kv_copy(act, i, lambda o, s: act.activation(o, s, ACT.Copy)).then_inc(s_tra, 1)
                if starts(i):
                    results(act, starts(i) - 1)
            results(act, NGRP - 1)

        @block.vector
        def _(dve):
            dve.wait_ge(s_peT, 1)
            dve.tensor_copy(kvT[:, :, 1, 0:CL], ps[:, 5, 0:2 * CL].rearrange("p (c l) -> p c l", c=2)).then_inc(s_pec, 1)
            for i in range(len(PAIRS)):
                if i % 2 == 1:
                    dve.wait_ge(s_tr, i + 1)
                    kv_copy(dve, i, dve.tensor_copy).then_inc(s_trd, 1)
                if starts(i):
                    v_out(dve, starts(i) - 1)
            v_out(dve, NGRP - 1)

        @block.tensor
        def _(pe):
            def accumulate(g):
                _, n, nb = group(g)
                pe.wait_ge(s_tra, UPTO[g] // 2)
                pe.wait_ge(s_trd, UPTO[g] // 2)
                if g == 0:
                    n = 2
                    pe.wait_ge(s_pec, 1)
                    pe.wait_ge(s_zero, 1 + KVH)
                if g >= 2:
                    pe.wait_ge(s_vt, g - 1)
                    pe.wait_ge(s_vc, g - 1)
                for c in range(2):
                    for l in range(CL):
                        last = pe.matmul(ps[:, 4 + 2 * c + g % 2, 0:n * nb].rearrange("p (s n) -> p s n", n=nb),
                                         phi[:, c, l, :], kvT[:, c, 0:n, l:l + GAPS * (nb - 1) + 1:GAPS],
                                         start=(l == 0), stop=(l == CL - 1))
                last.then_inc(s_acc, 1)

            def v_back(g):
                _, n, nb = group(g)
                pe.wait_ge(s_vt, g + 1)
                for s in range(n):
                    last = pe.transpose(ps[0:nb, 6 + g % 2, 256 + s * P:256 + (s + 1) * P], vT[:, s, 0:nb], ident)
                last.then_inc(s_vtp, 1)

            for i, (g, s, q) in enumerate(PAIRS):
                if i >= 4:
                    pe.wait_ge(s_tra if i % 2 == 0 else s_trd, (i - 4) // 2 + 1)
                for u in range(2):
                    k = 2 * (i - NP0) + u
                    if g > 0:
                        pe.wait_ge(s_page[k % RING], 16 * (k // RING + 1))
                    for c in range(2):
                        src = (rows[:, k % RING, c * P:(c + 1) * P] if g > 0
                               else proj[:, 2 * q + u, C_KC + c * P:C_KC + (c + 1) * P])
                        last = pe.transpose(ps[:, i % 4, c * 256 + u * P:c * 256 + (u + 1) * P], src, ident)
                last.then_inc(s_tr, 1)
                if i == 0:
                    pe.wait_ge(s_in, 96)
                    pe.transpose(ps[:, 5, 0:2 * CL], pe_in[0:2 * CL, :], ident[0:2 * CL, 0:2 * CL]).then_inc(s_peT, 1)
                if i == UPTO[g] - 1:
                    accumulate(g)
                if starts(i):
                    v_back(g - 1)
            v_back(NGRP - 1)

        @block.sync
        def _(sp):
            sp.dma_start(table[0:1, 0:NPG], io["page_table"].rearrange("b n -> (b n)").unsqueeze(0)).then_inc(s_pt, 16)
            sp.wait_ge(s_pt, 16)

            def load(k, u):
                page = sp.value_load(table[0:1, bass.ds(k, 1)] if not isinstance(k, int) else table[0:1, k:k + 1],
                                     min_val=0, max_val=cache.shape[0] - 1)
                sp.dma_start(rows[:, u, :], cache[bass.ds(page, 1), :, :].rearrange("n t c -> (n t) c")
                             ).then_inc(s_page[u], 16)
            for u in range(RING):
                load(u, u)
            with sp.Fori(1, NPG // RING) as q:
                for u in range(RING):
                    if u % 2 == 0:
                        sp.wait_ge(s_tr, NP0 + PPG * (q - 1) + u // 2 + 1)
                    load(RING * q + u, u)


BIG = 1e28


def past_buffers(core):
    top = Stack(core, core.z1 - 4 * PAST // PAGE * 256 - 64, core.z1)
    core.table = top.take(64).bitcast(I32)
    core.sel = top.take(4 * PAST // PAGE * 256).rearrange("p (u k n) -> p u k n", u=4, k=PAST // PAGE)
    core.win = core.proj[:, 0:ST, 0:SEQ // P * 256].rearrange("p u (k n) -> p u k n", k=SEQ // P)
    core.s_table = core.sem("table2_in", carry=True)
    core.s_sel = [core.sem(f"sel_in{i}", carry=True) for i in range(4)]
    core.s_win = [core.sem(f"old_win_in{i}", carry=True) for i in range(4)]


def load_past(core, eng, b):
    cache = core.io["cache_sel"].rearrange("a n t c h d -> (a n) t (c h d)")
    old_win = core.io["state_win"].rearrange("a b (k p) c h d -> (a b) p k (c h d)", p=P)
    for k in range(PAST // PAGE):
        at = b * PAST // PAGE + k
        page = eng.value_load(core.table[0:1, at:at + 1], min_val=0, max_val=cache.shape[0] - 1)
        eng.dma_start(core.sel[:, b % 4, k, :], cache[bass.ds(page, 1), :, :].rearrange("n t c -> (n t) c")
                      ).then_inc(core.s_sel[b % 4], 16)
    eng.dma_start(core.win[:, b % 4, :, :], old_win[b]).then_inc(core.s_win[b % 4], 16)


def prompt_attention(core):
    nc, io, ps = core.nc, core.io, core.psum
    proj, feat, mix, ident, kc, vc = core.proj, core.feat, core.mix, core.const("ident"), core.kc, core.vc
    own = Stack(core, core.z_att, core.z1)
    core.gates = own.take(NT * 24).rearrange("p (t n) -> p t n", t=NT)
    core.identb = own.take(P // 2).bitcast(BF16)
    core.maskb = own.take((P + 256 + 8 + 8 * NCMP_P) // 2).bitcast(BF16)
    core.z_samp = own.at
    gates, identb, maskb = core.gates, core.identb, core.maskb
    kz = own.take(2 * KVH * SEQ).rearrange("p (b h n) -> p b h n", b=2, h=KVH)
    kzc = own.take(KVH * NCMP_P)
    pp = own.take(2 * 2 * KVH * SEQ).rearrange("p (u b h n) -> p u b h n", u=2, b=2, h=KVH)
    pc = own.take(2 * KVH * NCMP_P).rearrange("p (u h n) -> p u h n", u=2, h=KVH)
    pT = own.take(2 * 4 * P).rearrange("p (u k n) -> p u k n", u=2, k=4)
    mx = own.take(2 * 6).rearrange("p (u n) -> p u n", u=2)
    su = own.take(2 * 6).rearrange("p (u n) -> p u n", u=2)
    co = own.take(2 * 6).rearrange("p (u n) -> p u n", u=2)
    tmp = own.take(6 * HD).rearrange("p (b n) -> p b n", b=6)
    NU = (SEQ // P) * GRP
    SC = HD ** -0.5

    s_zero, s_prep, s_ge = core.sem("kz_zeroed"), core.sem("prompt_prep"), core.sem("gates_exp")
    s_scw, s_scs, s_scc = core.sem("win_scores"), core.sem("sel_scores"), core.sem("cmp_scores")
    s_mx, s_p = core.sem("max_ready"), core.sem("probs_ready")
    s_pt, s_pta, s_ptd, s_o, s_ou = (core.sem(n) for n in ("pT_ps", "pT_by_act", "pT_by_dve", "po_ps", "po_used"))
    s_dve = core.sem("dve_p4")
    past_buffers(core)
    NR = 5

    with nc.Block() as block:
        @block.gpsimd
        def _(pool):
            for h in range(KVH):
                rows = slice(64 * (1 - h), 64 * (1 - h) + 64)
                pool.memset(kz[rows, :, h, :], 0.0).then_inc(s_zero, 1)
                pool.memset(kzc[rows, h * NCMP_P:(h + 1) * NCMP_P], 0.0).then_inc(s_zero, 1)
            pool.wait_ge(core.s_table, 16)
            load_past(core, pool, 1)
            load_past(core, pool, 3)

        @block.sync
        def _(sp):
            sp.dma_start(core.table[0:1, 0:NSEQ * PAST // PAGE],
                         core.io["page_table"].rearrange("b n -> (b n)").unsqueeze(0)).then_inc(core.s_table, 16)
            sp.wait_ge(core.s_table, 16)
            load_past(core, sp, 0)
            load_past(core, sp, 2)

        def move_pT(eng, k, copy):
            u, r = divmod(k, NR)
            nb = u // GRP + 1
            eng.wait_ge(s_pt, k + 1)
            if r == 0:
                return copy(pT[0:NCMP_P, k % 2, 0:KVH, :],
                            ps[0:NCMP_P, 5 + k % 2, 0:KVH * P].rearrange("p (k n) -> p k n", n=P))
            return copy(pT[:, k % 2, 0:nb, :], ps[:, 5 + k % 2, 0:nb * P].rearrange("p (k n) -> p k n", n=P))

        @block.scalar
        def _(act):
            act.activation(gates[:, 0:ST, :], proj[:, 0:ST, C_NG:C_NG + 24], ACT.Exp, scale=-1.0)
            act.activation(gates[0:64, ST, :], proj[0:64, ST, C_NG:C_NG + 24], ACT.Exp, scale=-1.0).then_inc(s_ge, 1)

            def exps(u):
                nk = (u // GRP + 1) * P
                act.wait_ge(s_mx, u + 1)
                for h in range(KVH):
                    act.activation(pc[:, u % 2, h, :], ps[:, 4, h * NCMP_P:(h + 1) * NCMP_P], ACT.Exp, scale=SC,
                                   bias=mx[:, u % 2, h:h + 1], accum_out=su[:, u % 2, h:h + 1])
                for b in range(2):
                    for h in range(KVH):
                        last = act.activation(pp[:, u % 2, b, h, 0:nk], ps[:, 2 * b + h, 0:nk], ACT.Exp, scale=SC,
                                              bias=mx[:, u % 2, 2 + 2 * b + h:3 + 2 * b + h],
                                              accum_out=su[:, u % 2, 2 + 2 * b + h:3 + 2 * b + h])
                last.then_inc(s_p, 1)

            exps(0)
            for u in range(NU):
                mine = [k for k in range(NR * u, NR * u + NR) if k % 2 == 0]
                for i, k in enumerate(mine):
                    if i == 1 and u + 1 < NU:
                        exps(u + 1)
                    move_pT(act, k, lambda o, s: act.activation(o, s, ACT.Copy)).then_inc(s_pta, 1)

        @block.vector
        def _(dve):
            link = linker(dve, s_dve)
            dve.wait_ge(s_zero, 4)
            for h in range(KVH):
                rows = slice(64 * h, 64 * h + 64)
                dve.tensor_copy(kz[rows, 0, h, :], feat[rows, KSF, 0:SEQ])
                dve.tensor_copy(kz[rows, 1, h, :], feat[rows, KWF, 0:SEQ])
                dve.tensor_copy(kzc[rows, h * NCMP_P:(h + 1) * NCMP_P], kc[rows, NSEQ, 0:NCMP_P])
            dve.tensor_copy(identb, ident)
            at = 0
            for name in ("causal", "new_keys", "win_old", "cmp_p"):
                m = core.const(name)
                last = dve.tensor_copy(maskb[:, at:at + m.shape[1]], m)
                at += m.shape[1]
            last.then_inc(s_prep, 1)
            dve.wait_ge(s_ge, 1)
            for g in (gates[:, 0:ST, :], gates[0:64, ST, :]):
                link(dve.tensor_scalar(g, g, 1.0, None, ALU.add))
                link(dve.reciprocal(g, g))

            def maxima(u):
                nk = (u // GRP + 1) * P
                m = mx[:, u % 2, :]
                dve.wait_ge(s_scc, u + 1)
                if u >= 2:
                    dve.wait_ge(s_p, u - 1)
                dve.tensor_reduce(m[:, 0:2], ps[:, 4, 0:KVH * NCMP_P].rearrange("p (h n) -> p h n", h=KVH), AX.X, ALU.max)
                dve.wait_ge(s_scs, u + 1)
                dve.tensor_reduce(m[:, 2:4], ps[:, 0:2, 0:nk], AX.X, ALU.max)
                dve.wait_ge(s_scw, u + 1)
                link(dve.tensor_reduce(m[:, 4:6], ps[:, 2:4, 0:nk], AX.X, ALU.max))
                dve.tensor_scalar(m, m, -SC, BIG, ALU.mult, ALU.min).then_inc(s_mx, 1)

            maxima(0)
            for u in range(NU):
                t, g = divmod(u, GRP)
                if u + 1 < NU:
                    maxima(u + 1)
                for k in range(NR * u, NR * u + NR):
                    if k % 2 == 1:
                        move_pT(dve, k, dve.tensor_copy).then_inc(s_ptd, 1)
                dve.wait_ge(s_p, u + 1)
                c, s = co[:, u % 2, :], su[:, u % 2, :]
                link(dve.tensor_scalar(c, s, 1e-30, None, ALU.max))
                link(dve.reciprocal(c, c))
                gv = gates[:, t, :].rearrange("p (h g b) -> p b h g", h=KVH, g=GRP)[:, :, :, g]
                cv = c.rearrange("p (b h) -> p b h", h=KVH)
                link(dve.tensor_tensor(cv, cv, gv, ALU.mult))
                dve.wait_ge(s_o, u + 1)
                o = ps[:, 7, 0:6 * HD].rearrange("p (b n) -> p b n", b=6)
                dve.tensor_tensor(tmp, o, bcast(c, 2, HD), ALU.mult).then_inc(s_ou, 1)
                dve.wait_ge(s_ou, u + 1)
                dst = mix[:, t, 512:1024].rearrange("p (h g d) -> p g h d", h=KVH, g=GRP)[:, g]
                link(dve.tensor_tensor(dst, tmp[:, 0:2, :], tmp[:, 2:4, :], ALU.add))
                link(dve.tensor_tensor(dst, dst, tmp[:, 4:6, :], ALU.add))

        @block.tensor
        def _(pe):
            cmp_at = P + 256 + 8

            def scores(u):
                t, g = divmod(u, GRP)
                nk = (t + 1) * P
                q = feat[:, QN + g, t * P:(t + 1) * P]
                if u >= 1:
                    pe.wait_ge(s_p, u)
                pe.matmul(ps[:, 4, 0:KVH * NCMP_P], q, kzc, start=True, stop=False)
                pe.matmul(ps[:, 4, 0:KVH * NCMP_P], identb,
                          maskb[:, cmp_at + t * 2 * NCMP_P:cmp_at + (t + 1) * 2 * NCMP_P],
                          start=False, stop=True).then_inc(s_scc, 1)
                for b, sem in enumerate((s_scs, s_scw)):
                    for h in range(KVH):
                        pe.matmul(ps[:, 2 * b + h, 0:nk], q, kz[:, b, h, 0:nk], start=True, stop=False)
                        last = pe.matmul(ps[:, 2 * b + h, nk - P:nk], identb, maskb[:, 0:P], start=False, stop=True)
                    last.then_inc(sem, 1)

            def to_key_major(k):
                u, r = divmod(k, NR)
                if k >= 2:
                    pe.wait_ge(s_pta if k % 2 == 0 else s_ptd, (k - 2) // 2 + 1)
                if r == 0:
                    for h in range(KVH):
                        last = pe.transpose(ps[0:NCMP_P, 5 + k % 2, h * P:(h + 1) * P], pc[:, u % 2, h, :], ident)
                else:
                    b, h = divmod(r - 1, KVH)
                    for kb in range(u // GRP + 1):
                        last = pe.transpose(ps[:, 5 + k % 2, kb * P:(kb + 1) * P],
                                            pp[:, u % 2, b, h, kb * P:(kb + 1) * P], ident)
                last.then_inc(s_pt, 1)

            def values(k):
                u, r = divmod(k, NR)
                pe.wait_ge(s_pta if k % 2 == 0 else s_ptd, k // 2 + 1)
                if r == 0 and u >= 1:
                    pe.wait_ge(s_ou, u)
                if r == 0:
                    for h in range(KVH):
                        last = pe.matmul(ps[:, 7, h * HD:(h + 1) * HD], pT[0:NCMP_P, k % 2, h, :],
                                         vc[0:NCMP_P, NSEQ, h * HD:(h + 1) * HD], start=True, stop=True)
                else:
                    b, h = divmod(r - 1, KVH)
                    c0 = (C_KS, C_KW)[b] + P + h * HD
                    nb = u // GRP + 1
                    for kb in range(nb):
                        last = pe.matmul(ps[:, 7, (2 + 2 * b + h) * HD:(3 + 2 * b + h) * HD], pT[:, k % 2, kb, :],
                                         proj[:, kb, c0:c0 + HD], start=(kb == 0), stop=(kb == nb - 1))
                if r == NR - 1:
                    last.then_inc(s_o, 1)

            pe.wait_ge(s_prep, 1)
            scores(0)
            for u in range(NU):
                if u + 1 < NU:
                    scores(u + 1)
                else:
                    pe.wait_ge(s_p, u + 1)
                for r in range(NR):
                    to_key_major(NR * u + r)
                    if r >= 1:
                        values(NR * u + r - 1)
                values(NR * u + NR - 1)


def sample_attention(core):
    nc, io, ps = core.nc, core.io, core.psum
    proj, feat, mix, ident, kc, vc = core.proj, core.feat, core.mix, core.const("ident"), core.kc, core.vc
    gates, identb, maskb = core.gates, core.identb, core.maskb
    own = Stack(core, core.z_samp, core.z1 - 4 * PAST // PAGE * 256 - 64)
    sel, win, s_vin, s_win = core.sel, core.win, core.s_sel, core.s_win
    NP, R = PAST // PAGE, NSEQ * TS
    NWT = SEQ // P
    NKS, NKW = PAST + R, SEQ + R
    qs = own.take(NSEQ * 64).rearrange("p (b n) -> p b n", b=NSEQ)
    grow = own.take(NSEQ // 2 * 3).rearrange("p (i b) -> p i b", b=3)
    kTs = own.take(2 * PAST).rearrange("p (s n) -> p s n", s=2)
    kTw = own.take(2 * SEQ).rearrange("p (s n) -> p s n", s=2)
    ss, ws, pc = own.take(NKS), own.take(NKW), own.take(64)
    pT = own.take(16 * P).rearrange("p (k n) -> p k n", k=16)
    im, sc, sc2, v8, bm = own.take(16), own.take(16), own.take(16), own.take(8), own.take(16)
    mx, su, co = own.take(3), own.take(3), own.take(3)
    res = own.take(2 * P).rearrange("p (u n) -> p u n", u=2)
    nsa_d = nc.dram_tensor("nsa_rows", [KVH, GRP, NSEQ, TS, HD], F32).ap()
    gate_d = nc.dram_tensor("gate_rows", [R, 24], F32).ap()
    NU, SC = NSEQ // 2, HD ** -0.5
    A, C, W, O, T0 = 0, 2, 3, 4, 5

    rounds = [("k", 0, r) for r in range(6)]
    for i in range(NU):
        if i + 1 < NU:
            rounds += [("k", i + 1, r) for r in range(6)]
        rounds += [("p", i, r) for r in range(4)]
    number = {x: n for n, x in enumerate(rounds)}

    s_zero, s_q, s_gd, s_gr = (core.sem(n) for n in ("qs_zeroed", "qs_ready", "gates_out", "gate_rows_in"))
    s_tr, s_ea, s_ed = core.sem("tr_ps"), core.sem("tr_by_act"), core.sem("tr_by_dve")
    s_sc, s_cc, s_wc, s_mc, s_ec = (core.sem(n) for n in ("scores_ps", "small_copied", "win_copied", "cmp_max", "cmp_exp"))
    s_im, s_imp, s_pn = core.sem("imp_rows"), core.sem("imp_ps"), core.sem("cmp_normed")
    s_ms, s_mw, s_es, s_ew = (core.sem(n) for n in ("sel_max", "win_max", "sel_exp", "win_exp"))
    s_pv, s_res, s_back = (core.sem(n) for n in ("pv_ps", "res_ready", "nsa_in"))
    s_rout = [core.sem(f"res_out{u}") for u in range(2)]
    s_dve = core.sem("dve_p5")

    def evacuate(eng, n, copy):
        kind, i, r = rounds[n]
        src = ps[:, T0 + n % 3, :]
        eng.wait_ge(s_tr, n + 1)
        if kind == "p":
            rows = 64 if r == 2 else P
            nb = 3 if r == 2 else 4
            return copy(pT[0:rows, 4 * r:4 * r + nb, :], src[0:rows, 0:nb * P].rearrange("p (k n) -> p k n", n=P))
        s, q = divmod(r, 3)
        if q < 2:
            return copy(kTs[:, s, q * 512:(q + 1) * 512], src)
        return copy(kTw[:, s, :], src)

    def by_act(n):
        return n % 2 == 0

    with nc.Block() as block:
        @block.sync
        def _(sp):
            sp.dma_start(gate_d, gates[0:R, ST, :]).then_inc(s_gd, 16)
            sp.wait_ge(s_gd, 16)
            for b in range(NSEQ):
                sp.dma_start(grow[64 * (b % 2):64 * (b % 2) + 64, b // 2, :],
                             gate_d[TS * b:TS * b + TS, :].rearrange("t (q b) -> q t b", b=3)).then_inc(s_gr, 16)
            for b in range(4, NSEQ, 2):
                sp.wait_ge(s_pv, (b - 4) // 2 + 1)
                load_past(core, sp, b)
            for u in range(2):
                sp.wait_ge(s_rout[u], 64 * NU // 2)
            sp.dma_start(mix[0:R, ST, 512:1024].rearrange("p (q d) -> p q d", d=HD),
                         nsa_d.rearrange("h g b t d -> (b t) (h g) d")).then_inc(s_back, 16)
            sp.wait_ge(s_back, 16)

        @block.gpsimd
        def _(pool):
            pool.memset(qs, 0.0).then_inc(s_zero, 1)
            pool.memset(pc, 0.0).then_inc(s_zero, 1)
            for i in range(NU):
                pool.wait_ge(s_res, i + 1)
                for s in range(2):
                    for h in range(KVH):
                        pool.dma_start(nsa_d[h, :, 2 * i + s, :, :],
                                       res[64 * s + 32 * h:64 * s + 32 * h + 32, i % 2, h * HD:(h + 1) * HD]
                                       ).then_inc(s_rout[i % 2], 16)
                if 2 * i + 5 < NSEQ:
                    pool.wait_ge(s_pv, i + 1)
                    load_past(core, pool, 2 * i + 5)

        @block.scalar
        def _(act):
            def copy(o, s):
                return act.activation(o, s, ACT.Copy)

            def turn(ns):
                for n in ns:
                    if by_act(n):
                        evacuate(act, n, copy).then_inc(s_ea, 1)

            turn(range(6))
            for i in range(NU):
                act.wait_ge(s_sc, i + 1)
                if i > 0:
                    act.wait_ge(s_tr, number[("p", i - 1, 3)] + 1)
                act.activation(ws[:, 0:SEQ], ps[:, W, :], ACT.Copy).then_inc(s_wc, 1)
                act.wait_ge(s_mc, i + 1)
                act.activation(pc[:, 0:NCMP_S], pc[:, 0:NCMP_S], ACT.Exp, scale=SC, bias=mx[:, 0:1],
                               accum_out=su[:, 0:1]).then_inc(s_ec, 1)
                act.wait_ge(s_mw, i + 1)
                act.activation(ws, ws, ACT.Exp, scale=SC, bias=mx[:, 2:3], accum_out=su[:, 2:3]).then_inc(s_ew, 1)
                act.wait_ge(s_ms, i + 1)
                act.activation(ss, ss, ACT.Exp, scale=SC, bias=mx[:, 1:2], accum_out=su[:, 1:2]).then_inc(s_es, 1)
                if i + 1 < NU:
                    turn(number[("k", i + 1, r)] for r in range(6))
                turn(number[("p", i, r)] for r in range(4))

        @block.vector
        def _(dve):
            link = linker(dve, s_dve)

            def turn(ns):
                for n in ns:
                    if not by_act(n):
                        evacuate(dve, n, dve.tensor_copy).then_inc(s_ed, 1)

            dve.wait_ge(s_zero, 2)
            for h in range(KVH):
                rows = slice(64 * h, 64 * h + 64)
                for g in range(GRP):
                    last = dve.tensor_copy(qs[rows, :, 32 * h + 8 * g:32 * h + 8 * g + 8],
                                           feat[rows, QN + g, SEQ:NTOK].rearrange("p (b t) -> p b t", t=TS))
            last.then_inc(s_q, 1)
            turn(range(6))
            for i in range(NU):
                dve.wait_ge(s_sc, i + 1)
                if i > 0:
                    dve.wait_ge(s_tr, number[("p", i - 1, 3)] + 1)
                link(dve.tensor_copy(pc[:, 0:NCMP_S], ps[:, C, 0:NCMP_S]))
                dve.tensor_copy(ss[:, PAST:NKS], ps[:, C, 64:64 + R])
                dve.tensor_copy(ws[:, SEQ:NKW], ps[:, C, 128:128 + R]).then_inc(s_cc, 1)
                link(dve.tensor_reduce(mx[:, 0:1], pc[:, 0:NCMP_S], AX.X, ALU.max))
                dve.tensor_scalar(mx[:, 0:1], mx[:, 0:1], -SC, BIG, ALU.mult, ALU.min).then_inc(s_mc, 1)
                dve.wait_ge(s_cc, i + 1)
                dve.wait_ge(s_wc, i + 1)
                link(dve.tensor_reduce(mx[:, 2:3], ws, AX.X, ALU.max))
                dve.tensor_scalar(mx[:, 2:3], mx[:, 2:3], -SC, BIG, ALU.mult, ALU.min).then_inc(s_mw, 1)
                dve.wait_ge(s_ec, i + 1)
                link(dve.tensor_scalar(co[:, 0:1], su[:, 0:1], 1e-30, None, ALU.max))
                link(dve.reciprocal(co[:, 0:1], co[:, 0:1]))
                link(dve.tensor_scalar(pc[:, 0:NCMP_S], pc[:, 0:NCMP_S], co[:, 0:1], None, ALU.mult))
                link(dve.tensor_reduce(im, pc.rearrange("p (j n) -> p j n", n=4), AX.X, ALU.add))
                dve.tensor_tensor(im[:, 1:16], im[:, 1:16], pc[:, 3:63:4], ALU.add).then_inc(s_im, 1)
                dve.wait_ge(s_imp, i + 1)
                link(dve.tensor_copy(sc, ps[:, O, 384:400]))
                link(dve.memset(sc[:, 0:16:15], -1.0))
                link(dve.max(v8, sc))
                link(dve.memset(v8[:, 5:8], 3e38))
                link(dve.match_replace(sc2, v8, sc, -2.0))
                link(dve.tensor_scalar(bm, sc2, -2.0, None, ALU.is_equal))
                link(dve.tensor_scalar(bm, bm, -1.0, -NEG, ALU.add, ALU.mult))
                link(dve.memset(bm[:, 0:16:15], 0.0))
                link(dve.tensor_tensor(ss[:, 0:PAST].rearrange("p (k n) -> p k n", k=NBLK_S),
                                       ps[:, A:A + 2, :].rearrange("p a n -> p (a n)").rearrange("p (k n) -> p k n", k=NBLK_S),
                                       bcast(bm, 2, 64), ALU.add))
                link(dve.tensor_reduce(mx[:, 1:2], ss, AX.X, ALU.max))
                dve.tensor_scalar(mx[:, 1:2], mx[:, 1:2], -SC, BIG, ALU.mult, ALU.min).then_inc(s_ms, 1)
                if i + 1 < NU:
                    turn(number[("k", i + 1, r)] for r in range(6))
                turn(number[("p", i, r)] for r in range(4))
                dve.wait_ge(s_ew, i + 1)
                dve.wait_ge(s_es, i + 1)
                link(dve.tensor_scalar(co[:, 1:3], su[:, 1:3], 1e-30, None, ALU.max))
                link(dve.reciprocal(co[:, 1:3], co[:, 1:3]))
                dve.wait_ge(s_gr, 16 * NSEQ)
                link(dve.tensor_tensor(co[:, 1:3], co[:, 1:3], grow[:, i, 1:3], ALU.mult))
                dve.wait_ge(s_pv, i + 1)
                if i >= 2:
                    dve.wait_ge(s_rout[i % 2], 64 * (i // 2))
                r = res[:, i % 2, :]
                link(dve.tensor_scalar(r, ps[:, O, 0:P], grow[:, i, 0:1], None, ALU.mult))
                link(dve.scalar_tensor_tensor(r, ps[:, O, P:2 * P], co[:, 1:2], r, ALU.mult, ALU.add))
                dve.scalar_tensor_tensor(r, ps[:, O, 2 * P:3 * P], co[:, 2:3], r, ALU.mult, ALU.add).then_inc(s_res, 1)

        @block.tensor
        def _(pe):
            def take_bank(n):
                if n >= 3:
                    m = n - 3
                    pe.wait_ge(s_ea if by_act(m) else s_ed, sum(by_act(x) == by_act(m) for x in range(m + 1)))

            def evacuated(n):
                pe.wait_ge(s_ea, sum(by_act(x) for x in range(n + 1)))
                pe.wait_ge(s_ed, sum(not by_act(x) for x in range(n + 1)))

            def keys(i):
                for r in range(6):
                    n = number[("k", i, r)]
                    s, q = divmod(r, 3)
                    b = 2 * i + s
                    if q == 0:
                        pe.wait_ge(s_vin[b % 4], 16 * NP * (b // 4 + 1))
                    if q == 2:
                        pe.wait_ge(s_win[b % 4], 16 * (b // 4 + 1))
                    take_bank(n)
                    for k in range(4):
                        src = sel[:, b % 4, 4 * q + k, 0:P] if q < 2 else win[:, b % 4, k, 0:P]
                        last = pe.transpose(ps[:, T0 + n % 3, k * P:(k + 1) * P], src, ident)
                    last.then_inc(s_tr, 1)

            def scores(i):
                evacuated(number[("k", i, 5)])
                if i > 0:
                    pe.wait_ge(s_ms, i)
                    pe.wait_ge(s_mw, i)
                nm = maskb[:, P + 64 * i:P + 64 * i + R]
                old = maskb[:, P + 256:P + 256 + TS]

                def rows(s, bank, a, b, rhs, stop):
                    return pe.matmul(ps[64 * s:64 * s + 64, bank, a:b], qs[:, 2 * i + s, :], rhs, start=True, stop=stop)
                for s in range(2):
                    last = rows(s, C, 0, NCMP_S, kc[:, 2 * i + s, :], True)
                for a, slot in ((64, KSF), (128, KWF)):
                    for s in range(2):
                        rows(s, C, a, a + R, feat[:, slot, SEQ:NTOK], False)
                    pe.matmul(ps[:, C, a:a + R], identb, nm, start=False, stop=True)
                for s in range(2):
                    rows(s, W, 0, SEQ, kTw[:, s, :], False)
                pe.matmul(ps[:, W, 0:TS], identb, old, start=False, stop=True)
                for half in range(2):
                    for s in range(2):
                        last = rows(s, A + half, 0, 512, kTs[:, s, half * 512:(half + 1) * 512], True)
                last.then_inc(s_sc, 1)

            def weights(i):
                for r in range(4):
                    n = number[("p", i, r)]
                    if r == 0:
                        pe.wait_ge(s_es, i + 1)
                        pe.wait_ge(s_ew, i + 1)
                    take_bank(n)
                    if r == 0 and i > 0:
                        pe.wait_ge(s_pv, i)
                    srcs = {0: [ss[:, k * P:(k + 1) * P] for k in range(4)],
                            1: [ss[:, k * P:(k + 1) * P] for k in range(4, 8)],
                            2: [ss[:, PAST:NKS], ws[:, SEQ:NKW], pc],
                            3: [ws[:, k * P:(k + 1) * P] for k in range(4)]}[r]
                    for k, src in enumerate(srcs):
                        last = pe.transpose(ps[0:src.shape[1], T0 + n % 3, k * P:(k + 1) * P], src, ident)
                    last.then_inc(s_tr, 1)
                evacuated(number[("p", i, 3)])
                if i > 0:
                    pe.wait_ge(s_res, i)
                for s in range(2):
                    b, c = 2 * i + s, slice(64 * s, 64 * s + 64)

                    def group(br, terms):
                        for k, (w, v) in enumerate(terms):
                            last = pe.matmul(ps[c, O, br * P:(br + 1) * P], w, v, start=(k == 0), stop=(k == len(terms) - 1))
                        return last
                    group(0, [(pT[0:NCMP_S, 10, c], vc[0:NCMP_S, b, :])])
                    group(1, [(pT[:, k, c], sel[:, b % 4, k, P:256]) for k in range(NP)]
                          + [(pT[0:64, 8, c], proj[0:64, ST, C_KS + P:C_KS + 256])])
                    last = group(2, [(pT[:, 12 + k, c], win[:, b % 4, k, P:256]) for k in range(NWT)]
                                 + [(pT[0:64, 9, c], proj[0:64, ST, C_KW + P:C_KW + 256])])
                last.then_inc(s_pv, 1)

            pe.wait_ge(s_q, 1)
            keys(0)
            scores(0)
            for i in range(NU):
                pe.wait_ge(s_im, i + 1)
                if i > 0:
                    pe.wait_ge(s_res, i)
                pe.matmul(ps[:, O, 384:400], core.const("same_q"), im, start=True, stop=True).then_inc(s_imp, 1)
                if i + 1 < NU:
                    keys(i + 1)
                    scores(i + 1)
                weights(i)


def output_and_router(core):
    nc, io, ps = core.nc, core.io, core.psum
    x, mix, ident = core.x, core.mix, core.const("ident")
    own = Stack(core, core.pf, core.z1)
    core.gate2 = own.take(2 * D).rearrange("p (w n) -> p w n", w=2)
    core.blocks = own.take(NSLOT + 5).bitcast(I32)
    core.z_moe = own.at
    mixT = own.take(KT * NTOK).rearrange("p (k n) -> p k n", k=KT)
    wout = own.take(KT * D).rearrange("p (k n) -> p k n", k=KT)
    gate2 = core.gate2
    slot = own.take(NT * TOPK).bitcast(I32).rearrange("p (t j) -> p t j", t=NT)
    wt = own.take(NT * TOPK).rearrange("p (t j) -> p t j", t=NT)
    pair = own.take(NT * TOPK * 2).rearrange("p (t j w) -> p t j w", t=NT, j=TOPK)
    ex = own.take(6 * D).rearrange("p (w v n) -> p w v n", w=2, v=3)
    wr = own.take(KT * NE).rearrange("p (k n) -> p k n", k=KT)
    gffn, br, junk = own.take(D), own.take(NE), own.take(D)
    h2 = own.take(2 * D).rearrange("p (u n) -> p u n", u=2)
    h2T = own.take(KT * P).rearrange("p (k n) -> p k n", k=KT)
    stat = own.take(2 * NT)
    lg = own.take(NT * NE).rearrange("p (t e) -> p t e", t=NT)
    v8 = own.take(NT * 8).rearrange("p (t e) -> p t e", t=NT)
    i8 = own.take(NT * 8).bitcast(U32).rearrange("p (t e) -> p t e", t=NT)
    i8f = own.take(NT * TOPK).rearrange("p (t e) -> p t e", t=NT)
    nv0, wsum = own.take(NT), own.take(NT)
    oh = own.take(NT * TOPK * NE).rearrange("p (t j e) -> p t j e", t=NT, j=TOPK)
    selb = own.take(NT * NE // 2).bitcast(BF16).rearrange("p (t e) -> p t e", t=NT)
    beforeb, onesb = own.take(P // 2).bitcast(BF16), own.take(P // 2).bitcast(BF16)
    cnt, nblk, bend, base, ones = (own.take(NE) for _ in range(5))
    rk = own.take(NE)
    pick = own.take(TOPK * NE).rearrange("p (j e) -> p j e", j=TOPK)
    slotf = own.take(NT * TOPK).rearrange("p (t j) -> p t j", t=NT)
    cmpk = own.take((NSLOT + 1) * NE).rearrange("p (k e) -> p k e", e=NE)
    ek = own.take(NSLOT + 5)
    upper = Stack(core, core.z1 + NT * D, ARENA)
    b32 = own.take(3 * D)
    filler = own.take(BLK * 2).bitcast(I32).rearrange("p (c w) -> p c w", w=2)
    zero = upper.take(D)
    bparts = upper.take(3 * 3 * D // 2).bitcast(BF16).rearrange("p (a n) -> p a n", a=3)
    core.h2_d = nc.dram_tensor("h2_rows", [NTOK + BLK, D], F32).ap()
    core.ffn_d = nc.dram_tensor("ffn_rows", [NTOK + BLK, D], F32).ap()
    core.slot_d = nc.dram_tensor("slot_rows", [NSLOT * BLK, 2], I32).ap()
    core.bias_d = nc.dram_tensor("bias_parts", [NE, 3, 3 * D], BF16).ap()

    (s_w, s_wo, s_b, s_rt, s_exp, s_exps, s_exd, s_mt, s_mta, s_mtd, s_yp, s_res, s_rs, s_h, s_hd, s_hd1, s_htp, s_ht, s_lp,
     s_lg, s_nv, s_ew, s_ohr, s_rk, s_cnt, s_slot, s_blk, s_fill, s_bp, s_bo, s_wb, s_tok, s_zero, s_zo) = (core.sem(n) for n in (
         "g_ffn_in", "w_out_in", "biases_in", "router_in", "prompt_mod_in", "sample_mod_in", "scales_ready", "mixT_ps",
         "mixT_by_act", "mixT_by_dve", "y_ps", "residual", "rstd2_ready", "h2_ready", "h2_out0", "h2_out1", "h2T_ps",
         "h2T_ready", "logits_ps", "logits_ready", "neg_max", "weights_exp", "chosen", "ranks_ps", "ranks_read",
         "slots_ready", "blocks_ready", "filler_ready", "bias_parts", "bias_out", "bf16_consts", "fillers_out", "zero_ready", "zeros_out"))
    s_dve, s_act, s_pool = core.sem("dve_p6"), core.sem("act_p6"), core.sem("pool_p6")
    s_scat = core.sem("slots_scattered")
    s_h2o = [s_hd, s_hd1]
    core.w, core.mats, core.s_w = expert_weights(core)

    with nc.Block() as block:
        @block.sync
        def _(sp):
            sp.dma_start(wout, io["w_out"].rearrange("a (p k) n -> (a p) k n", k=KT)).then_inc(s_wo, 16)
            sp.dma_start(wr, io["w_router"].rearrange("a (p k) n -> (a p) k n", k=KT)).then_inc(s_rt, 16)
            sp.dma_start(br, io["b_router"].to_broadcast([P, NE])).then_inc(s_rt, 16)
            sp.dma_start(ex[:, 0, :, :].rearrange("p v n -> p (v n)"), core.mod_d[0:1, 2 * D:5 * D].to_broadcast([P, 3 * D])
                         ).then_inc(s_exp, 16)
            sp.dma_start(gate2[:, 0, :], core.mod_d[0:1, 5 * D:6 * D].to_broadcast([P, D])).then_inc(s_exp, 16)
            sp.dma_start(gffn, io["g_ffn"].to_broadcast([P, D])).then_inc(s_w, 16)
            for s in range(NSEQ):
                rows = slice(TS * s, TS * s + TS)
                sp.dma_start(ex[rows, 1, :, :].rearrange("p v n -> p (v n)"),
                             core.mod_d[1 + s:2 + s, 2 * D:5 * D].to_broadcast([TS, 3 * D])).then_inc(s_exps, 16)
                sp.dma_start(gate2[rows, 1, :], core.mod_d[1 + s:2 + s, 5 * D:6 * D].to_broadcast([TS, D])
                             ).then_inc(s_exps, 16)
            for i, name in enumerate(("b_gate", "b_up", "b_down")):
                sp.dma_start(b32[0:NE, i * D:(i + 1) * D], io[name][0]).then_inc(s_b, 16)
            sp.wait_ge(s_zero, 1)
            zeroed = 1
            sp.dma_start(core.h2_d[NTOK:, :], zero).then_inc(s_zo, 16)
            for t0 in range(0, NTOK + BLK, P):
                sp.dma_start(core.ffn_d[t0:min(t0 + P, NTOK + BLK), :], zero[0:min(P, NTOK + BLK - t0), :]).then_inc(s_zo, 16)
                zeroed += 1
            for t, (t0, n) in enumerate(TILES):
                sp.wait_ge(s_h, t + 1)
                sp.dma_start(core.h2_d[t0:t0 + n, :], h2[0:n, t % 2, :]).then_inc(s_h2o[t % 2], 16)
            for u in range(2):
                sp.wait_ge(s_h2o[u], 16 * ((NT + 1 - u) // 2))
            sp.wait_ge(s_zo, 16 * zeroed)
            sp.wait_ge(s_yp, NT)
            sp.wait_ge(s_blk, 1)
            e = sp.value_load(core.blocks[0:1, 0:1], min_val=0, max_val=NE - 1)
            for i in range(LANDING):
                load_half(core, sp, e, i // 2, i % 2, i)

        @block.gpsimd
        def _(pool):
            link = linker(pool, s_pool)
            pool.memset(zero, 0.0).then_inc(s_zero, 1)
            link(pool.memset(filler[0:NSLOT], 0))
            pool.iota(filler[0:NSLOT, :, 0], [[1, BLK]], base=NTOK, channel_multiplier=0).then_inc(s_fill, 1)
            pool.wait_ge(s_fill, 1)
            pool.dma_start(core.slot_d.rearrange("(k c) w -> k c w", c=BLK), filler[0:NSLOT]).then_inc(s_tok, 16)
            pool.wait_ge(s_b, 48)
            b = b32[0:NE, :]
            for a in range(3):
                if a < 2:
                    link(pool.tensor_copy(bparts[0:NE, a, :], b))
                    link(pool.tensor_tensor(b, b, bparts[0:NE, a, :], ALU.subtract))
                else:
                    pool.tensor_copy(bparts[0:NE, a, :], b).then_inc(s_bp, 1)
            pool.wait_ge(s_bp, 1)
            pool.dma_start(core.bias_d, bparts[0:NE, :, :]).then_inc(s_bo, 16)
            pool.wait_ge(s_tok, 16)
            pool.wait_ge(s_slot, 1)
            for t, (t0, n) in enumerate(TILES):
                for j in range(TOPK):
                    pool.indirect_dma_start(core.slot_d, bass.IndirectOffsetOnAxis(ap=slot[0:n, t, j:j + 1].bitcast(U32), axis=0),
                                            pair[0:n, t, j, :].bitcast(I32), None).then_inc(s_scat, 16)
            pool.wait_ge(s_scat, 16 * NT * TOPK)
            pool.wait_ge(s_bo, 16)

        @block.tensor
        def _(pe):
            def to_feature_major(src, n, bank):
                v = src.rearrange("s (p k) -> s k p", k=KT)
                for kt in range(KT):
                    last = pe.transpose(ps[:, bank + kt // 4, (kt % 4) * n:(kt % 4) * n + n], v[:, kt, :], ident[0:n, 0:n])
                return last

            for t, (t0, n) in enumerate(TILES):
                if t >= 2:
                    pe.wait_ge(s_mta, t - 1)
                    pe.wait_ge(s_mtd, t - 1)
                to_feature_major(mix[0:n, t, :], n, 2 * (t % 2)).then_inc(s_mt, 1)
            pe.wait_ge(s_mta, NT)
            pe.wait_ge(s_mtd, NT)
            pe.wait_ge(s_wo, 16)
            pe.wait_ge(s_rt, 32)

            def project_out(t):
                t0, n = TILES[t]
                if t >= 2:
                    pe.wait_ge(s_res, t - 1)
                for kt in range(KT):
                    for c in range(2):
                        last = pe.matmul(ps[0:n, 4 + 2 * (t % 2) + c, :], mixT[:, kt, t0:t0 + n],
                                         wout[:, kt, c * 512:(c + 1) * 512], start=(kt == 0), stop=(kt == KT - 1))
                last.then_inc(s_yp, 1)

            def route(t):
                t0, n = TILES[t]
                pe.wait_ge(s_h, t + 1)
                to_feature_major(h2[0:n, t % 2, :], n, 0).then_inc(s_htp, 1)
                pe.wait_ge(s_ht, t + 1)
                if t >= 2:
                    pe.wait_ge(s_lg, t - 1)
                for kt in range(KT):
                    last = pe.matmul(ps[0:n, 2 + t % 2, 0:NE], h2T[:, kt, 0:n], wr[:, kt, :],
                                     start=(kt == 0), stop=(kt == KT - 1))
                last.then_inc(s_lp, 1)

            for t in range(NT):
                project_out(t)
                if t >= 1:
                    route(t - 1)
            route(NT - 1)
            pe.wait_ge(s_ohr, NT)
            pe.wait_ge(s_wb, 1)
            pe.wait_ge(s_res, NT)
            for t in range(NT + 1):
                m = TILES[t][1] if t < NT else P
                terms = [(onesb[0:TILES[q][1], 0:m], q) for q in range(min(t, NT))]
                if t < NT:
                    terms.append((beforeb[0:m, 0:m], t))
                for i, (w, q) in enumerate(terms):
                    last = pe.matmul(ps[0:m, 4, t * NE:(t + 1) * NE], w, selb[0:TILES[q][1], q, :],
                                     start=(i == 0), stop=(i == len(terms) - 1))
            last.then_inc(s_rk, 1)

        @block.scalar
        def _(act):
            link = linker(act, s_act)
            for t, (t0, n) in enumerate(TILES):
                act.wait_ge(s_mt, t + 1)
                act.activation(mixT[:, 0:4, t0:t0 + n], ps[:, 2 * (t % 2), 0:4 * n].rearrange("p (k n) -> p k n", k=4),
                               ACT.Copy).then_inc(s_mta, 1)
            for t, (t0, n) in enumerate(TILES):
                act.wait_ge(s_res, t + 1)
                link(act.activation(junk[0:n, :], x[0:n, t, :], ACT.Square, accum_out=stat[0:n, t:t + 1]))
                link(act.activation(stat[0:n, NT + t:NT + t + 1], stat[0:n, t:t + 1], ACT.Ln,
                                    scale=1.0 / D, bias=core.const("eps")[0:n, :]))
                act.activation(stat[0:n, NT + t:NT + t + 1], stat[0:n, NT + t:NT + t + 1], ACT.Exp,
                               scale=-0.5).then_inc(s_rs, 1)
                act.wait_ge(s_htp, t + 1)
                act.activation(h2T[:, :, 0:n].rearrange("p (a k) n -> p a k n", a=2),
                               ps[:, 0:2, 0:4 * n].rearrange("p a (k n) -> p a k n", k=4), ACT.Copy).then_inc(s_ht, 1)
                act.wait_ge(s_nv, t + 1)
                act.activation(wt[0:n, t, :], v8[0:n, t, 0:TOPK], ACT.Exp, bias=nv0[0:n, t:t + 1],
                               accum_out=wsum[0:n, t:t + 1]).then_inc(s_ew, 1)

        @block.vector
        def _(dve):
            link = linker(dve, s_dve)
            link(dve.memset(ones, 1.0))
            dve.tensor_copy(beforeb, core.const("before"))
            dve.tensor_copy(onesb, bcast(core.const("one")[:, 0], 1, P))
            dve.tensor_copy(pair.bitcast(I32)[:, :, :, 0], bcast(core.const("token"), 2, TOPK)).then_inc(s_wb, 1)

            def scales(who, rows):
                dve.wait_ge(s_exps if who else s_exp, 32 * NSEQ if who else 32)
                dve.scalar_tensor_tensor(ex[0:rows, who, 2, :], ex[0:rows, who, 2, :], 1.0, gffn[0:rows, :], ALU.add, ALU.mult
                                         ).then_inc(s_exd, 1)
            for t, (t0, n) in enumerate(TILES):
                dve.wait_ge(s_mt, t + 1)
                dve.tensor_copy(mixT[:, 4:8, t0:t0 + n],
                                ps[:, 2 * (t % 2) + 1, 0:4 * n].rearrange("p (k n) -> p k n", k=4)).then_inc(s_mtd, 1)
            dve.wait_ge(s_w, 16)
            scales(0, P)

            def choose(t):
                n = TILES[t][1]
                dve.wait_ge(s_lp, t + 1)
                dve.tensor_tensor(lg[0:n, t, :], ps[0:n, 2 + t % 2, 0:NE], br[0:n, :], ALU.add).then_inc(s_lg, 1)
                dve.wait_ge(s_lg, t + 1)
                link(dve.max(v8[0:n, t, :], lg[0:n, t, :]))
                dve.tensor_scalar(nv0[0:n, t:t + 1], v8[0:n, t, 0:1], -1.0, None, ALU.mult).then_inc(s_nv, 1)
                link(dve.max_index(i8[0:n, t, :], v8[0:n, t, :], lg[0:n, t, :]))
                link(dve.tensor_copy(i8f[0:n, t, :], i8[0:n, t, 0:TOPK]))
                for j in range(TOPK):
                    last = dve.tensor_scalar(oh[0:n, t, j, :], core.const("iota_e")[0:n, :], i8f[0:n, t, j:j + 1], None,
                                             ALU.is_equal)
                link(last)
                with nc.allow_low_precision(reason="sums of 0 and 1 that are 0 or 1"):
                    dve.tensor_reduce(selb[0:n, t, :], oh[0:n, t, :, :].rearrange("p j e -> p e j"), AX.X, ALU.add
                                      ).then_inc(s_ohr, 1)
                dve.wait_ge(s_ew, t + 1)
                link(dve.reciprocal(wsum[0:n, t:t + 1], wsum[0:n, t:t + 1]))
                dve.tensor_scalar(pair[0:n, t, :, 1], wt[0:n, t, :], wsum[0:n, t:t + 1], None, ALU.mult)

            for t, (t0, n) in enumerate(TILES):
                who = int(t == ST)
                if who:
                    scales(1, n)
                dve.wait_ge(s_exd, 1 + who)
                hh = h2[0:n, t % 2, :]
                dve.wait_ge(s_yp, t + 1)
                if t >= 2:
                    dve.wait_ge(s_h2o[t % 2], 16 * (t // 2))
                    dve.wait_ge(s_htp, t - 1)
                link(dve.tensor_tensor(hh, ps[0:n, 4 + 2 * (t % 2):6 + 2 * (t % 2), :].rearrange("p b n -> p (b n)"),
                                       ex[0:n, who, 0, :], ALU.mult))
                dve.tensor_tensor(x[0:n, t, :], x[0:n, t, :], hh, ALU.add).then_inc(s_res, 1)
                if t >= 1:
                    choose(t - 1)
                dve.wait_ge(s_rs, t + 1)
                link(dve.scalar_tensor_tensor(hh, x[0:n, t, :], stat[0:n, NT + t:NT + t + 1], ex[0:n, who, 2, :],
                                              ALU.mult, ALU.mult))
                dve.tensor_tensor(hh, hh, ex[0:n, who, 1, :], ALU.add).then_inc(s_h, 1)
            choose(NT - 1)
            dve.wait_ge(s_rk, 1)
            link(dve.tensor_copy(cnt, ps[:, 4, NT * NE:(NT + 1) * NE]))
            link(dve.tensor_scalar(nblk, cnt, 0.0, None, ALU.is_gt))
            for b in range(1, -(-NTOK // BLK)):
                link(dve.scalar_tensor_tensor(nblk, cnt, float(b * BLK), nblk, ALU.is_gt, ALU.add))
            link(dve.tensor_tensor_scan(bend, ones, nblk, 0.0, ALU.mult, ALU.add))
            link(dve.tensor_tensor(base, bend, nblk, ALU.subtract))
            link(dve.tensor_scalar(base, base, float(BLK), None, ALU.mult))
            one = slice(0, 1)
            link(dve.tensor_tensor(cmpk[one], bcast(bend[one, :], 1, NSLOT + 1), bcast(core.const("iota_k")[one, :], 2, NE),
                                   ALU.is_le))
            link(dve.tensor_reduce(ek[one, 0:NSLOT + 1], cmpk[one], AX.X, ALU.add))
            link(dve.tensor_scalar(ek[one, 0:NSLOT], ek[one, 0:NSLOT], float(NE - 1), None, ALU.min))
            for i in range(5):
                link(dve.tensor_scalar(ek[one, NSLOT + i:NSLOT + i + 1], bend[one, NE - 1:NE], float(-i), None, ALU.add))
            dve.tensor_copy(core.blocks[one, :], ek[one, :]).then_inc(s_blk, 1)
            for t, (t0, n) in enumerate(TILES):
                link(dve.tensor_tensor(rk[0:n, :], ps[0:n, 4, t * NE:(t + 1) * NE], base[0:n, :], ALU.add))
                link(dve.tensor_tensor(pick[0:n], oh[0:n, t], bcast(rk[0:n, :], 1, TOPK), ALU.mult))
                link(dve.tensor_reduce(slotf[0:n, t, :], pick[0:n], AX.X, ALU.add))
                last = dve.tensor_copy(slot[0:n, t, :], slotf[0:n, t, :])
            last.then_inc(s_slot, 1)


LIMIT, ALPHA = 7.0, 1.702


def is_zero(n):
    return isinstance(n, int) and n == 0


HK = KT // 2
N_SPLIT = 2 * 4 * (HK // 2) * D + 4 * KT * P
LANDING = 3


def expert_weights(core):
    words = ARENA - N_SPLIT - core.z_moe
    core.moe = Stack(core, 0, words, core.named("expert_buffers", core.z_moe, words))
    w = core.moe.take(LANDING * HK * D).rearrange("p (s k n) -> p s k n", s=LANDING, k=HK)
    mats = [core.io[n].rearrange("a e (p k) n -> (a e) p k n", k=KT) for n in ("w_gate", "w_up", "w_down")]
    return w, mats, [core.sem(f"w_in{i}", carry=True) for i in range(LANDING)]


def load_half(core, sp, e, m, half, place):
    sp.dma_start(core.w[:, place, :, :],
                 core.mats[m][bass.ds(e, 1), :, half * HK:(half + 1) * HK, :].rearrange("e p k n -> (e p) k n")
                 ).then_inc(core.s_w[place], 16)


QK = HK // 2
RING_Q = 4


def experts(core):
    nc, ps = core.nc, core.psum
    blocks = core.blocks
    n_split = N_SPLIT
    split = core.named("split", ARENA - N_SPLIT, N_SPLIT)
    high, rest = [split[:, i * RING_Q * QK * D:(i + 1) * RING_Q * QK * D].rearrange("p (s k n) -> p s k n", s=RING_Q, k=QK)
                  for i in range(2)]
    xh, xl, ah, al = (split[:, n_split - (4 - i) * KT * P:n_split - (3 - i) * KT * P] for i in range(4))
    own = core.moe
    ident, one = own.take(P), own.take(1)
    w, s_w = core.w, core.s_w
    bias = own.take(3 * D // 2).bitcast(BF16).rearrange("p (m n) -> p m n", m=3)
    ones = own.take(P // 2).bitcast(BF16)
    xg, g, u, s, y = (own.take(D) for _ in range(5))
    sums = [own.take(1), own.take(1)]
    tokens, none = own.take(1).bitcast(I32), own.take(1).bitcast(I32)
    row_in, row_out = own.take(2), own.take(2)
    slot_blk = core.slot_d.rearrange("(k p) w -> k p w", p=BLK)
    GB, UB, DB, TB = 0, 2, 4, 6

    s_bias = [core.sem(f"bias_in{i}") for i in range(3)]
    s_high, s_rest, s_used = (core.sem(n) for n in ("quarters_rounded", "quarters_split", "quarters_used"))
    s_ones, s_row, s_rowo, s_xg, s_xtp, s_xh, s_xt = (core.sem(n) for n in (
        "ones_ready", "tokens_in", "weights_in", "rows_gathered", "xT_ps", "xT_rounded", "xT_split"))
    s_g, s_u, s_sig, s_a, s_atp, s_ah, s_at = (core.sem(n) for n in (
        "gate_read", "up_read", "sigmoid", "act_ready", "aT_ps", "aT_rounded", "aT_split"))
    s_y, s_yo, s_t = core.sem("down_read"), core.sem("rows_added"), core.sem("swiglu_part")
    s_tok, s_none = core.sem("tokens_taken"), core.sem("none_ready")
    s_const = core.sem("constants_in")
    s_sum = [core.sem("gather_allowed"), core.sem("add_allowed")]

    def first_of(prev):
        return 8 + 12 * prev

    def landed(j, prev):
        half = j // 2 + (0 if prev is None else 4)
        number = j if prev is None else first_of(prev) + j
        return w[:, half % LANDING, QK * (j % 2):QK * (j % 2 + 1)], half, number

    def used_blocks(eng, n=4):
        return [eng.value_load(blocks[0:1, NSLOT + i:NSLOT + i + 1], min_val=NTOK * TOPK // BLK - i, max_val=NSLOT - i)
                for i in range(n)]

    with nc.Block() as block:
        @block.sync
        def _(sp):
            _, nb1, nb2, nb3, nb4 = used_blocks(sp, 5)

            def expert(k):
                return sp.value_load(blocks[0:1, bass.ds(k, 1)], min_val=0, max_val=NE - 1)

            def biases(m, e, used):
                if used is not None:
                    sp.wait_ge(s_used, used)
                sp.dma_start(bias[0:3, m, :], core.bias_d[bass.ds(e, 1), :, m * D:(m + 1) * D]
                             .rearrange("e a n -> (e a) n")).then_inc(s_bias[m], 16)

            def halves(m, e, prev, c):
                for i in range(2):
                    sp.wait_ge(s_rest, 12 * prev + 4 + 2 * (c + i))
                    load_half(core, sp, e, m, i, (4 + c + i) % LANDING)

            def slots_in(k):
                if not is_zero(k):
                    sp.wait_ge(s_tok, k)
                sp.dma_start(row_in.bitcast(I32), slot_blk[bass.ds(k, 1), :, :].rearrange("k p w -> (k p) w")).then_inc(s_row, 16)

            def slots_out(k):
                if not is_zero(k):
                    sp.wait_ge(s_yo, 16 * k)
                sp.dma_start(row_out.bitcast(I32), slot_blk[bass.ds(k, 1), :, :].rearrange("k p w -> (k p) w")).then_inc(s_rowo, 16)

            for dst, name in ((ident, "ident"), (one, "one")):
                at, n = CONST_COLS[name]
                with nc.allow_non_contiguous_dma(reason="a few columns of a small array"):
                    sp.dma_start(dst, core.io["consts"][:, at:at + n]).then_inc(s_const, 16)
            slots_in(0)
            e = expert(0)
            biases(0, e, None)
            biases(1, e, None)
            slots_in(1)
            sp.wait_ge(s_rest, 2)
            load_half(core, sp, e, 1, 1, 0)
            slots_in(2)

            def step(k, prev, before, next_rows=True):
                free = [12 * prev, 12 * prev + 4, 12 * prev + 8]
                if is_zero(prev):
                    free = [4, 8, None]
                e = expert(k)
                biases(0, e, free[0])
                halves(0, e, prev, 0)
                if before is not None:
                    slots_out(before)
                e = expert(k)
                biases(1, e, free[1])
                halves(1, e, prev, 2)
                if next_rows:
                    slots_in(k + 2)
                e = expert(prev)
                biases(2, e, free[2])
                halves(2, e, prev, 4)

            step(1, 0, None)
            step(2, 1, 0)
            with sp.Fori(3, nb2) as k:
                step(k, k - 1, k - 2)
            step(nb2, nb3, nb4, next_rows=False)
            step(nb1, nb2, nb3, next_rows=False)
            e = expert(nb1)
            halves(2, e, nb1, 0)
            slots_out(nb2)
            biases(2, e, first_of(nb1))
            slots_out(nb1)

        @block.gpsimd
        def _(pool):
            nb, nb1, nb2, nb3 = used_blocks(pool)

            def take_waits(sem, n):
                if not is_zero(n):
                    pool.wait_ge(sem, n)
                pool.tensor_tensor(sums[s_sum.index(sem)], one, one, ALU.add).then_inc(sem, 1)

            def gather(k):
                pool.wait_ge(s_row, 16 * (k + 1))
                if not is_zero(k):
                    pool.wait_ge(s_xg, 16 * k)
                pool.tensor_tensor(tokens, row_in[:, 0:1].bitcast(I32), none, ALU.add).then_inc(s_tok, 1)
                pool.wait_ge(s_tok, k + 1)
                if not is_zero(k):
                    pool.wait_ge(s_xtp, k)
                take_waits(s_sum[0], k)
                pool.indirect_dma_start(xg, None, core.h2_d, bass.IndirectOffsetOnAxis(ap=tokens.bitcast(U32), axis=0)
                                        ).then_inc(s_xg, 16)

            def add_rows(n, done):
                pool.wait_ge(s_y, n)
                take_waits(s_sum[1], done)
                pool.indirect_dma_start(core.ffn_d, bass.IndirectOffsetOnAxis(ap=row_out[:, 0:1].bitcast(U32), axis=0), y, None,
                                        compute_op=ALU.add).then_inc(s_yo, 16)

            pool.memset(none, 0).then_inc(s_none, 1)
            pool.wait_ge(s_none, 1)
            pool.wait_ge(s_const, 32)
            for k in range(4):
                gather(k)
            add_rows(1, 0)
            with pool.Fori(4, nb) as k:
                gather(k)
                add_rows(k - 2, k - 3)
            add_rows(nb2, nb3)
            add_rows(nb1, nb2)
            add_rows(nb, nb1)
            pool.wait_ge(s_yo, 16 * nb)

        @block.tensor
        def _(pe):
            nb, nb1, nb2, _ = used_blocks(pe)

            def product(m, n, xs, bank, before):
                pe.wait_ge(s_bias[m], 16 * n)
                for c in range(2):
                    pe.matmul(ps[:, bank + c, :], ones[0:3, :], bias[0:3, m, c * 512:(c + 1) * 512], start=True, stop=False)
                for q in range(4):
                    j = 4 * m + q
                    pe.wait_ge(s_rest, before + q + 1)
                    for i in range(QK):
                        kt = QK * q + i
                        hi = [high[:, j % RING_Q, i, c * 512:(c + 1) * 512] for c in range(2)]
                        lo = [rest[:, j % RING_Q, i, c * 512:(c + 1) * 512] for c in range(2)]
                        terms = [(xs[0], hi[0], 0), (xs[0], hi[1], 1), (xs[0], lo[0], 0), (xs[0], lo[1], 1),
                                 (xs[1], hi[0], 0), (xs[1], hi[1], 1)]
                        for x, wt, c in terms:
                            last = pe.matmul(ps[:, bank + c, :], x[:, kt * P:(kt + 1) * P].bitcast(F32R), wt.bitcast(F32R),
                                             start=False, stop=(kt == KT - 1 and x is xs[1]))
                    last.then_inc(s_used, 1)

            def turn(src, sem):
                v = src.rearrange("s (p k) -> s k p", k=KT)
                for kt in range(KT):
                    last = pe.transpose(ps[:, TB + kt // 4, (kt % 4) * P:(kt % 4 + 1) * P], v[:, kt, :], ident)
                last.then_inc(sem, 1)

            def gate(k, before):
                pe.wait_ge(s_xt, k + 1)
                if not is_zero(k):
                    pe.wait_ge(s_g, k)
                product(0, k + 1, (xh, xl), GB, before)

            def up(k, before):
                if not is_zero(k):
                    pe.wait_ge(s_u, k)
                product(1, k + 1, (xh, xl), UB, before)

            def turn_rows(k, first=False):
                pe.wait_ge(s_xg, 16 * (k + 1))
                if not first:
                    pe.wait_ge(s_at, k - 1)
                elif k == 1:
                    pe.wait_ge(s_xt, 1)
                turn(xg, s_xtp)

            def turn_act(k):
                pe.wait_ge(s_a, k)
                pe.wait_ge(s_xt, k + 1)
                turn(u, s_atp)

            def down(n, done, before):
                pe.wait_ge(s_at, n)
                if not is_zero(done):
                    pe.wait_ge(s_y, done)
                product(2, n, (ah, al), DB, before)

            pe.wait_ge(s_ones, 1)
            pe.wait_ge(s_const, 32)
            turn_rows(0, first=True)
            gate(0, 0)
            up(0, 4)
            turn_rows(1, first=True)

            def step(k, prev, last=False):
                gate(k, first_of(prev))
                turn_act(k)
                up(k, first_of(prev) + 4)
                if not last:
                    turn_rows(k + 1)
                down(k, prev, first_of(prev) + 8)

            step(1, 0)
            with pe.Fori(2, nb1) as k:
                step(k, k - 1)
            step(nb1, nb2, last=True)
            pe.wait_ge(s_a, nb)
            turn(u, s_atp)
            down(nb, nb1, first_of(nb1))

        @block.scalar
        def _(act):
            nb, nb1, nb2, _ = used_blocks(act)

            def high_part(j, prev):
                v, half, number = landed(j, prev)
                act.wait_ge(s_w[half % LANDING], 16 * (half // LANDING + 1) + (0 if prev is None else 32 * prev))
                if not (prev is None and j < RING_Q):
                    act.wait_ge(s_used, number - (RING_Q - 1))
                act.activation(high[:, j % RING_Q].bitcast(F32R), v, ACT.Copy).then_inc(s_high, 1)

            def rounded(dst, sem):
                act.activation(dst.bitcast(F32R), ps[:, TB:TB + 2, :].rearrange("p b n -> p (b n)"), ACT.Copy).then_inc(sem, 1)

            def rows_T(k):
                act.wait_ge(s_xtp, k + 1)
                rounded(xh, s_xh)

            def acts_T(k):
                act.wait_ge(s_atp, k)
                rounded(ah, s_ah)

            def sigmoid(k):
                act.wait_ge(s_g, k + 1)
                act.activation(s, g, ACT.Sigmoid, scale=ALPHA).then_inc(s_sig, 1)

            def weigh(n, done, used):
                act.wait_ge(s_used, used)
                act.wait_ge(s_rowo, 16 * n)
                if not is_zero(done):
                    act.wait_ge(s_yo, 16 * done)
                act.activation(y, ps[:, DB:DB + 2, :].rearrange("p b n -> p (b n)"), ACT.Copy, scale=row_out[:, 1:2]
                               ).then_inc(s_y, 1)

            for j in range(4):
                high_part(j, None)
            rows_T(0)
            for j in range(4, 7):
                high_part(j, None)
            sigmoid(0)
            high_part(7, None)
            rows_T(1)
            for j in range(4):
                high_part(j, 0)

            def step(k, prev, last=False):
                for j in range(4, 7):
                    high_part(j, prev)
                sigmoid(k)
                high_part(7, prev)
                acts_T(k)
                for j in range(8, 12):
                    high_part(j, prev)
                if not last:
                    rows_T(k + 1)
                for j in range(3):
                    high_part(j, k)
                weigh(k, prev, first_of(prev) + 12)
                high_part(3, k)

            step(1, 0)
            with act.Fori(2, nb1) as k:
                step(k, k - 1)
            step(nb1, nb2, last=True)
            acts_T(nb)
            weigh(nb, nb1, first_of(nb1) + 4)

        @block.vector
        def _(dve):
            nb, nb1, nb2, _ = used_blocks(dve)
            dve.memset(ones, 1.0).then_inc(s_ones, 1)

            def rest_part(j, prev):
                v, _, number = landed(j, prev)
                dve.wait_ge(s_high, number + 1)
                dve.tensor_tensor(rest[:, j % RING_Q].bitcast(F32R), v, high[:, j % RING_Q], ALU.subtract).then_inc(s_rest, 1)

            def rest_T(hi, lo, sem, n, out):
                dve.wait_ge(sem, n)
                dve.tensor_tensor(lo.bitcast(F32R), ps[:, TB:TB + 2, :].rearrange("p b n -> p (b n)"), hi, ALU.subtract).then_inc(out, 1)

            def read_gate(k, used):
                dve.wait_ge(s_used, used)
                if not is_zero(k):
                    dve.wait_ge(s_a, k)
                dve.tensor_scalar(g, ps[:, GB:GB + 2, :].rearrange("p b n -> p (b n)"), LIMIT, None, ALU.min).then_inc(s_g, 1)

            def activations(k, used):
                dve.wait_ge(s_used, used)
                if not is_zero(k):
                    dve.wait_ge(s_atp, k)
                dve.tensor_scalar(u, ps[:, UB:UB + 2, :].rearrange("p b n -> p (b n)"), -LIMIT, LIMIT, ALU.max, ALU.min
                                  ).then_inc(s_u, 1)
                dve.wait_ge(s_u, k + 1)
                dve.scalar_tensor_tensor(u, u, 1.0, g, ALU.add, ALU.mult).then_inc(s_t, 1)
                dve.wait_ge(s_t, k + 1)
                dve.wait_ge(s_sig, k + 1)
                dve.tensor_tensor(u, u, s, ALU.mult).then_inc(s_a, 1)

            for j in range(4):
                rest_part(j, None)
            rest_T(xh, xl, s_xh, 1, s_xt)
            for j in range(4, 7):
                rest_part(j, None)
            read_gate(0, 4)
            rest_part(7, None)
            activations(0, 8)
            rest_T(xh, xl, s_xh, 2, s_xt)
            for j in range(4):
                rest_part(j, 0)

            def step(k, prev, last=False):
                at = first_of(prev)
                for j in range(4, 7):
                    rest_part(j, prev)
                read_gate(k, at + 4)
                rest_part(7, prev)
                rest_T(ah, al, s_ah, k, s_at)
                for j in range(8, 11):
                    rest_part(j, prev)
                activations(k, at + 8)
                rest_part(11, prev)
                if not last:
                    rest_T(xh, xl, s_xh, k + 2, s_xt)
                for j in range(4):
                    rest_part(j, k)

            step(1, 0)
            with dve.Fori(2, nb1) as k:
                step(k, k - 1)
            step(nb1, nb2, last=True)
            rest_T(ah, al, s_ah, nb, s_at)


def combine(core):
    nc, io = core.nc, core.io
    x, gate2 = core.x, core.gate2
    own = Stack(core, core.z_moe, ARENA)
    f = own.take(NT * D).rearrange("p (t d) -> p t d", t=NT)
    junk, gfin = own.take(2 * D).rearrange("p (u d) -> p u d", u=2), own.take(D)
    out = own.take(NT * D).rearrange("p (t d) -> p t d", t=NT)
    stat = own.take(2 * NT)
    s_gf, s_one, s_x, s_rs, s_o, s_out, s_act, s_dve = (core.sem(n) for n in (
        "g_final_in", "stat_filled", "x_final", "rstd3_ready", "out_ready", "out_stored", "act_p8", "dve_p8"))
    s_f = [core.sem(f"sums_in{t}") for t in range(NT)]

    with nc.Block() as block:
        @block.sync
        def _(sp):
            for t, (t0, n) in enumerate(TILES):
                sp.dma_start(f[0:n, t, :], core.ffn_d[t0:t0 + n, :]).then_inc(s_f[t], 16)
                if t == 0:
                    sp.dma_start(gfin, io["g_final"].unsqueeze(0).to_broadcast([P, D])).then_inc(s_gf, 16)
            for t, (t0, n) in enumerate(TILES):
                sp.wait_ge(s_o, t + 1)
                dst = io["out_0"][0, t0:t0 + n, :] if t < ST else io["out_1"].rearrange("b t d -> (b t) d")
                sp.dma_start(dst, out[0:n, t, :]).then_inc(s_out, 16)
            sp.wait_ge(s_out, 16 * NT)

        @block.scalar
        def _(act):
            link = linker(act, s_act)
            for t, (t0, n) in enumerate(TILES):
                act.wait_ge(s_x, t + 1)
                if t == 0:
                    act.wait_ge(s_one, 1)
                last = act.activation(junk[0:n, t % 2, :], x[0:n, t, :], ACT.Square, accum_out=stat[0:n, t:t + 1])
                if t < NT - 1:
                    link(last)
            link(last)
            link(act.activation(stat[:, NT:2 * NT], stat[:, 0:NT], ACT.Ln, scale=1.0 / D, bias=core.const("eps")))
            act.activation(stat[:, NT:2 * NT], stat[:, NT:2 * NT], ACT.Exp, scale=-0.5).then_inc(s_rs, 1)

        @block.vector
        def _(dve):
            link = linker(dve, s_dve)
            dve.memset(stat, 1.0).then_inc(s_one, 1)

            def finish(t):
                n = TILES[t][1]
                dve.scalar_tensor_tensor(out[0:n, t, :], x[0:n, t, :], stat[0:n, NT + t:NT + t + 1], gfin[0:n, :],
                                         ALU.mult, ALU.mult).then_inc(s_o, 1)

            for t, (t0, n) in enumerate(TILES):
                dve.wait_ge(s_f[t], 16)
                link(dve.tensor_tensor(f[0:n, t, :], f[0:n, t, :], gate2[0:n, int(t == ST), :], ALU.mult))
                dve.tensor_tensor(x[0:n, t, :], x[0:n, t, :], f[0:n, t, :], ALU.add).then_inc(s_x, 1)
            dve.wait_ge(s_gf, 16)
            dve.wait_ge(s_rs, 1)
            for t in range(NT):
                finish(t)


STAGES = [project, gla, compress, prompt_attention, sample_attention, output_and_router, experts, combine]


INPUTS = ["x_prompt", "x_sample", "c_prompt", "c_sample", "cache_cmp", "cache_sel", "state_win", "state_gla",
          "page_table", "w_ada", "b_ada", "g_mix", "g_ffn", "w_in", "w_a2", "b_a", "g_gla", "phi_pe", "phi_w", "w_out",
          "w_router", "b_router", "w_gate", "b_gate", "w_up", "b_up", "w_down", "b_down", "g_final"]
KV = (2, KVH, HD)
OUTPUTS = [(1, SEQ, D), (NSEQ, TS, D), (1, 1, SEQ) + KV, (1, 1, SEQ) + KV, (1, 1, SEQ) + KV, (1, 1, GH, DK, DV),
           (1, NSEQ, TS) + KV, (1, NSEQ, TS) + KV, (1, NSEQ, SEQ) + KV, (1, NSEQ, GH, DK, DV)]

ZONE = ARENA - 22464 - NT * D - NF * NTOK


def build(nc, io, stages=None):
    with ExitStack() as ctx:
        core = Core(nc, ctx, io)
        core.x = core.take(NT * D).rearrange("p (t d) -> p t d", t=NT)
        core.mod = core.take(3 * 512).rearrange("p (b n) -> p b n", b=3)
        core.consts = core.take(N_CONST_A + N_CONST_B)
        core.pf = core.top
        core.proj_flat = core.take(NT * DIN)
        core.proj = core.proj_flat.rearrange("p (t n) -> p t n", t=NT)
        core.z0, core.z1 = core.top, core.top + ZONE
        mixed = Stack(core, core.z1, ARENA)
        core.mix = mixed.take(NT * D).rearrange("p (t d) -> p t d", t=NT)
        core.feat = mixed.take(NF * NTOK).rearrange("p (i n) -> p i n", i=NF)
        for stage in stages or STAGES:
            stage(core)
            core.stage_done()


def kernel(**inputs):
    import concourse.bacc as bacc
    from concourse.bass_utils import run_bass_kernel_spmd

    nc = bacc.Bacc("TRN2", target_bir_lowering=False, num_devices=1)
    arrays, io = {}, {}
    for name in INPUTS:
        a = np.ascontiguousarray(inputs[name])
        arrays["in_" + name] = a
        io[name] = nc.dram_tensor("in_" + name, a.shape, mybir.dt.from_np(a.dtype), kind="ExternalInput").ap()
    arrays["consts"] = CONST_ARRAY
    io["consts"] = nc.dram_tensor("consts", CONST_ARRAY.shape, F32, kind="ExternalInput").ap()
    for i, shape in enumerate(OUTPUTS):
        io[f"out_{i}"] = nc.dram_tensor(f"out_{i}", shape, F32, kind="ExternalOutput").ap()
    build(nc, io)
    r = run_bass_kernel_spmd(nc, [arrays], core_ids=[0])
    return tuple(np.asarray(r.results[0][f"out_{i}"]) for i in range(len(OUTPUTS)))
```
